# Optimizing a Trainium2 kernel written in Bass

```python
import math
import jax, jax.numpy as jnp
from jax import lax
import numpy as np
import jax
import jax.numpy as jnp

D_MODEL = 1024
BATCH = 1
SEQ = 256
DEPTH = 2

N_A_LAYERS = DEPTH // 2
N_B_LAYERS = DEPTH - N_A_LAYERS
POOL_WINDOWS = (2, 4, 8, 16)
N_POOL_GROUPS = len(POOL_WINDOWS)
POOL_GROUP = D_MODEL // N_POOL_GROUPS
HEAD_DIM = 64
N_HEADS = D_MODEL // HEAD_DIM
MOBA_BLOCK = 256
MOBA_TOPK = 3
Q_BLOCK = 128
NUM_BUCKETS = 32
MAX_DISTANCE = 128
D_FF = -(-8 * D_MODEL // (3 * 256)) * 256
EPS = 1e-6


def rmsnorm(x, g):
    xf = x.astype(jnp.float32)
    y = xf * lax.rsqrt(jnp.mean(xf * xf, axis=-1, keepdims=True) + EPS)
    return (y * g.astype(jnp.float32)).astype(x.dtype)

def pool_mixer(h, w, scale):
    B, T, D = h.shape
    hf = h.astype(jnp.float32)
    csum = jnp.concatenate([jnp.zeros((B, 1, D), jnp.float32), jnp.cumsum(hf, axis=1)], axis=1)
    t = jnp.arange(T)
    outs = []
    for g, win in enumerate(POOL_WINDOWS):
        sl = slice(g * POOL_GROUP, (g + 1) * POOL_GROUP)
        start = jnp.maximum(t + 1 - win, 0)
        cnt = (t + 1 - start).astype(jnp.float32)
        window_sum = csum[:, 1:, sl] - jnp.take(csum[:, :, sl], start, axis=1)
        outs.append(window_sum / cnt[None, :, None] - hf[:, :, sl])
    d = jnp.stack(outs, axis=2).astype(h.dtype)
    y = jnp.einsum('btgc,gce->btge', d, w).reshape(B, T, D)
    return y * scale

def swiglu(h, w_gate_up, w_down):
    gu = h @ w_gate_up
    gate, up = jnp.split(gu, 2, axis=-1)
    return (jax.nn.silu(gate) * up) @ w_down

def rel_bucket(n):
    max_exact = NUM_BUCKETS // 2
    nf = jnp.maximum(n, max_exact).astype(jnp.float32)
    large = max_exact + (jnp.log(nf / max_exact) / math.log(MAX_DISTANCE / max_exact)
                         * (NUM_BUCKETS - max_exact)).astype(jnp.int32)
    large = jnp.minimum(large, NUM_BUCKETS - 1)
    return jnp.where(n < max_exact, n, large)

def shared_kv(x, g, w_kv):
    B, T, D = x.shape
    h = rmsnorm(x, g)
    kv = h @ w_kv
    k, v = jnp.split(kv, 2, axis=-1)
    n_blocks = -(-T // MOBA_BLOCK)
    pad = n_blocks * MOBA_BLOCK - T

    def to_blocks(a):
        a = a.reshape(B, T, N_HEADS, HEAD_DIM).transpose(0, 2, 1, 3)
        a = jnp.pad(a, ((0, 0), (0, 0), (0, pad), (0, 0)))
        return a.reshape(B, N_HEADS, n_blocks, MOBA_BLOCK, HEAD_DIM)

    k_blocks = to_blocks(k)
    v_blocks = to_blocks(v)
    k_mean = jnp.mean(k_blocks.astype(jnp.float32), axis=3).astype(k_blocks.dtype)
    return k_blocks, v_blocks, k_mean

def moba_attention(q, k_blocks, v_blocks, k_mean, rel_bias):
    B, T = q.shape[0], q.shape[1]
    n_q = T // Q_BLOCK
    n_blocks = k_blocks.shape[2]
    topk = min(MOBA_TOPK, n_blocks)
    scale = HEAD_DIM ** -0.5
    h_idx = jnp.arange(N_HEADS)[:, None, None]
    bias_t = rel_bias.T.astype(jnp.float32)
    q_blocks = q.transpose(0, 2, 1, 3).reshape(B, N_HEADS, n_q, Q_BLOCK, HEAD_DIM)
    q_blocks = q_blocks.transpose(0, 2, 1, 3, 4).reshape(B * n_q, N_HEADS, Q_BLOCK, HEAD_DIM)
    b_idx = jnp.repeat(jnp.arange(B), n_q)
    qb_idx = jnp.tile(jnp.arange(n_q), B)
    j_blk = jnp.arange(MOBA_BLOCK)

    def step(args):
        qblk, b, qb = args
        kb = k_blocks[b]
        vb = v_blocks[b]
        km = k_mean[b]
        qs = qb * Q_BLOCK
        own = qs // MOBA_BLOCK
        qpos = qs + jnp.arange(Q_BLOCK)
        gate = jnp.einsum('hqd,hnd->hqn', qblk, km).astype(jnp.float32)
        gate = jnp.where(jnp.arange(n_blocks)[None, None, :] < own, gate, -jnp.inf)
        _, sel = lax.top_k(gate, topk)
        sel_valid = jnp.arange(topk) < jnp.minimum(own, topk)
        k_sel = kb[h_idx, sel]
        v_sel = vb[h_idx, sel]
        s_sel = jnp.einsum('hqd,hqkjd->hqkj', qblk, k_sel).astype(jnp.float32) * scale
        kpos_sel = sel[..., None] * MOBA_BLOCK + j_blk
        k_own = lax.dynamic_index_in_dim(kb, own, axis=1, keepdims=False)
        v_own = lax.dynamic_index_in_dim(vb, own, axis=1, keepdims=False)
        s_own = jnp.einsum('hqd,hjd->hqj', qblk, k_own).astype(jnp.float32) * scale
        kpos_own = own * MOBA_BLOCK + j_blk
        L_sel = topk * MOBA_BLOCK
        s = jnp.concatenate([s_sel.reshape(N_HEADS, Q_BLOCK, L_sel), s_own], axis=-1)
        kpos = jnp.concatenate([kpos_sel.reshape(N_HEADS, Q_BLOCK, L_sel),
                                jnp.broadcast_to(kpos_own[None, None, :], (N_HEADS, Q_BLOCK, MOBA_BLOCK))], axis=-1)
        valid_sel = jnp.broadcast_to(sel_valid[None, None, :, None], (N_HEADS, Q_BLOCK, topk, MOBA_BLOCK)).reshape(N_HEADS, Q_BLOCK, L_sel)
        valid_own = jnp.broadcast_to(kpos_own[None, None, :] <= qpos[None, :, None], (N_HEADS, Q_BLOCK, MOBA_BLOCK))
        valid = jnp.concatenate([valid_sel, valid_own], axis=-1)
        bucket = rel_bucket(jnp.maximum(qpos[None, :, None] - kpos, 0))
        bias = bias_t[h_idx, bucket]
        s = jnp.where(valid, s + bias, -jnp.inf)
        p = jax.nn.softmax(s, axis=-1).astype(vb.dtype)
        p_sel = p[..., :L_sel].reshape(N_HEADS, Q_BLOCK, topk, MOBA_BLOCK)
        p_own = p[..., L_sel:]
        return (jnp.einsum('hqkj,hqkjd->hqd', p_sel, v_sel)
                + jnp.einsum('hqj,hjd->hqd', p_own, v_own))

    o = lax.map(step, (q_blocks, b_idx, qb_idx))
    o = o.reshape(B, n_q, N_HEADS, Q_BLOCK, HEAD_DIM).transpose(0, 1, 3, 2, 4)
    return o.reshape(B, T, D_MODEL)

def first_inputs(seed: int = 0) -> dict:
    key = jax.random.key(seed)
    ks = jax.random.split(key, 14)
    f32 = jnp.float32
    nrm = lambda k, shape: jax.random.normal(k, shape, f32)
    x = nrm(ks[0], (BATCH, SEQ, D_MODEL))
    norm_mixer = 1.0 + 0.05 * nrm(ks[1], (DEPTH, D_MODEL))
    norm_ffn = 1.0 + 0.05 * nrm(ks[2], (DEPTH, D_MODEL))
    pool_w = nrm(ks[3], (N_A_LAYERS, N_POOL_GROUPS, POOL_GROUP, POOL_GROUP)) * POOL_GROUP ** -0.5
    pool_scale = 1.0 + 0.05 * nrm(ks[4], (N_A_LAYERS, D_MODEL))
    kv_norm = 1.0 + 0.05 * nrm(ks[5], (D_MODEL,))
    w_kv = nrm(ks[6], (D_MODEL, 2 * D_MODEL)) * D_MODEL ** -0.5
    w_q = nrm(ks[7], (N_B_LAYERS, D_MODEL, D_MODEL)) * D_MODEL ** -0.5
    w_o = nrm(ks[8], (N_B_LAYERS, D_MODEL, D_MODEL)) * D_MODEL ** -0.5
    rel_bias = 0.5 * nrm(ks[9], (NUM_BUCKETS, N_HEADS))
    w_gate_up = nrm(ks[10], (DEPTH, D_MODEL, 2 * D_FF)) * D_MODEL ** -0.5
    w_down = nrm(ks[11], (DEPTH, D_FF, D_MODEL)) * D_FF ** -0.5
    final_norm = 1.0 + 0.05 * nrm(ks[12], (D_MODEL,))
    return {'x': x, 'norm_mixer': norm_mixer, 'norm_ffn': norm_ffn, 'pool_w': pool_w,
            'pool_scale': pool_scale, 'kv_norm': kv_norm, 'w_kv': w_kv, 'w_q': w_q, 'w_o': w_o,
            'rel_bias': rel_bias, 'w_gate_up': w_gate_up, 'w_down': w_down, 'final_norm': final_norm}

def first_block(x, norm_mixer, norm_ffn, pool_w, pool_scale, kv_norm, w_kv, w_q, w_o,
              rel_bias, w_gate_up, w_down, final_norm):
    B, T, D = x.shape
    k_blocks = v_blocks = k_mean = None
    for layer in range(DEPTH):
        if layer < N_A_LAYERS:
            x = x + pool_mixer(rmsnorm(x, norm_mixer[layer]), pool_w[layer], pool_scale[layer])
        else:
            j = layer - N_A_LAYERS
            if j == 0:
                k_blocks, v_blocks, k_mean = shared_kv(x, kv_norm, w_kv)
            h = rmsnorm(x, norm_mixer[layer])
            q = (h @ w_q[j]).reshape(B, T, N_HEADS, HEAD_DIM)
            o = moba_attention(q, k_blocks, v_blocks, k_mean, rel_bias)
            x = x + o @ w_o[j]
        x = x + swiglu(rmsnorm(x, norm_ffn[layer]), w_gate_up[layer], w_down[layer])
    return rmsnorm(x, final_norm)


DEPTH_2 = 1

F32 = jnp.float32
RMS_EPS = 1e-6
N_ATTN_HEADS = 8
ATTN_HEAD_DIM = 64
ATTN_W = N_ATTN_HEADS * ATTN_HEAD_DIM
IDX_HEADS = 16
IDX_DIM = 32
IDX_Q = IDX_HEADS * IDX_DIM
TOPK_MAX = 256
Q_BLOCK_2 = 64
N_BUCKETS = 32
RWKV_HEADS = 8
RWKV_HEAD = 64
RWKV_W = RWKV_HEADS * RWKV_HEAD
DECAY_LORA = 64
ICLR_LORA = 64
GATE_LORA = 128
RWKV_IN = 3 * RWKV_W + DECAY_LORA + ICLR_LORA + GATE_LORA
GN_EPS = 64e-5
RWKV_START = 3 * ATTN_W + IDX_Q + IDX_DIM + IDX_HEADS
N_IN = RWKV_START + RWKV_IN + 2 * D_MODEL
IN_SPLITS = (ATTN_W, 2 * ATTN_W, 3 * ATTN_W, 3 * ATTN_W + IDX_Q,
             3 * ATTN_W + IDX_Q + IDX_DIM, RWKV_START,
             RWKV_START + RWKV_IN, RWKV_START + RWKV_IN + D_MODEL)
RWKV_SPLITS = (RWKV_W, 2 * RWKV_W, 3 * RWKV_W, 3 * RWKV_W + DECAY_LORA,
               3 * RWKV_W + DECAY_LORA + ICLR_LORA)
N_EXPERTS = 64
N_GROUPS = 8
TOPK_GROUPS = 4
MOE_TOPK = 8
EXPERT_FF = 256
ROUTED_SCALE = 2.5
EXPERT_BLOCK = 128


def rms_norm(x, g):
    xf = x.astype(F32)
    y = xf * lax.rsqrt(jnp.mean(xf * xf, axis=-1, keepdims=True) + RMS_EPS)
    return (y * g.astype(F32)).astype(x.dtype)

def t5_bucket(rel):
    n = jnp.maximum(rel, 0)
    max_exact = N_BUCKETS // 2
    nf = jnp.maximum(n, 1).astype(F32)
    large = max_exact + (jnp.log(nf / max_exact) / math.log(MAX_DISTANCE / max_exact)
                         * (N_BUCKETS - max_exact)).astype(jnp.int32)
    large = jnp.minimum(large, N_BUCKETS - 1)
    return jnp.where(n < max_exact, n, large)

def dsa_sparse_attention(q, k, v, q_idx, k_idx, w_idx, rel_bias):
    B, S = q.shape[0], q.shape[1]
    top_k = min(TOPK_MAX, S // 4)
    nb = S // Q_BLOCK_2
    k_flat = k.reshape(B, S, ATTN_W)
    v_flat = v.reshape(B, S, ATTN_W)
    key_pos = jnp.arange(S, dtype=jnp.int32)
    idx_scale = (IDX_HEADS ** -0.5) * (IDX_DIM ** -0.5)

    def to_blocks(t):
        return jnp.moveaxis(t.reshape((B, nb, Q_BLOCK_2) + t.shape[2:]), 1, 0)

    def block(args):
        qb, qib, wib, start = args
        q_pos = start + jnp.arange(Q_BLOCK_2, dtype=jnp.int32)
        dots = jnp.einsum('bqhd,bsd->bqhs', qib, k_idx, preferred_element_type=F32)
        idx_score = jnp.einsum('bqhs,bqh->bqs', jax.nn.relu(dots), wib.astype(F32)) * idx_scale
        causal = key_pos[None, :] <= q_pos[:, None]
        idx_score = jnp.where(causal[None], idx_score, -jnp.inf)
        _, sel = lax.top_k(idx_score, top_k)
        kg = jax.vmap(lambda kf, i: kf[i])(k_flat, sel).reshape(B, Q_BLOCK_2, top_k, N_ATTN_HEADS, ATTN_HEAD_DIM)
        vg = jax.vmap(lambda vf, i: vf[i])(v_flat, sel).reshape(B, Q_BLOCK_2, top_k, N_ATTN_HEADS, ATTN_HEAD_DIM)
        logits = jnp.einsum('bqhd,bqkhd->bqhk', qb, kg, preferred_element_type=F32) * (ATTN_HEAD_DIM ** -0.5)
        rel = q_pos[None, :, None] - sel
        bias = rel_bias[t5_bucket(rel)].astype(F32)
        logits = logits + jnp.moveaxis(bias, -1, 2)
        valid = sel <= q_pos[None, :, None]
        logits = jnp.where(valid[:, :, None, :], logits, -jnp.inf)
        p = jax.nn.softmax(logits, axis=-1).astype(vg.dtype)
        return jnp.einsum('bqhk,bqkhd->bqhd', p, vg)

    starts = jnp.arange(nb, dtype=jnp.int32) * Q_BLOCK_2
    out = lax.map(block, (to_blocks(q), to_blocks(q_idx), to_blocks(w_idx), starts))
    return jnp.moveaxis(out, 0, 1).reshape(B, S, ATTN_W)

def wkv7_scan(r, decay, k, v, a, b):
    B, S, H, N = r.shape

    def step(state, inp):
        r_t, w_t, k_t, v_t, a_t, b_t = inp
        sa = jnp.einsum('bhij,bhj->bhi', state, a_t)
        state = state * w_t[:, :, None, :] + sa[..., None] * b_t[:, :, None, :] + v_t[..., None] * k_t[:, :, None, :]
        y = jnp.einsum('bhij,bhj->bhi', state, r_t)
        return state, y

    xs = tuple(jnp.moveaxis(t, 1, 0) for t in (r, decay, k, v, a, b))
    _, ys = lax.scan(step, jnp.zeros((B, H, N, N), F32), xs)
    return jnp.moveaxis(ys, 0, 1)

def rwkv7_branch(z, tshift_mu, decay_w0, decay_up, iclr_a0, iclr_up, gate_up, k_k, k_a, r_k, lnx_g, lnx_b):
    B, S = z.shape[0], z.shape[1]
    z_prev = jnp.pad(z[:, :-1], ((0, 0), (1, 0), (0, 0)))
    z = (z + tshift_mu * (z_prev - z)).astype(F32)
    r, k, v, wd, ad, gd = jnp.split(z, RWKV_SPLITS, axis=-1)
    w_log = -jax.nn.softplus(-(decay_w0.astype(F32) + jnp.tanh(wd) @ decay_up.astype(F32))) - 0.5
    decay = jnp.exp(-jnp.exp(w_log))
    a = jax.nn.sigmoid(iclr_a0.astype(F32) + ad @ iclr_up.astype(F32))
    g = jax.nn.sigmoid(gd) @ gate_up.astype(F32)
    heads = lambda t: t.reshape(B, S, RWKV_HEADS, RWKV_HEAD)
    kk = heads(k * k_k.astype(F32))
    kk = kk / jnp.maximum(jnp.sqrt(jnp.sum(kk * kk, axis=-1, keepdims=True)), 1e-12)
    k = k * (1.0 + (a - 1.0) * k_a.astype(F32))
    r, k, v, decay, a = heads(r), heads(k), heads(v), heads(decay), heads(a)
    y = wkv7_scan(r, decay, k, v, -kk, kk * a)
    mu = jnp.mean(y, axis=-1, keepdims=True)
    var = jnp.mean(jnp.square(y - mu), axis=-1, keepdims=True)
    yn = ((y - mu) * lax.rsqrt(var + GN_EPS)).reshape(B, S, RWKV_W)
    yn = yn * lnx_g.astype(F32) + lnx_b.astype(F32)
    bonus = (jnp.sum(r * k * r_k.astype(F32), axis=-1, keepdims=True) * v).reshape(B, S, RWKV_W)
    return (yn + bonus) * g

def swiglu_2(h, wg, wu, wd):
    return (jax.nn.silu(h @ wg) * (h @ wu)) @ wd

def moe_ffn(h, router_w, router_bias, exp_gate, exp_up, exp_down, sh_gate, sh_up, sh_down):
    B, S, D = h.shape
    T = B * S
    hf = h.reshape(T, D)
    scores = jax.nn.sigmoid(jnp.einsum('td,de->te', hf, router_w, preferred_element_type=F32))
    choice = scores + router_bias.astype(F32)
    grp_score = lax.top_k(choice.reshape(T, N_GROUPS, N_EXPERTS // N_GROUPS), 2)[0].sum(-1)
    _, top_g = lax.top_k(grp_score, TOPK_GROUPS)
    gmask = jnp.any(top_g[:, :, None] == jnp.arange(N_GROUPS)[None, None, :], axis=1)
    emask = jnp.repeat(gmask, N_EXPERTS // N_GROUPS, axis=1)
    _, top_e = lax.top_k(jnp.where(emask, choice, -jnp.inf), MOE_TOPK)
    gw = jnp.take_along_axis(scores, top_e, axis=1)
    gw = gw / jnp.sum(gw, axis=-1, keepdims=True) * ROUTED_SCALE
    A = T * MOE_TOPK
    flat_e = top_e.reshape(A)
    order = jnp.argsort(flat_e)
    se = flat_e[order]
    counts = jnp.bincount(flat_e, length=N_EXPERTS)
    padded = (counts + EXPERT_BLOCK - 1) // EXPERT_BLOCK * EXPERT_BLOCK
    start = jnp.cumsum(counts) - counts
    pend = jnp.cumsum(padded)
    pstart = pend - padded
    dest = pstart[se] + jnp.arange(A, dtype=jnp.int32) - start[se]
    n_blocks = -(-A // EXPERT_BLOCK) + N_EXPERTS
    P = n_blocks * EXPERT_BLOCK
    slot_tok = jnp.zeros((P,), jnp.int32).at[dest].set((order // MOE_TOPK).astype(jnp.int32))
    slot_w = jnp.zeros((P,), F32).at[dest].set(gw.reshape(A)[order])
    block_start = jnp.arange(n_blocks, dtype=jnp.int32) * EXPERT_BLOCK
    block_e = jnp.minimum(jnp.sum(pend[None, :] <= block_start[:, None], axis=1), N_EXPERTS - 1)

    def step(y, blk):
        tok, wt, e = blk
        out = swiglu_2(hf[tok], exp_gate[e], exp_up[e], exp_down[e])
        return y.at[tok].add(out.astype(F32) * wt[:, None]), None

    y, _ = lax.scan(step, jnp.zeros((T, D), F32),
                    (slot_tok.reshape(n_blocks, EXPERT_BLOCK), slot_w.reshape(n_blocks, EXPERT_BLOCK), block_e))
    shared = swiglu_2(hf, sh_gate, sh_up, sh_down)
    return (y.astype(h.dtype) + shared).reshape(B, S, D)

def hybrid_layer(x, c, ada_w, ada_b, norm1_g, w_in, rel_bias, tshift_mu, decay_w0, decay_up,
                 iclr_a0, iclr_up, gate_up, k_k, k_a, r_k, lnx_g, lnx_b, w_attn_br, w_rwkv_br,
                 w_out, norm2_g, router_w, router_bias, exp_gate, exp_up, exp_down,
                 sh_gate, sh_up, sh_down):
    B, S, D = x.shape
    mod = (jax.nn.silu(c.astype(F32)) @ ada_w.astype(F32) + ada_b.astype(F32)).astype(x.dtype)
    sh1, sc1, g1, sh2, sc2, g2 = [m[:, None, :] for m in jnp.split(mod, 6, axis=-1)]
    h = rms_norm(x, norm1_g) * (1 + sc1) + sh1
    z = h @ w_in
    q, k, v, iq, ik, iw, zr, ga, gr = jnp.split(z, IN_SPLITS, axis=-1)
    hs = lambda t: t.reshape(B, S, N_ATTN_HEADS, ATTN_HEAD_DIM)
    attn = dsa_sparse_attention(hs(q), hs(k), hs(v), iq.reshape(B, S, IDX_HEADS, IDX_DIM), ik, iw, rel_bias)
    rw = rwkv7_branch(zr, tshift_mu, decay_w0, decay_up, iclr_a0, iclr_up, gate_up,
                      k_k, k_a, r_k, lnx_g, lnx_b).astype(x.dtype)
    mixed = jax.nn.sigmoid(ga) * (attn @ w_attn_br) + jax.nn.sigmoid(gr) * (rw @ w_rwkv_br)
    x = x + g1 * (mixed @ w_out)
    h2 = rms_norm(x, norm2_g) * (1 + sc2) + sh2
    x = x + g2 * moe_ffn(h2, router_w, router_bias, exp_gate, exp_up, exp_down, sh_gate, sh_up, sh_down)
    return x

def second_inputs(seed: int = 0) -> dict:
    key = jax.random.key(seed)
    ks = iter(jax.random.split(key, 40))
    L, D = DEPTH_2, D_MODEL

    def nrm(shape, scale):
        return jax.random.normal(next(ks), shape, F32) * scale

    def uni(shape, lo, hi):
        return jax.random.uniform(next(ks), shape, F32, lo, hi)

    return {
        'x': nrm((BATCH, SEQ, D), 1.0),
        'c': nrm((BATCH, D), 1.0),
        'ada_w': nrm((L, D, 6 * D), 0.5 * D ** -0.5),
        'ada_b': nrm((L, 6 * D), 0.02),
        'norm1_g': 1.0 + nrm((L, D), 0.02),
        'w_in': nrm((L, D, N_IN), D ** -0.5),
        'rel_bias': nrm((N_BUCKETS, N_ATTN_HEADS), 0.5),
        'tshift_mu': uni((L, RWKV_IN), 0.0, 1.0),
        'decay_w0': uni((L, RWKV_W), -3.0, 1.0),
        'decay_up': nrm((L, DECAY_LORA, RWKV_W), 0.1),
        'iclr_a0': nrm((L, RWKV_W), 0.5),
        'iclr_up': nrm((L, ICLR_LORA, RWKV_W), ICLR_LORA ** -0.5),
        'gate_up': nrm((L, GATE_LORA, RWKV_W), GATE_LORA ** -0.5),
        'k_k': 0.85 + nrm((L, RWKV_W), 0.02),
        'k_a': 1.0 + nrm((L, RWKV_W), 0.02),
        'r_k': nrm((L, RWKV_HEADS, RWKV_HEAD), 0.1),
        'lnx_g': 1.0 + nrm((L, RWKV_W), 0.02),
        'lnx_b': nrm((L, RWKV_W), 0.02),
        'w_attn_br': nrm((L, ATTN_W, D), ATTN_W ** -0.5),
        'w_rwkv_br': nrm((L, RWKV_W, D), RWKV_W ** -0.5),
        'w_out': nrm((L, D, D), D ** -0.5),
        'norm2_g': 1.0 + nrm((L, D), 0.02),
        'router_w': nrm((L, D, N_EXPERTS), D ** -0.5),
        'router_bias': nrm((L, N_EXPERTS), 0.01),
        'exp_gate': nrm((L, N_EXPERTS, D, EXPERT_FF), D ** -0.5),
        'exp_up': nrm((L, N_EXPERTS, D, EXPERT_FF), D ** -0.5),
        'exp_down': nrm((L, N_EXPERTS, EXPERT_FF, D), EXPERT_FF ** -0.5),
        'sh_gate': nrm((L, D, EXPERT_FF), D ** -0.5),
        'sh_up': nrm((L, D, EXPERT_FF), D ** -0.5),
        'sh_down': nrm((L, EXPERT_FF, D), EXPERT_FF ** -0.5),
        'final_g': 1.0 + nrm((D,), 0.02),
    }

def second_block(x, c, ada_w, ada_b, norm1_g, w_in, rel_bias, tshift_mu, decay_w0, decay_up,
              iclr_a0, iclr_up, gate_up, k_k, k_a, r_k, lnx_g, lnx_b, w_attn_br, w_rwkv_br,
              w_out, norm2_g, router_w, router_bias, exp_gate, exp_up, exp_down,
              sh_gate, sh_up, sh_down, final_g):
    for l in range(DEPTH_2):
        x = hybrid_layer(x, c, ada_w[l], ada_b[l], norm1_g[l], w_in[l], rel_bias, tshift_mu[l],
                         decay_w0[l], decay_up[l], iclr_a0[l], iclr_up[l], gate_up[l], k_k[l],
                         k_a[l], r_k[l], lnx_g[l], lnx_b[l], w_attn_br[l], w_rwkv_br[l], w_out[l],
                         norm2_g[l], router_w[l], router_bias[l], exp_gate[l], exp_up[l],
                         exp_down[l], sh_gate[l], sh_up[l], sh_down[l])
    return rms_norm(x, final_g)


def setup_inputs(seed=0):
    out = dict(first_inputs(seed))
    for name, value in second_inputs(seed + 1).items():
        if name != "x":
            out[name + "_2"] = value
    return out


def reference(
    x, norm_mixer, norm_ffn, pool_w, pool_scale, kv_norm, w_kv, w_q, w_o, rel_bias, w_gate_up,
    w_down, final_norm, c_2, ada_w_2, ada_b_2, norm1_g_2, w_in_2, rel_bias_2, tshift_mu_2,
    decay_w0_2, decay_up_2, iclr_a0_2, iclr_up_2, gate_up_2, k_k_2, k_a_2, r_k_2, lnx_g_2,
    lnx_b_2, w_attn_br_2, w_rwkv_br_2, w_out_2, norm2_g_2, router_w_2, router_bias_2,
    exp_gate_2, exp_up_2, exp_down_2, sh_gate_2, sh_up_2, sh_down_2, final_g_2,
):
    x = first_block(
        x, norm_mixer, norm_ffn, pool_w, pool_scale, kv_norm, w_kv, w_q, w_o, rel_bias,
        w_gate_up, w_down, final_norm,
    )
    return second_block(
        x, c_2, ada_w_2, ada_b_2, norm1_g_2, w_in_2, rel_bias_2, tshift_mu_2, decay_w0_2,
        decay_up_2, iclr_a0_2, iclr_up_2, gate_up_2, k_k_2, k_a_2, r_k_2, lnx_g_2, lnx_b_2,
        w_attn_br_2, w_rwkv_br_2, w_out_2, norm2_g_2, router_w_2, router_bias_2, exp_gate_2,
        exp_up_2, exp_down_2, sh_gate_2, sh_up_2, sh_down_2, final_g_2,
    )


_drawn_inputs = setup_inputs


def setup_inputs(seed=0):
    import zlib

    import numpy as np

    out = dict(_drawn_inputs(seed))
    spreads = {}
    factors = {'norm1_g_2': 2.681,
     'k_k_2': 47.576,
     'k_a_2': 4.667,
     'lnx_g_2': 30.829,
     'lnx_b_2': 23.595,
     'final_g_2': 7.565,
     'norm2_g_2': 4.289}
    for name, (base, spread) in spreads.items():
        noise = np.random.default_rng([zlib.crc32(name.encode()), seed]).standard_normal(out[name].shape)
        drawn = base * np.exp(spread * noise) if base else spread * noise
        out[name] = jnp.asarray(drawn.astype(out[name].dtype))
    for name, factor in factors.items():
        out[name] = (out[name] * factor).astype(out[name].dtype)
    return out
```

```python
import math
from contextlib import ExitStack

import numpy as np
import concourse.bass as bass
from concourse import mybir

F32 = mybir.dt.float32
BF16 = mybir.dt.bfloat16
ALU = mybir.AluOpType
ACT = mybir.ActivationFunctionType
AX_X = mybir.AxisListType.X

P = 128
T = 256
TB = T // P
D = 1024
KC = D // P
D_FF = 2816
FFN_CHUNKS = D_FF // P
HEADS_1, HEADS_2, HEAD = 16, 8, 64
ATTN_W = HEADS_2 * HEAD
AC = ATTN_W // P
IDX_HEADS, IDX_DIM, TOP_KEYS = 16, 32, 64
BUCKETS, MAX_DISTANCE = 32, 128
WINDOWS = (2, 4, 8, 16)
PAD = 16
CH = 64
NCH = T // CH
ZR = 14
EXPERTS, GROUPS, TOP_GROUPS, MOE_TOPK, EXPERT_FF = 64, 8, 4, 8, 256
ROUTED_SCALE = 2.5
EPS, GN_EPS = 1e-6, 64e-5
SHIFTS = 32
MASKED = -1e30
TAKEN = -3e38

TILE = KC * P
SLOT = 3 * TILE
RING = 11
S_FFN1 = 0
S_KVQO = S_FFN1 + FFN_CHUNKS
S_ADA = S_KVQO + 11
S_FFN2 = S_ADA + 16
S_WIN = S_FFN2 + FFN_CHUNKS
S_BR = S_WIN + 16
N_SLOTS = S_BR + 6
UNIT = KC * 2 * EXPERT_FF + 2 * D
UNITS = 4

VEC_PARTS = [("norm_mixer0", 8), ("norm_mixer1", 8), ("norm_ffn0", 8), ("norm_ffn1", 8), ("pool_scale", 8),
             ("kv_norm", 8), ("final_norm", 8), ("norm1_g", 8), ("norm2_g", 8), ("final_g", 8), ("c", 8),
             ("ada_b", 48), ("tshift_mu", 14), ("decay_w0", 4), ("iclr_a0", 4), ("k_k", 4), ("k_a", 4),
             ("r_k", 4), ("lnx_g", 4), ("lnx_b", 4)]
VEC = {}
_n = 0
for _name, _w in VEC_PARTS:
    VEC[_name] = (_n, _n + _w)
    _n += _w
N_VEC = _n

LEVELS = [2, 4, 8, 16, 32]
CONST_PARTS = [("ident", 128), ("headones", 128), ("strict_t", 64), ("upto_t", 64), ("first", 64), ("first_t", 64),
               ("levels_t", 64 * len(LEVELS)), ("eye", 64), ("causal", 384)]
CONST = {}
_n = 0
for _name, _w in CONST_PARTS:
    CONST[_name] = (_n, _n + _w)
    _n += _w
N_CONST = _n


def constants():
    c = np.zeros((P, N_CONST), np.float32)

    def put(name, a):
        c[:, CONST[name][0]:CONST[name][1]] = a

    put("ident", np.eye(P))
    put("headones", np.kron(np.eye(2), np.ones((HEAD, HEAD))))
    s, t = np.meshgrid(np.arange(CH), np.arange(CH), indexing="ij")
    two = lambda m: np.concatenate([m, m], 0)
    put("strict_t", two(s < t))
    put("upto_t", two(s <= t))
    put("first", two((s // 2 == t // 2) & (s > t)))
    put("first_t", two((s // 2 == t // 2) & (s < t)))
    put("levels_t", np.concatenate([two((s // (2 * b) == t // (2 * b)) & (s // b % 2 == 0) & (t // b % 2 == 1)) for b in LEVELS], 1))
    put("eye", two(s == t))
    q = np.arange(P)[:, None]
    k = np.arange(T)[None, :]
    put("causal", np.concatenate([np.where(k <= q + P, 0.0, MASKED), np.where(k[:, :P] <= q, 0.0, MASKED)], 1))
    return c


def bias_selector():
    dist = 255 - np.arange(2 * T)
    n = np.maximum(dist, 0)
    half = BUCKETS // 2
    far = half + (np.log(np.maximum(n, half).astype(np.float32) / np.float32(half)) / np.float32(math.log(MAX_DISTANCE / half)) * half).astype(np.int32)
    bucket = np.where(n < half, n, np.minimum(far, BUCKETS - 1))
    m = np.zeros((BUCKETS + 1, 2 * T), np.float32)
    m[bucket, np.arange(2 * T)] = dist >= 0
    m[BUCKETS] = np.where(dist >= 0, 0.0, MASKED)
    return m


def pool_inverse_counts():
    t = np.arange(T)
    rows = [1.0 / np.minimum(t + 1, w).astype(np.float32) for w in WINDOWS]
    return np.broadcast_to(np.stack(rows).astype(np.float32)[None], (P, 4, T)).copy()


def build(nc, xT, vec, consts, selector, inv_count, pool_w, ws, rel, lora, router, router_bias, experts, out):
    bias_line = nc.dram_tensor("bias_line", (HEADS_1 + HEADS_2, SHIFTS, 2 * T), F32, kind="Internal").ap()
    mod_line = nc.dram_tensor("mod_line", (6 * D,), F32, kind="Internal").ap()
    gate_rows = nc.dram_tensor("gate_rows", (EXPERTS, T), F32, kind="Internal").ap()

    with ExitStack() as ctx:
        def sb(name, shape, dt=F32):
            return ctx.enter_context(nc.sbuf_tensor(name, shape, dt))

        def sem(name):
            return ctx.enter_context(nc.semaphore(name))

        ring = sb("ring", [P, RING * SLOT])
        x = sb("x", [P, KC, T])
        vecs = sb("vecs", [P, N_VEC])
        con = sb("con", [P, N_CONST])
        ones = sb("ones", [P, P])
        zeros = sb("zeros", [P, 512], BF16)
        scr = sb("scr", [P, 14600])
        rt = sb("rt", [P, T])
        rinv = sb("rinv", [P, T])
        small = sb("small", [P, 64])
        mod = sb("mod", [P, 48])
        scale1 = sb("scale1", [P, KC])
        scale2 = sb("scale2", [P, KC])
        relw = sb("relw", [BUCKETS + 1, HEADS_1 + HEADS_2])
        banks = ctx.enter_context(nc.psum_tensor("banks", [P, 8, 512], F32))
        B = [banks[:, i, :] for i in range(8)]

        def view(lo, *dims, base=scr):
            n = int(np.prod(dims))
            v = base[:, lo:lo + n]
            if len(dims) == 2:
                return v.rearrange("p (a b) -> p a b", a=dims[0])
            if len(dims) == 3:
                return v.rearrange("p (a b c) -> p a b c", a=dims[0], b=dims[1])
            return v

        def slot(n):
            return ring[:, (n % RING) * SLOT:(n % RING + 1) * SLOT]

        def vcol(name, c):
            return vecs[:, VEC[name][0] + c:VEC[name][0] + c + 1]

        def cst(name):
            return con[:, CONST[name][0]:CONST[name][1]]

        ident = cst("ident")
        headones = cst("headones")
        eps, gn_eps = small[:, 0:1], small[:, 1:2]

        h = view(0, KC, T)
        sq = view(2048, KC, T)
        hp, pw_b, pw_c = view(4352, KC, PAD + T), view(6528, KC, PAD + T), view(8704, KC, PAD + T)
        icnt, poolw = view(10880, 4, T), view(11904, 4, 2, T)
        sig_f, gated, act_f = view(4352, 2, T), view(4864, 2, T), view(5376, 2, T)
        hq = sq
        ex, pts = view(2048, 2, 384), view(2816, 2, 384)
        nmax, rsum, rrec = small[:, 8:12], small[:, 12:16], small[:, 16:20]
        q1, k1, v1, bias1 = view(4352, KC, T), view(6400, KC, T), view(8448, TB, D), view(10496, HEADS_1, T)
        csil, csig = small[:, 20:28], small[:, 28:36]
        modrow, mod48 = view(8448, 3, 512), view(10496, P)
        line_sb, sel_sb = view(2048, 2 * T), view(2816, 2 * T)
        q2, k2, v2, iqT = view(2048, AC, T), view(3072, AC, T), view(4096, TB, ATTN_W), view(5120, AC, T)
        ikr, iw = view(6144, T), view(6400, TB, IDX_HEADS)
        zr = view(6432, ZR, T + 1)
        sig_a, sig_r = view(10030, KC, T), view(12078, KC, T)
        o2, rw = view(0, AC, T), view(1024, AC, T)

        def spare(lo, *dims):
            return view(5 * SLOT + lo, *dims, base=ring)

        bias2, relu_i = spare(0, HEADS_2, T), spare(2048, 2, 8, T)
        work, mask2, top8 = spare(6144, 384), spare(6528, 384), spare(6912, 2, 8)
        ex2, pts2 = spare(8192, 2, 384), spare(8960, 2, 384)
        zs = spare(0, ZR, T)
        r_t, k_t, v_t, lo_t = zs[:, 0:4, :], zs[:, 4:8, :], zs[:, 8:12, :], zs[:, 12:14, :]
        b1, b2, b3, b4, b5, b6 = (spare(3584 + 1024 * i, AC, T) for i in range(6))
        vt, bt, kt = (spare(9728 + 1024 * i, NCH * AC, CH) for i in range(3))
        m_ab, m_lev = spare(12800, NCH * AC, CH), spare(13824, NCH * AC, CH)
        loraw = spare(12800, 2 * ATTN_W)
        m_ak, m_rb, m_rk, inv = (view(2048 + 1024 * i, NCH * AC, CH) for i in range(4))
        f0, f1, f2 = (view(2048 + 1024 * i, AC, T) for i in range(3))
        inv_t, xm = view(6432, NCH * AC, CH), view(7456, NCH * AC, CH)
        gst, rhs_u, u_sb = view(8480, 2, AC, CH), view(8992, AC, CH), view(9248, AC, CH)
        p_end = small[:, 40:56].rearrange("p (a b) -> p a b", a=AC)
        mixed, mixed_r = view(6432, KC, T), view(4096, KC, T)
        score_e, choice, grp8, gsum, gtop, gwork, cwork, sel_e, den = (
            view(6432, TB, EXPERTS), view(6560, TB, EXPERTS), view(6688, TB, GROUPS, 8), view(6816, TB, GROUPS), view(6832, TB, 8),
            view(6848, TB, GROUPS), view(6864, TB, EXPERTS), view(6992, TB, EXPERTS), view(7120, TB))
        gates_t = view(7424, T)
        routerw, rbias = view(10030, KC, EXPERTS), view(10542, EXPERTS)
        wb = view(8192, UNITS, T)
        weighted = view(9216, 2, T)

        def unit(u):
            return ring[:, u * UNIT:(u + 1) * UNIT]

        SHARED_UNIT = ring[:, 8 * SLOT:10 * SLOT]

        landed = [sem(f"weights_landed{i}") for i in range(RING)]
        w_used = sem("weights_used")
        x_loaded, vec_loaded, const_loaded, sel_loaded, pool_loaded = (sem(s) for s in ("x_loaded", "vec_loaded", "const_loaded", "sel_loaded", "pool_loaded"))
        sq_ready, ss_ready, rt_ready, h_ready, x_ready = (sem(s) for s in ("sq_ready", "ss_ready", "rt_ready", "h_ready", "x_ready"))
        ones_ready, line_ready, line_copied, line_stored, bias_loaded = (sem(s) for s in ("ones_ready", "line_ready", "line_copied", "line_stored", "bias_loaded"))
        pool_d, pool_y = sem("pool_d"), sem("pool_y")
        gu_ready, sig_ready, act_ready = sem("gu_ready"), sem("sig_ready"), sem("act_ready")
        proj_ready, proj_used, res_ready = sem("proj_ready"), sem("proj_used"), sem("res_ready")
        s_ready, s_used, max_ready, exp_ready, p_ready, pt_ready, pts_ready, o_ready, o_copied = (
            sem(s) for s in ("s_ready", "s_used", "max_ready", "exp_ready", "p_ready", "pt_ready", "pts_ready", "o_ready", "o_copied"))
        csig_ready, csil_ready, mod_rows, mod_copied, mod_stored, mod_back, mod_turned, mod_ready = (
            sem(s) for s in ("csig_ready", "csil_ready", "mod_rows", "mod_copied", "mod_stored", "mod_back", "mod_turned", "mod_ready"))
        out_ready, out_done = sem("out_ready"), sem("out_done")
        bias2_loaded, lora_loaded, router_loaded = sem("bias2_loaded"), sem("lora_loaded"), sem("router_loaded")
        idx_ready, relu_ready, relu_used = sem("idx_ready"), sem("relu_ready"), sem("relu_used")
        shifted, lora_in, lora_out, decay_ready, iclr_ready = (sem(n) for n in ("shifted", "lora_in", "lora_out", "decay_ready", "iclr_ready"))
        kk_sq, kk_sum, kk_norm, bonus_in, bonus_sum, bonus_used = (sem(n) for n in ("kk_sq", "kk_sum", "kk_norm", "bonus_in", "bonus_sum", "bonus_used"))
        v_ready, tilde_ready, turned, turned_used = (sem(n) for n in ("v_ready", "tilde_ready", "turned", "turned_used"))
        pair_ready, pair_used, level_m, level_x, x_copied, level_d, inv_ready = (
            sem(n) for n in ("pair_ready", "pair_used", "level_m", "level_x", "x_copied", "level_d", "inv_ready"))
        rhs_ready, rhs_copied, u_ready, u_copied, g_ready, state_ready, y_ready, y_copied = (
            sem(n) for n in ("rhs_ready", "rhs_copied", "u_ready", "u_copied", "g_ready", "state_ready", "y_ready", "y_copied"))
        gn_sum, gn_sq, gn_var, gn_rt, rw_ready = (sem(n) for n in ("gn_sum", "gn_sq", "gn_var", "gn_rt", "rw_ready"))
        br_ready, mixed_ready = sem("br_ready"), sem("mixed_ready")
        logits_ready, scores_ready, gates_ready, gates_turned, gates_copied, gates_stored = (
            sem(n) for n in ("logits_ready", "scores_ready", "gates_ready", "gates_turned", "gates_copied", "gates_stored"))
        unit_landed, wb_landed = [sem(f"unit_landed{u}") for u in range(UNITS)], [sem(f"wb_landed{u}") for u in range(UNITS)]
        shared_landed, unit_used, y_all = sem("shared_landed"), sem("unit_used"), sem("y_all")
        dve_step, act_step = sem("dve_step"), sem("act_step")
        block = ctx.enter_context(nc.Block())

        H_BASE = [0, 8, 16, 32, 40, 40, 48, 56]

        PROJ_BANKS = [B[4], B[5], B[7]]
        U_V1, U_K1, U_Q1 = 0, 6, 14
        U_Z = 22
        VGROUPS1 = [(0, 3), (3, 3), (6, 2)]

        @block.sync
        def _(sp):
            sp.dma_start(x[:], xT).then_inc(x_loaded, 16)
            sp.dma_start(vecs[:], vec).then_inc(vec_loaded, 16)
            sp.dma_start(con[:], consts).then_inc(const_loaded, 16)
            sp.dma_start(poolw, pool_w).then_inc(pool_loaded, 16)
            sp.dma_start(icnt, inv_count).then_inc(pool_loaded, 16)
            sp.dma_start(sel_sb[0:BUCKETS + 1, :], selector).then_inc(sel_loaded, 16)
            sp.dma_start(relw[:], rel).then_inc(sel_loaded, 16)

            def load(n, i=0):
                sp.dma_start(slot(n), ws[n + RING * i]).then_inc(landed[n % RING], 16)

            for n in range(RING):
                load(n)
            with sp.Fori(1, N_SLOTS // RING) as i:
                for s in range(RING):
                    sp.wait_ge(w_used, RING * i + (s + 1 - RING))
                    sp.dma_start(slot(s), ws[RING * i + s]).then_inc(landed[s], 16)
            for n in range(N_SLOTS // RING * RING, N_SLOTS):
                sp.wait_ge(w_used, n + 1 - RING)
                load(n)
            sp.wait_ge(x_ready, 24)
            sp.dma_start(SHARED_UNIT, experts[0]).then_inc(shared_landed, 16)
            for u in range(UNITS):
                sp.dma_start(unit(u), experts[1 + u]).then_inc(unit_landed[u], 16)
            with sp.Fori(1, EXPERTS // UNITS) as i:
                for u in range(UNITS):
                    sp.wait_ge(unit_used, UNITS * i + (u + 1 - UNITS))
                    sp.dma_start(unit(u), experts[UNITS * i + (1 + u)]).then_inc(unit_landed[u], 16)
            sp.wait_ge(out_ready, 1)
            sp.dma_start(out, x[:]).then_inc(out_done, 16)
            sp.wait_ge(out_done, 16)

        @block.gpsimd
        def _(pool):
            def load_toeplitz(dst, first, heads, signal):
                for a in range(P // SHIFTS):
                    start = first * SHIFTS * 2 * T + P - 1 - SHIFTS * a
                    src = bass.AP(bias_line.tensor, start, [[2 * T - 1, SHIFTS], [SHIFTS * 2 * T, heads], [1, T]])
                    pool.dma_start(dst[SHIFTS * a:SHIFTS * (a + 1)], src).then_inc(signal, 16)

            pool.wait_ge(line_copied, 1)
            pool.dma_start(bias_line, line_sb[0:HEADS_1 + HEADS_2, :].unsqueeze(1).broadcast_to([HEADS_1 + HEADS_2, SHIFTS, 2 * T])).then_inc(line_stored, 16)
            pool.wait_ge(line_stored, 16)
            pool.wait_ge(x_ready, 4)
            load_toeplitz(bias1, 0, HEADS_1, bias_loaded)
            pool.wait_ge(mod_copied, 4)
            by_row = mod_line.rearrange("(b q n) -> q b n", b=3, q=4)
            for q in range(4):
                pool.dma_start(by_row[q:q + 1], modrow[32 * q:32 * q + 1, :, :]).then_inc(mod_stored, 16)
            pool.wait_ge(mod_stored, 64)
            pool.dma_start(mod48[0:48, :], mod_line.rearrange("(r p) -> r p", p=P)).then_inc(mod_back, 16)
            pool.wait_ge(w_used, S_BR)
            load_toeplitz(bias2, HEADS_1, HEADS_2, bias2_loaded)
            pool.dma_start(loraw, lora).then_inc(lora_loaded, 16)
            pool.wait_ge(x_ready, 24)
            pool.dma_start(routerw, router).then_inc(router_loaded, 16)
            pool.dma_start(rbias, router_bias.partition_broadcast(P)).then_inc(router_loaded, 16)
            pool.wait_ge(gates_copied, 1)
            pool.dma_start(gate_rows, gates_t[0:EXPERTS, :]).then_inc(gates_stored, 16)
            pool.wait_ge(gates_stored, 16)
            for u in range(UNITS):
                pool.dma_start(wb[:, u, :], gate_rows[u:u + 1, :].partition_broadcast(P)).then_inc(wb_landed[u], 16)
            with pool.Fori(1, EXPERTS // UNITS) as i:
                for u in range(UNITS):
                    pool.wait_ge(unit_used, UNITS * i + (u + 1 - UNITS))
                    pool.dma_start(wb[:, u, :], gate_rows[bass.ds(UNITS * i + u, 1), :].partition_broadcast(P)).then_inc(wb_landed[u], 16)

        @block.tensor
        def _(pe):
            def wait_slot(n, i=0):
                pe.wait_ge(landed[n % RING], 16 * (n // RING + 1) + 16 * i)

            def norm_sum(k):
                for g in range(4):
                    pe.wait_ge(sq_ready, 4 * k + g + 1)
                    for c in (2 * g, 2 * g + 1):
                        mm = nc.tensor.matmul(B[6][:, 0:T], ones[:], sq[:, c, :], start=(c == 0), stop=(c == KC - 1))
                mm.then_inc(ss_ready, 1)

            def clear_y():
                for b in range(4):
                    nc.tensor.matmul(B[b], zeros[:, 0:P], zeros[:], start=True, stop=False, skip_group_check=True)

            def gate_up(bank, gate, up):
                for half, w in ((0, gate), (T, up)):
                    for c in range(KC):
                        mm = nc.tensor.matmul(bank[:, half:half + T], w(c), h[:, c, :], start=(c == 0), stop=(c == KC - 1))
                mm.then_inc(gu_ready, 1)

            def down(w, a):
                for c in range(KC):
                    mm = nc.tensor.matmul(B[c // 2][:, c % 2 * T:c % 2 * T + T], w(c), a, start=False, stop=False, skip_group_check=True)
                return mm

            def ffn(base, k, done):
                clear_y()
                pe.wait_ge(h_ready, H_BASE[k] + KC)
                with pe.Fori(0, 2) as i:
                    for s in range(RING + 1):
                        if s < RING:
                            w = slot(base + s)
                            pe.wait_ge(landed[(base + s) % RING], 16 * ((base + s) // RING + 1) + 16 * i)
                            gate_up(B[4 + s % 2], lambda c: w[:, c * P:(c + 1) * P], lambda c: w[:, TILE + c * P:TILE + (c + 1) * P])
                        if s >= 1:
                            w2 = slot(base + s - 1)
                            pe.wait_ge(act_ready, RING * i + (done + s))
                            down(lambda c: w2[:, 2 * TILE + c * P:2 * TILE + (c + 1) * P], act_f[:, (s - 1) % 2, :]).then_inc(w_used, 1)

            def tile_w(base, i):
                return slot(base + i // 3)[:, i % 3 * TILE:(i % 3 + 1) * TILE]

            def proj(u, n, lhs, rhs, chunks=KC):
                bank = PROJ_BANKS[u % 3]
                if u >= 3:
                    pe.wait_ge(proj_used, u - 2)
                for c in range(chunks):
                    mm = nc.tensor.matmul(bank[:, 0:n], lhs(c), rhs(c), start=(c == 0), stop=(c == chunks - 1))
                return mm.then_inc(proj_ready, 1)

            def attention(heads, n0, qT, kT, v, ex, pts):
                for j in range(heads + 2):
                    if j < heads:
                        r, b = j % 2 * HEAD, B[j % 2]
                        if n0 + j >= 2:
                            pe.wait_ge(s_used, n0 + j - 1)
                        lo = slice(r, r + HEAD)
                        nc.tensor.matmul(b[:, 0:T], qT[lo, j // 2, P:T], kT[lo, j // 2, :], start=True, stop=True)
                        nc.tensor.matmul(b[:, T:T + P], qT[lo, j // 2, 0:P], kT[lo, j // 2, 0:P], start=True, stop=True).then_inc(s_ready, 1)
                    if 1 <= j <= heads:
                        a = j - 1
                        pe.wait_ge(p_ready, n0 + a + 1)
                        b, e = B[2 + a % 2], ex[:, a % 2, :]
                        for d, s in ((0, T), (P, 0), (2 * P, P)):
                            mm = nc.tensor.transpose(b[:, d:d + P], e[:, s:s + P], ident)
                        mm.then_inc(pt_ready, 1)
                    if j >= 2:
                        a = j - 2
                        pe.wait_ge(pts_ready, n0 + a + 1)
                        r, b, pt = a % 2 * HEAD, B[4 + a // 2 % 2], pts[:, a % 2, :]
                        if a % 2 == 0 and (n0 + a) // 2 >= 2:
                            pe.wait_ge(o_copied, (n0 + a) // 2 - 1)
                        nc.tensor.matmul(b[r:r + HEAD, 0:T], v[:, 0, a * HEAD:(a + 1) * HEAD], pt[:, 0:T], start=True, stop=False, skip_group_check=True)
                        nc.tensor.matmul(b[r:r + HEAD, P:T], v[:, 1, a * HEAD:(a + 1) * HEAD], pt[:, T:T + P], start=False, stop=True, skip_group_check=True).then_inc(o_ready, 1)

            pe.wait_ge(ones_ready, 1)
            pe.wait_ge(sel_loaded, 32)
            nc.tensor.matmul(B[7][0:HEADS_1 + HEADS_2, :], relw[:], sel_sb[0:BUCKETS + 1, :], start=True, stop=True).then_inc(line_ready, 1)

            norm_sum(0)
            pe.wait_ge(pool_loaded, 32)
            pe.wait_ge(const_loaded, 16)
            for g in range(4):
                pe.wait_ge(pool_d, g + 1)
                for e in range(2):
                    for c in range(2):
                        mm = nc.tensor.matmul(B[g][:, e * T:(e + 1) * T], poolw[:, g, c, e * P:(e + 1) * P], h[:, 2 * g + c, :], start=(c == 0), stop=(c == 1))
                mm.then_inc(pool_y, 1)
            norm_sum(1)
            ffn(S_FFN1, 1, 0)
            norm_sum(2)
            pe.wait_ge(h_ready, H_BASE[2] + KC)
            for g, (t0, nt) in enumerate(VGROUPS1):
                wait_slot(S_KVQO + g)
                w = slot(S_KVQO + g)[:, 0:nt * TILE].rearrange("p (t c m) -> p t c m", t=nt, c=KC)
                for tb in range(TB):
                    proj(U_V1 + 2 * g + tb, nt * P, lambda c: h[:, c, tb * P:(tb + 1) * P], lambda c: w[:, :, c, :])
            used = 0
            for i in range(8, 24):
                if i == 16:
                    pe.wait_ge(h_ready, H_BASE[2] + 2 * KC)
                wait_slot(S_KVQO + i // 3)
                w = tile_w(S_KVQO, i)
                src = h if i < 16 else hq
                proj(U_K1 + i - 8, T, lambda c: w[:, c * P:(c + 1) * P], lambda c: src[:, c, :])
            pe.wait_ge(proj_ready, U_Z)
            pe.sem_inc(w_used, 8)
            pe.wait_ge(proj_used, U_Z)
            attention(HEADS_1, 0, q1, k1, v1, ex, pts)
            pe.wait_ge(o_copied, HEADS_1 // 2)
            for i in range(24, 32):
                wait_slot(S_KVQO + i // 3)
                w, dc = tile_w(S_KVQO, i), i - 24
                for c in range(KC):
                    mm = nc.tensor.matmul(B[dc // 2][:, dc % 2 * T:dc % 2 * T + T], w[:, c * P:(c + 1) * P], h[:, c, :], start=(c == 0), stop=(c == KC - 1))
                if dc % 2:
                    mm.then_inc(res_ready, 1)
            pe.wait_ge(res_ready, 4)
            pe.sem_inc(w_used, 3)
            pe.wait_ge(csil_ready, 1)
            pe.wait_ge(x_ready, 12)
            for n in range(16):
                wait_slot(S_ADA + n)
                c, w = n // 2, slot(S_ADA + n)
                for b in range(6):
                    j = n % 2 * 6 + b
                    r = 32 * (j % 4)
                    mm = nc.tensor.matmul(B[j // 4][r:r + 1, :], csil[:, c:c + 1], w[:, b * 512:(b + 1) * 512], start=(c == 0), stop=(c == KC - 1),
                                          skip_group_check=True, tile_position=(0, r))
                mm.then_inc(mod_rows, 1)
                if n >= 1:
                    pe.wait_ge(mod_rows, n)
                    pe.sem_inc(w_used, 1)
            pe.wait_ge(mod_rows, 16)
            pe.sem_inc(w_used, 1)

            norm_sum(3)
            pe.wait_ge(mod_copied, 4)
            ffn(S_FFN2, 3, FFN_CHUNKS)
            pe.wait_ge(mod_back, 16)
            nc.tensor.transpose(B[7][:, 0:48], mod48[0:48, :], ident[0:48, 0:48]).then_inc(mod_turned, 1)
            norm_sum(4)
            norm_sum(5)
            pe.wait_ge(h_ready, H_BASE[5] + KC)
            u = U_Z
            for t0, w0, nt in ((0, 0, 3 * P), (3, 3, P), (4, 4, IDX_HEADS)):
                wait_slot(S_WIN + t0 // 3)
                w = tile_w(S_WIN, t0)
                if t0 == 0:
                    w3 = slot(S_WIN).rearrange("p (t c m) -> p t c m", t=3, c=KC)
                for tb in range(TB):
                    proj(u, nt, lambda c: h[:, c, tb * P:(tb + 1) * P], (lambda c: w3[:, :, c, :]) if t0 == 0 else (lambda c: w[:, c * P:c * P + nt]))
                    u += 1
                if t0 == 0:
                    pe.wait_ge(proj_ready, u)
                    pe.sem_inc(w_used, 1)
            for i in range(5, 48):
                wait_slot(S_WIN + i // 3)
                w = tile_w(S_WIN, i)
                proj(u, T, lambda c: w[:, c * P:(c + 1) * P], lambda c: h[:, c, :])
                u += 1
                if i % 3 == 0:
                    pe.wait_ge(proj_ready, u - 1)
                    pe.sem_inc(w_used, 1)
            pe.wait_ge(proj_ready, u)
            pe.sem_inc(w_used, 1)
            pe.wait_ge(proj_used, u)

            for n in range(4):
                qb, cp = n // 2, n % 2
                nk = (qb + 1) * P
                if n >= 2:
                    pe.wait_ge(relu_ready, n - 1)
                for cc in range(2):
                    for r in range(4):
                        mm = nc.tensor.matmul(B[n % 2 * 4 + r][:, cc * T:cc * T + nk], iqT[32 * r:32 * r + 32, 2 * cp + cc, qb * P:(qb + 1) * P],
                                              ikr[32 * r:32 * r + 32, 0:nk], start=True, stop=True)
                mm.then_inc(idx_ready, 1)
            pe.wait_ge(relu_ready, 4)
            attention(HEADS_2, HEADS_1, q2, k2, v2, ex2, pts2)
            pe.wait_ge(o_copied, (HEADS_1 + HEADS_2) // 2)
            pe.wait_ge(lora_loaded, 16)
            pe.wait_ge(lora_in, 2)
            for b0, lo, src, col in ((0, slice(0, 64), 0, 0), (2, slice(64, 128), 0, 0), (4, slice(0, 128), 1, ATTN_W)):
                for c in range(AC):
                    mm = nc.tensor.matmul(B[b0 + c // 2][:, c % 2 * T:c % 2 * T + T], loraw[lo, col + c * P:col + (c + 1) * P], lo_t[lo, src, :], start=True, stop=True)
                mm.then_inc(lora_out, 1)

            def head_sums(src, b0):
                for c in range(AC):
                    mm = nc.tensor.matmul(B[b0 + c // 2][:, c % 2 * T:c % 2 * T + T], headones, src[:, c, :], start=True, stop=True)
                return mm

            def pairs(fn):
                for c in range(NCH):
                    for hp in range(AC):
                        for p in range(2):
                            mm = fn(c, hp, slice(p * HEAD, (p + 1) * HEAD))
                return mm

            def block_of(b0, c, hp, rows):
                n = (c * AC + hp) * CH
                return B[b0 + n // 512][rows, n % 512:n % 512 + CH]

            pe.wait_ge(kk_sq, 1)
            head_sums(f0, 6).then_inc(kk_sum, 1)
            pe.wait_ge(lora_out, 3)
            pe.wait_ge(decay_ready, 1)
            pe.wait_ge(bonus_in, 1)
            head_sums(f2, 0).then_inc(bonus_sum, 1)
            pe.wait_ge(tilde_ready, 1)
            pe.wait_ge(bonus_used, 1)
            for n, src in enumerate((v_t, b5, k_t)):
                pairs(lambda c, hp, rows: nc.tensor.matmul(block_of(2 * n, c, hp, rows), src[rows, hp, c * CH:(c + 1) * CH], ident[rows, rows], start=True, stop=True)).then_inc(turned, 1)

            pair_list = [(b5, b4, 6), (b4, b5, 0), (k_t, b4, 2), (b5, b3, 4), (k_t, b3, 6)]
            for n, (lhs, rhs, b0) in enumerate(pair_list):
                if n in (1, 2, 3):
                    pe.wait_ge(turned_used, n)
                if n == 4:
                    pe.wait_ge(pair_used, 1)

                def product(c, hp, rows):
                    t = slice(c * CH, (c + 1) * CH)
                    return nc.tensor.matmul(block_of(b0, c, hp, rows), lhs[rows, hp, t], rhs[rows, hp, t], start=True, stop=True)

                pairs(product).then_inc(pair_ready, 1)
            pe.wait_ge(pair_used, 5)
            for n in range(len(LEVELS)):
                blk = lambda a, c, hp, rows: a[rows, c * AC + hp, :]
                pe.wait_ge(level_m, n + 1)
                pairs(lambda c, hp, rows: nc.tensor.matmul(block_of(0, c, hp, rows), blk(m_lev, c, hp, rows), blk(inv, c, hp, rows), start=True, stop=True)).then_inc(level_x, 1)
                pe.wait_ge(x_copied, n + 1)
                pairs(lambda c, hp, rows: nc.tensor.matmul(block_of(2, c, hp, rows), blk(inv_t, c, hp, rows), blk(xm, c, hp, rows), start=True, stop=True))
                pairs(lambda c, hp, rows: nc.tensor.matmul(block_of(4, c, hp, rows), blk(xm, c, hp, rows), blk(inv_t, c, hp, rows), start=True, stop=True)).then_inc(level_d, 1)
            pe.wait_ge(inv_ready, 1)
            halves = [(hp, slice(p * HEAD, (p + 1) * HEAD)) for hp in range(AC) for p in range(2)]
            for c in range(NCH):
                t = slice(c * CH, (c + 1) * CH)
                g_in = gst[:, (c - 1) % 2]
                if c:
                    pe.wait_ge(state_ready, c)
                for hp, rows in halves:
                    o, n = B[0][rows, hp * CH:(hp + 1) * CH], c * AC + hp
                    if c:
                        nc.tensor.matmul(o, b4[rows, hp, t], g_in[rows, hp, :], start=True, stop=False)
                    mm = nc.tensor.matmul(o, m_ak[rows, n, :], vt[rows, n, :], start=(c == 0), stop=True)
                mm.then_inc(rhs_ready, 1)
                pe.wait_ge(rhs_copied, c + 1)
                for hp, rows in halves:
                    n = c * AC + hp
                    mm = nc.tensor.matmul(B[1][rows, hp * CH:(hp + 1) * CH], inv_t[rows, n, :], rhs_u[rows, hp, :], start=True, stop=True)
                mm.then_inc(u_ready, 1)
                pe.wait_ge(u_copied, c + 1)
                for hp, rows in halves:
                    o, n = B[2][rows, hp * CH:(hp + 1) * CH], c * AC + hp
                    nc.tensor.matmul(o, bt[rows, n, :], u_sb[rows, hp, :], start=True, stop=False)
                    mm = nc.tensor.matmul(o, kt[rows, n, :], vt[rows, n, :], start=False, stop=True)
                mm.then_inc(g_ready, 1)
                if c >= 2:
                    pe.wait_ge(y_copied, c - 1)
                for hp, rows in halves:
                    o, n = B[3 + c % 2][rows, hp * CH:(hp + 1) * CH], c * AC + hp
                    if c:
                        nc.tensor.matmul(o, g_in[rows, hp, :], b3[rows, hp, t], start=True, stop=False)
                    nc.tensor.matmul(o, u_sb[rows, hp, :], m_rb[rows, n, :], start=(c == 0), stop=False)
                    mm = nc.tensor.matmul(o, vt[rows, n, :], m_rk[rows, n, :], start=False, stop=True)
                mm.then_inc(y_ready, 1)
            pe.wait_ge(y_copied, NCH)
            head_sums(b1, 6).then_inc(gn_sum, 1)
            pe.wait_ge(gn_sq, 1)
            head_sums(f0, 0).then_inc(gn_var, 1)
            pe.wait_ge(rw_ready, 1)
            for n, (src, b0) in enumerate(((o2, 0), (rw, 4))):
                for i in range(4):
                    k = 4 * n + i
                    wait_slot(S_BR + k // 3)
                    w = tile_w(S_BR, k)
                    for e in range(2):
                        for c in range(AC):
                            mm = nc.tensor.matmul(B[b0 + i][:, e * T:(e + 1) * T], w[:, (e * AC + c) * P:(e * AC + c + 1) * P], src[:, c, :], start=(c == 0), stop=(c == AC - 1))
                    mm.then_inc(br_ready, 1)
            for dc in range(KC):
                k = 8 + dc
                wait_slot(S_BR + k // 3)
                w = tile_w(S_BR, k)
                if dc == 0:
                    pe.wait_ge(mixed_ready, 4)
                for c in range(KC):
                    mm = nc.tensor.matmul(B[dc // 2][:, dc % 2 * T:dc % 2 * T + T], w[:, c * P:(c + 1) * P], mixed[:, c, :], start=(c == 0), stop=(c == KC - 1))
                if dc % 2:
                    mm.then_inc(res_ready, 1)
            norm_sum(6)
            pe.wait_ge(h_ready, H_BASE[6] + KC)
            pe.wait_ge(router_loaded, 32)
            for tb in range(TB):
                for c in range(KC):
                    mm = nc.tensor.matmul(B[7][:, tb * EXPERTS:(tb + 1) * EXPERTS], h[:, c, tb * P:(tb + 1) * P], routerw[:, c, :], start=(c == 0), stop=(c == KC - 1))
            mm.then_inc(logits_ready, 1)
            clear_y()

            def expert_gate_up(w, f, bank):
                gate_up(bank, lambda c: w[:, c * 512 + f * P:c * 512 + (f + 1) * P], lambda c: w[:, c * 512 + EXPERT_FF + f * P:c * 512 + EXPERT_FF + (f + 1) * P])

            def expert_down(w, f):
                o = KC * 512 + f * D
                return down(lambda c: w[:, o + c * P:o + (c + 1) * P], act_f[:, f, :])

            done = 2 * FFN_CHUNKS
            pe.wait_ge(shared_landed, 16)
            for f in range(2):
                expert_gate_up(SHARED_UNIT, f, B[4 + f])
            pe.wait_ge(gates_ready, 1)
            for tb in range(TB):
                mm = nc.tensor.transpose(B[7][0:EXPERTS, T + tb * P:T + (tb + 1) * P], sel_e[:, tb, :], ident)
            mm.then_inc(gates_turned, 1)
            for f in range(2):
                pe.wait_ge(act_ready, done + f + 1)
                mm = expert_down(SHARED_UNIT, f)
            done += 2
            with pe.Fori(0, EXPERTS // UNITS) as i:
                for s in range(2 * UNITS + 1):
                    if s < 2 * UNITS:
                        if s % 2 == 0:
                            pe.wait_ge(unit_landed[s // 2], 16 * i + 16)
                        expert_gate_up(unit(s // 2), s % 2, B[4 + s % 2])
                    if s >= 1:
                        pe.wait_ge(act_ready, 2 * UNITS * i + (done + s))
                        mm = expert_down(unit((s - 1) // 2), (s - 1) % 2)
                        if s % 2 == 0:
                            mm.then_inc(unit_used, 1)
            norm_sum(7)

        @block.scalar
        def _(act):
            def norm_squares(k):
                for g in range(4):
                    if k == 0:
                        act.wait_ge(x_loaded, 16)
                    else:
                        act.wait_ge(x_ready, 4 * (k - 1) + g + 1)
                    nc.scalar.activation(sq[:, 2 * g:2 * g + 2, :], x[:, 2 * g:2 * g + 2, :], ACT.Square).then_inc(sq_ready, 1)
                act.wait_ge(ss_ready, k + 1)
                nc.scalar.activation(rt[:], B[6][:, 0:T], ACT.Sqrt, scale=1.0 / D, bias=eps).then_inc(rt_ready, 1)

            def ffn(done):
                with act.Fori(0, 2) as i:
                    for s in range(RING):
                        act.wait_ge(gu_ready, RING * i + (done + s + 1))
                        nc.scalar.activation(sig_f[:, s % 2, :], B[4 + s % 2][:, 0:T], ACT.Sigmoid).then_inc(sig_ready, 1)

            def evacuate(u, dst, n=T, func=ACT.Copy):
                act.wait_ge(proj_ready, u + 1)
                nc.scalar.activation(dst, PROJ_BANKS[u % 3][:, 0:n], func).then_inc(proj_used, 1)

            def attention(heads, n0, oT, ex, pts):
                for j in range(heads + 2):
                    if j < heads:
                        act.wait_ge(max_ready, n0 + j + 1)
                        e, k = ex[:, j % 2, :], 2 * (j % 2)
                        nc.scalar.activation(e[:, 0:T], e[:, 0:T], ACT.Exp, bias=nmax[:, k:k + 1], accum_out=rsum[:, k:k + 1])
                        nc.scalar.activation(e[:, T:T + P], e[:, T:T + P], ACT.Exp, bias=nmax[:, k + 1:k + 2], accum_out=rsum[:, k + 1:k + 2]).then_inc(exp_ready, 1)
                    if 1 <= j <= heads:
                        a = j - 1
                        act.wait_ge(pt_ready, n0 + a + 1)
                        if a >= 2:
                            act.wait_ge(o_ready, n0 + a - 1)
                        nc.scalar.activation(pts[:, a % 2, :], B[2 + a % 2][:, 0:384], ACT.Copy).then_inc(pts_ready, 1)
                    if j >= 2 and j % 2:
                        a = (j - 2) // 2
                        act.wait_ge(o_ready, n0 + 2 * a + 2)
                        nc.scalar.activation(oT[:, a, :], B[4 + a % 2][:, 0:T], ACT.Copy).then_inc(o_copied, 1)

            act.wait_ge(line_ready, 1)
            nc.scalar.activation(line_sb[0:HEADS_1 + HEADS_2, :], B[7][0:HEADS_1 + HEADS_2, :], ACT.Copy).then_inc(line_copied, 1)
            act.wait_ge(line_stored, 16)
            act.wait_ge(ones_ready, 1)
            norm_squares(0)
            norm_squares(1)
            ffn(0)
            norm_squares(2)
            for g, (t0, nt) in enumerate(VGROUPS1):
                for tb in range(TB):
                    evacuate(U_V1 + 2 * g + tb, v1[:, tb, t0 * P:(t0 + nt) * P], nt * P)
            for c in range(KC):
                evacuate(U_K1 + c, k1[:, c, :])
            for c in range(KC):
                evacuate(U_Q1 + c, q1[:, c, :])
            attention(HEADS_1, 0, h, ex, pts)
            act.wait_ge(vec_loaded, 16)
            nc.scalar.activation(csig, vecs[:, VEC["c"][0]:VEC["c"][1]], ACT.Sigmoid).then_inc(csig_ready, 1)
            norm_squares(3)
            act.wait_ge(mod_rows, 16)
            for q in range(4):
                nc.scalar.activation(modrow[32 * q:32 * q + 1, :, :], banks[32 * q:32 * q + 1, 0:3, :], ACT.Copy).then_inc(mod_copied, 1)
            ffn(FFN_CHUNKS)
            norm_squares(4)
            norm_squares(5)
            u = U_Z
            for t0, nt in ((0, 3 * P), (3, P)):
                for tb in range(TB):
                    evacuate(u, v2[:, tb, t0 * P:t0 * P + nt], nt)
                    u += 1
            for tb in range(TB):
                evacuate(u, iw[:, tb, :], IDX_HEADS)
                u += 1
            dsts = [q2[:, c, :] for c in range(AC)] + [k2[:, c, :] for c in range(AC)] + [iqT[:, c, :] for c in range(AC)] + [ikr]
            dsts += [zr[:, c, 1:] for c in range(ZR)]
            for d in dsts:
                evacuate(u, d)
                u += 1
            for d in (sig_a, sig_r):
                for c in range(KC):
                    evacuate(u, d[:, c, :], func=ACT.Sigmoid)
                    u += 1
            for n in range(4):
                nk = (n // 2 + 1) * P
                act.wait_ge(idx_ready, n + 1)
                act.wait_ge(bias2_loaded, 16 * P // SHIFTS)
                if n >= 2:
                    act.wait_ge(relu_used, n - 1)
                for r in range(4):
                    dst = relu_i[:, n % 2, 2 * r:2 * r + 2, 0:nk]
                    src = B[n % 2 * 4 + r].rearrange("p (a t) -> p a t", a=2)[:, :, 0:nk]
                    mm = nc.scalar.activation(dst, src, ACT.Relu)
                mm.then_inc(relu_ready, 1)
            attention(HEADS_2, HEADS_1, o2, ex2, pts2)
            act.wait_ge(shifted, ZR)
            nc.scalar.activation(lo_t[0:64, 0, :], lo_t[0:64, 0, :], ACT.Tanh).then_inc(lora_in, 1)
            nc.scalar.activation(lo_t[:, 1, :], lo_t[:, 1, :], ACT.Sigmoid).then_inc(lora_in, 1)
            act.wait_ge(lora_out, 1)
            for c in range(AC):
                nc.scalar.activation(b1[:, c, :], B[c // 2][:, c % 2 * T:c % 2 * T + T], ACT.Sigmoid, bias=vcol("decay_w0", c)).then_inc(act_step, 1)
            act.wait_ge(lora_out, 2)
            for c in range(AC):
                mm = nc.scalar.activation(b5[:, c, :], B[2 + c // 2][:, c % 2 * T:c % 2 * T + T], ACT.Sigmoid, bias=vcol("iclr_a0", c))
            mm.then_inc(iclr_ready, 1)
            act.wait_ge(lora_out, 3)
            nc.scalar.activation(b6, banks[:, 4:6, :].rearrange("p a (b t) -> p (a b) t", b=2), ACT.Copy)
            act.wait_ge(act_step, AC)
            nc.scalar.activation(b1, b1, ACT.Exp, scale=-math.exp(-0.5)).then_inc(decay_ready, 1)
            act.wait_ge(kk_sum, 1)
            nc.scalar.activation(f0, banks[:, 6:8, :].rearrange("p a (b t) -> p (a b) t", b=2), ACT.Sqrt).then_inc(kk_norm, 1)

            def pair_bank(b0):
                return banks[:, b0:b0 + 2, :].rearrange("p a (b t) -> p (a b) t", t=CH)

            for n, dst in enumerate((vt, bt, kt)):
                act.wait_ge(turned, n + 1)
                nc.scalar.activation(dst, pair_bank(2 * n), ACT.Copy).then_inc(turned_used, 1)
            for n in range(len(LEVELS)):
                act.wait_ge(level_x, n + 1)
                nc.scalar.activation(xm, pair_bank(0), ACT.Copy).then_inc(x_copied, 1)

            def quarter(b):
                return B[b][:, 0:T].rearrange("p (a t) -> p a t", a=AC)

            for c in range(NCH):
                act.wait_ge(rhs_ready, c + 1)
                nc.scalar.activation(rhs_u, quarter(0), ACT.Copy).then_inc(rhs_copied, 1)
                act.wait_ge(u_ready, c + 1)
                if c:
                    act.wait_ge(y_ready, c)
                nc.scalar.activation(u_sb, quarter(1), ACT.Copy).then_inc(u_copied, 1)
                act.wait_ge(y_ready, c + 1)
                nc.scalar.activation(b1[:, :, c * CH:(c + 1) * CH], quarter(3 + c % 2), ACT.Copy).then_inc(y_copied, 1)
            act.wait_ge(gn_var, 1)
            nc.scalar.activation(f1, banks[:, 0:2, :].rearrange("p a (b t) -> p (a b) t", b=2), ACT.Sqrt, scale=1.0 / HEAD, bias=gn_eps).then_inc(gn_rt, 1)
            norm_squares(6)
            act.wait_ge(logits_ready, 1)
            nc.scalar.activation(score_e, B[7][:, 0:TB * EXPERTS].rearrange("p (a e) -> p a e", a=TB), ACT.Sigmoid).then_inc(scores_ready, 1)
            done = 2 * FFN_CHUNKS
            for f in range(2):
                act.wait_ge(gu_ready, done + f + 1)
                nc.scalar.activation(sig_f[:, f, :], B[4 + f][:, 0:T], ACT.Sigmoid).then_inc(sig_ready, 1)
            done += 2
            act.wait_ge(gates_turned, 1)
            nc.scalar.activation(gates_t[0:EXPERTS, :], B[7][0:EXPERTS, T:2 * T], ACT.Copy).then_inc(gates_copied, 1)
            with act.Fori(0, EXPERTS // UNITS) as i:
                for s in range(2 * UNITS):
                    act.wait_ge(gu_ready, 2 * UNITS * i + (done + s + 1))
                    nc.scalar.activation(sig_f[:, s % 2, :], B[4 + s % 2][:, 0:T], ACT.Sigmoid).then_inc(sig_ready, 1)
            norm_squares(7)

        @block.vector
        def _(dve):
            steps = [0]

            def then(ins):
                steps[0] += 1
                ins.then_inc(dve_step, 1)
                dve.wait_ge(dve_step, steps[0])

            def norm_scale(k, weight, dst):
                dve.wait_ge(rt_ready, k + 1)
                then(nc.vector.reciprocal(rinv[:], rt[:]))
                for c in range(KC):
                    nc.vector.scalar_tensor_tensor(dst(c), x[:, c, :], weight(c), rinv[:], ALU.mult, ALU.mult).then_inc(h_ready, 1)

            def ffn(base, done, k):
                with dve.Fori(0, 2) as i:
                    for s in range(RING):
                        dve.wait_ge(sig_ready, RING * i + (done + s + 1))
                        gu = B[4 + s % 2]
                        nc.vector.tensor_tensor(gated[:, s % 2, :], gu[:, 0:T], sig_f[:, s % 2, :], ALU.mult).then_inc(dve_step, 1)
                        dve.wait_ge(dve_step, RING * i + (steps[0] + s + 1))
                        nc.vector.tensor_tensor(act_f[:, s % 2, :], gated[:, s % 2, :], gu[:, T:2 * T], ALU.mult).then_inc(act_ready, 1)
                steps[0] += FFN_CHUNKS
                dve.wait_ge(w_used, base + FFN_CHUNKS)
                for b in range(4):
                    xb = x[:, 2 * b:2 * b + 2, :]
                    nc.vector.tensor_tensor(xb, B[b].rearrange("p (a t) -> p a t", a=2), xb, ALU.add).then_inc(x_ready, 1)

            def attention(heads, n0, bias, extra, ex):
                for j in range(heads + 1):
                    if j < heads:
                        b, e, k = B[j % 2], ex[:, j % 2, :], 2 * (j % 2)
                        dve.wait_ge(s_ready, n0 + j + 1)
                        if j >= 2:
                            dve.wait_ge(pt_ready, n0 + j - 1)
                        nc.vector.scalar_tensor_tensor(e[:, 0:T], b[:, 0:T], HEAD ** -0.5, bias[:, j, :], ALU.mult, ALU.add)
                        m = nc.vector.scalar_tensor_tensor(e[:, T:T + P], b[:, T:T + P], HEAD ** -0.5, bias[:, j, P:T], ALU.mult, ALU.add)
                        m.then_inc(s_used, 1)
                        dve.wait_ge(s_used, n0 + j + 1)
                        if extra is not None:
                            then(nc.vector.tensor_tensor(e, e, extra, ALU.add))
                        nc.vector.tensor_reduce(nmax[:, k:k + 1], e[:, 0:T], AX_X, ALU.max, negate=True)
                        nc.vector.tensor_reduce(nmax[:, k + 1:k + 2], e[:, T:T + P], AX_X, ALU.max, negate=True).then_inc(max_ready, 1)
                    if j >= 1:
                        a = j - 1
                        e, k = ex[:, a % 2, :], 2 * (a % 2)
                        dve.wait_ge(exp_ready, n0 + a + 1)
                        then(nc.vector.reciprocal(rrec[:, k:k + 2], rsum[:, k:k + 2]))
                        nc.vector.tensor_scalar(e[:, 0:T], e[:, 0:T], rrec[:, k:k + 1], None, ALU.mult)
                        nc.vector.tensor_scalar(e[:, T:T + P], e[:, T:T + P], rrec[:, k + 1:k + 2], None, ALU.mult).then_inc(p_ready, 1)

            def residual(first):
                for b in range(4):
                    dve.wait_ge(res_ready, first + b + 1)
                    xb = x[:, 2 * b:2 * b + 2, :]
                    nc.vector.tensor_tensor(xb, B[b].rearrange("p (a t) -> p a t", a=2), xb, ALU.add).then_inc(x_ready, 1)

            nc.vector.memset(ones[:], 1.0)
            nc.vector.memset(zeros[:], 0.0)
            nc.vector.memset(eps, EPS)
            then(nc.vector.memset(gn_eps, GN_EPS))
            nc.vector.memset(hp[:, :, 0:PAD], 0.0).then_inc(ones_ready, 1)

            dve.wait_ge(vec_loaded, 16)
            norm_scale(0, lambda c: vcol("norm_mixer0", c), lambda c: hp[:, c, PAD:])
            dve.wait_ge(h_ready, KC)
            W = PAD + T
            then(nc.vector.tensor_tensor(pw_b[:, :, 1:W], hp[:, :, 1:W], hp[:, :, 0:W - 1], ALU.add))
            then(nc.vector.tensor_tensor(pw_c[:, 2:, 3:W], pw_b[:, 2:, 3:W], pw_b[:, 2:, 1:W - 2], ALU.add))
            then(nc.vector.tensor_tensor(pw_b[:, 4:, 7:W], pw_c[:, 4:, 7:W], pw_c[:, 4:, 3:W - 4], ALU.add))
            then(nc.vector.tensor_tensor(pw_c[:, 6:, 15:W], pw_b[:, 6:, 15:W], pw_b[:, 6:, 7:W - 8], ALU.add))
            dve.wait_ge(pool_loaded, 32)
            for g in range(4):
                win = (pw_b, pw_c)[g % 2][:, 2 * g:2 * g + 2, PAD:]
                hg = h[:, 2 * g:2 * g + 2, :]
                then(nc.vector.tensor_tensor(hg, win, icnt[:, g:g + 1, :].broadcast_to([P, 2, T]), ALU.mult))
                nc.vector.tensor_tensor(hg, hg, hp[:, 2 * g:2 * g + 2, PAD:], ALU.subtract).then_inc(pool_d, 1)
            for g in range(4):
                dve.wait_ge(pool_y, g + 1)
                for e in range(2):
                    c = 2 * g + e
                    last = nc.vector.scalar_tensor_tensor(x[:, c, :], B[g][:, e * T:(e + 1) * T], vcol("pool_scale", c), x[:, c, :], ALU.mult, ALU.add)
                last.then_inc(x_ready, 1)
            norm_scale(1, lambda c: vcol("norm_ffn0", c), lambda c: h[:, c, :])
            ffn(S_FFN1, 0, 1)
            norm_scale(2, lambda c: vcol("kv_norm", c), lambda c: h[:, c, :])
            for c in range(KC):
                nc.vector.scalar_tensor_tensor(hq[:, c, :], x[:, c, :], vcol("norm_mixer1", c), rinv[:], ALU.mult, ALU.mult).then_inc(h_ready, 1)
            dve.wait_ge(bias_loaded, 16 * P // SHIFTS)
            attention(HEADS_1, 0, bias1, None, ex)
            residual(0)
            dve.wait_ge(csig_ready, 1)
            nc.vector.tensor_tensor(csil, csig, vecs[:, VEC["c"][0]:VEC["c"][1]], ALU.mult).then_inc(csil_ready, 1)
            norm_scale(3, lambda c: vcol("norm_ffn1", c), lambda c: h[:, c, :])
            ffn(S_FFN2, FFN_CHUNKS, 3)
            dve.wait_ge(mod_turned, 1)
            then(nc.vector.tensor_tensor(mod[:], B[7][:, 0:48], vecs[:, VEC["ada_b"][0]:VEC["ada_b"][1]], ALU.add))
            for dst, col, g in ((scale1, 8, "norm1_g"), (scale2, 32, "norm2_g")):
                last = nc.vector.scalar_tensor_tensor(dst[:], mod[:, col:col + 8], 1.0, vecs[:, VEC[g][0]:VEC[g][1]], ALU.add, ALU.mult)
            then(last)
            dve.wait_ge(rt_ready, 5)
            then(nc.vector.reciprocal(rinv[:], rt[:]))
            for c in range(KC):
                last = nc.vector.scalar_tensor_tensor(x[:, c, :], x[:, c, :], vcol("final_norm", c), rinv[:], ALU.mult, ALU.mult)
                if c % 2:
                    last.then_inc(x_ready, 1)
            def norm_modulated(k, scale, shift):
                dve.wait_ge(rt_ready, k + 1)
                then(nc.vector.reciprocal(rinv[:], rt[:]))
                for c in range(KC):
                    last = nc.vector.scalar_tensor_tensor(h[:, c, :], x[:, c, :], scale[:, c:c + 1], rinv[:], ALU.mult, ALU.mult)
                then(last)
                for c in range(KC):
                    nc.vector.tensor_scalar(h[:, c, :], h[:, c, :], mod[:, shift + c:shift + c + 1], None, ALU.add).then_inc(h_ready, 1)

            norm_modulated(5, scale1, 0)
            dve.wait_ge(proj_used, U_Z + 6)
            then(nc.vector.tensor_scalar(iw, iw, IDX_HEADS ** -0.5 * IDX_DIM ** -0.5, None, ALU.mult))
            causal = cst("causal")
            parts = {1: slice(0, T), 0: slice(T, T + P)}
            dve.wait_ge(bias2_loaded, 16 * P // SHIFTS)
            for n in range(4):
                qb, cp = n // 2, n % 2
                nk = (qb + 1) * P
                dve.wait_ge(relu_ready, n + 1)
                for r in range(4):
                    for cc in range(2):
                        head = (2 * cp + cc) * 4 + r
                        acc, rl, w = work[:, parts[qb]], relu_i[:, n % 2, 2 * r + cc, 0:nk], iw[:, qb, head:head + 1]
                        prev = causal[:, parts[qb]] if cp == 0 and r == 0 and cc == 0 else acc
                        then(nc.vector.scalar_tensor_tensor(acc, rl, w, prev, ALU.mult, ALU.add))
                dve.sem_inc(relu_used, 1)
            for it in range(TOP_KEYS // 8):
                for qb in range(2):
                    last = nc.vector.max(top8[:, qb, :], work[:, parts[qb]])
                then(last)
                for qb in range(2):
                    last = nc.vector.match_replace(work[:, parts[qb]], top8[:, qb, :], work[:, parts[qb]], TAKEN)
                then(last)
            then(nc.vector.tensor_scalar(mask2, work, TAKEN / 2, MASKED, ALU.is_gt, ALU.mult))
            then(nc.vector.tensor_tensor(mask2, mask2, causal, ALU.add))
            attention(HEADS_2, HEADS_1, bias2, mask2, ex2)
            dve.wait_ge(o_copied, (HEADS_1 + HEADS_2) // 2)
            then(nc.vector.memset(zr[:, :, 0:1], 0.0))
            then(nc.vector.tensor_tensor(zs, zr[:, :, 0:T], zr[:, :, 1:], ALU.subtract))
            for c in (12, 13, *range(12)):
                nc.vector.scalar_tensor_tensor(zs[:, c, :], zs[:, c, :], vcol("tshift_mu", c), zr[:, c, 1:], ALU.mult, ALU.add).then_inc(shifted, 1)
            dve.wait_ge(shifted, ZR)

            def per_chunk(fn):
                for c in range(AC):
                    last = fn(c)
                then(last)

            per_chunk(lambda c: nc.vector.tensor_scalar(b4[:, c, :], k_t[:, c, :], vcol("k_k", c), None, ALU.mult))
            nc.vector.tensor_tensor(f0, b4, b4, ALU.mult).then_inc(kk_sq, 1)
            dve.wait_ge(iclr_ready, 1)
            per_chunk(lambda c: nc.vector.tensor_scalar(f1[:, c, :], b5[:, c, :], 1.0, vcol("k_a", c), ALU.subtract, ALU.mult))
            then(nc.vector.scalar_tensor_tensor(k_t, f1, 1.0, k_t, ALU.add, ALU.mult))
            then(nc.vector.tensor_tensor(f1, r_t, k_t, ALU.mult))
            for c in range(AC):
                last = nc.vector.tensor_scalar(f2[:, c, :], f1[:, c, :], vcol("r_k", c), None, ALU.mult)
            last.then_inc(bonus_in, 1)
            starts = lambda a: a.rearrange("p a (c t) -> p a c t", t=CH)
            dve.wait_ge(decay_ready, 1)
            then(nc.vector.memset(b3, 0.0))
            then(nc.vector.tensor_copy(starts(b3)[:, :, :, 0], starts(b1)[:, :, :, 0]))
            then(nc.vector.memset(starts(b1)[:, :, :, 0:1], 0.0))
            per_chunk(lambda c: nc.vector.tensor_tensor_scan(b2[:, c, :], b1[:, c, :], b3[:, c, :], 0.0, ALU.mult, ALU.add))
            nc.vector.tensor_copy(p_end, starts(b2)[:, :, :, CH - 1])
            then(nc.vector.tensor_copy(b3[:, :, 1:], b2[:, :, 0:T - 1]))
            then(nc.vector.memset(starts(b3)[:, :, :, 0:1], 1.0))
            dve.wait_ge(kk_norm, 1)
            then(nc.vector.tensor_scalar(f0, f0, 1e-12, None, ALU.max))
            then(nc.vector.reciprocal(f0, f0))
            then(nc.vector.tensor_tensor(b4, b4, f0, ALU.mult))
            then(nc.vector.reciprocal(b1, b2))
            then(nc.vector.tensor_tensor(b5, b4, b5, ALU.mult))
            then(nc.vector.scalar_tensor_tensor(b4, b4, -1.0, b3, ALU.mult, ALU.mult))
            nc.vector.tensor_tensor(b5, b5, b1, ALU.mult)
            nc.vector.tensor_tensor(b3, r_t, b2, ALU.mult)
            then(nc.vector.tensor_tensor(k_t, k_t, b1, ALU.mult))
            dve.sem_inc(tilde_ready, 1)
            dve.wait_ge(bonus_sum, 1)
            nc.vector.tensor_tensor(b2, banks[:, 0:2, :].rearrange("p a (b t) -> p (a b) t", b=2), v_t, ALU.mult).then_inc(bonus_used, 1)

            def pair_bank(b0):
                return banks[:, b0:b0 + 2, :].rearrange("p a (b t) -> p (a b) t", t=CH)

            def every(name, lo=0):
                a = CONST[name][0] + lo
                return con[:, a:a + CH].unsqueeze(1).broadcast_to([P, NCH * AC, CH])

            dve.wait_ge(pair_ready, 1)
            nc.vector.tensor_tensor(m_ab, pair_bank(6), every("strict_t"), ALU.mult).then_inc(pair_used, 1)
            dve.wait_ge(pair_used, 1)
            then(nc.vector.tensor_tensor(inv_t, m_ab, every("first_t"), ALU.mult))
            then(nc.vector.tensor_tensor(inv_t, inv_t, every("eye"), ALU.add))
            dve.wait_ge(pair_ready, 2)
            nc.vector.tensor_tensor(inv, pair_bank(0), every("first"), ALU.mult).then_inc(pair_used, 1)
            dve.wait_ge(pair_used, 2)
            then(nc.vector.tensor_tensor(inv, inv, every("eye"), ALU.add))
            for n, (dst, b0, m) in enumerate(((m_ak, 2, "strict_t"), (m_rb, 4, "upto_t"), (m_rk, 6, "upto_t"))):
                dve.wait_ge(pair_ready, n + 3)
                nc.vector.tensor_tensor(dst, pair_bank(b0), every(m), ALU.mult).then_inc(pair_used, 1)
            for n in range(len(LEVELS)):
                if n:
                    dve.wait_ge(level_x, n)
                nc.vector.tensor_tensor(m_lev, m_ab, every("levels_t", CH * n), ALU.mult).then_inc(level_m, 1)
                dve.wait_ge(level_d, n + 1)
                nc.vector.tensor_tensor(inv, inv, pair_bank(2), ALU.add)
                last = nc.vector.tensor_tensor(inv_t, inv_t, pair_bank(4), ALU.add)
                then(last)
            dve.sem_inc(inv_ready, 1)
            for c in range(NCH):
                dve.wait_ge(g_ready, c + 1)
                g_new, g_old = gst[:, c % 2], gst[:, (c - 1) % 2]
                add = B[2][:, 0:T].rearrange("p (a t) -> p a t", a=AC)
                pc = p_end[:, :, c:c + 1].broadcast_to([P, AC, CH])
                if c:
                    dve.wait_ge(y_ready, c)
                    then(nc.vector.tensor_tensor(g_new, add, g_old, ALU.add))
                    nc.vector.tensor_tensor(g_new, g_new, pc, ALU.mult).then_inc(state_ready, 1)
                else:
                    nc.vector.tensor_tensor(g_new, add, pc, ALU.mult).then_inc(state_ready, 1)
                dve.wait_ge(state_ready, c + 1)
            dve.wait_ge(gn_sum, 1)
            full = lambda b0: banks[:, b0:b0 + 2, :].rearrange("p a (b t) -> p (a b) t", b=2)
            then(nc.vector.scalar_tensor_tensor(b1, full(6), -1.0 / HEAD, b1, ALU.mult, ALU.add))
            nc.vector.tensor_tensor(f0, b1, b1, ALU.mult).then_inc(gn_sq, 1)
            dve.wait_ge(gn_rt, 1)
            then(nc.vector.reciprocal(f1, f1))
            then(nc.vector.tensor_tensor(b1, b1, f1, ALU.mult))
            per_chunk(lambda c: nc.vector.tensor_scalar(b1[:, c, :], b1[:, c, :], vcol("lnx_g", c), vcol("lnx_b", c), ALU.mult, ALU.add))
            then(nc.vector.tensor_tensor(b1, b1, b2, ALU.add))
            nc.vector.tensor_tensor(rw, b1, b6, ALU.mult).then_inc(rw_ready, 1)
            for b in range(4):
                dve.wait_ge(br_ready, b + 1)
                two = lambda a: a[:, 2 * b:2 * b + 2, :]
                pair = lambda k: B[k].rearrange("p (a t) -> p a t", a=2)
                nc.vector.tensor_tensor(two(mixed), pair(b), two(sig_a), ALU.mult)
            for b in range(4):
                dve.wait_ge(br_ready, b + 5)
                then(nc.vector.tensor_tensor(two(mixed_r), pair(4 + b), two(sig_r), ALU.mult))
                nc.vector.tensor_tensor(two(mixed), two(mixed), two(mixed_r), ALU.add).then_inc(mixed_ready, 1)

            def gated_residual(first, sem_of, gate):
                for b in range(4):
                    dve.wait_ge(sem_of, first + b + 1) if first is not None else None
                    for c in (2 * b, 2 * b + 1):
                        last = nc.vector.scalar_tensor_tensor(x[:, c, :], B[b][:, c % 2 * T:c % 2 * T + T], mod[:, gate + c:gate + c + 1], x[:, c, :], ALU.mult, ALU.add)
                    last.then_inc(x_ready, 1)

            gated_residual(4, res_ready, 16)
            norm_modulated(6, scale2, 24)
            dve.wait_ge(scores_ready, 1)
            dve.wait_ge(router_loaded, 32)
            then(nc.vector.tensor_tensor(choice, score_e, rbias.unsqueeze(1).broadcast_to([P, TB, EXPERTS]), ALU.add))
            nc.vector.memset(gtop, 3e38)
            for tb in range(TB):
                for g in range(GROUPS):
                    last = nc.vector.max(grp8[:, tb, g, :], choice[:, tb, g * 8:(g + 1) * 8])
            then(last)
            then(nc.vector.tensor_tensor(gsum, grp8[:, :, :, 0], grp8[:, :, :, 1], ALU.add))
            for tb in range(TB):
                last = nc.vector.max(gwork[:, tb, :], gsum[:, tb, :])
            then(last)
            then(nc.vector.tensor_copy(gtop[:, :, 0:TOP_GROUPS], gwork[:, :, 0:TOP_GROUPS]))
            for tb in range(TB):
                last = nc.vector.match_replace(gwork[:, tb, :], gtop[:, tb, :], gsum[:, tb, :], TAKEN)
            then(last)
            then(nc.vector.tensor_scalar(gwork, gwork, TAKEN / 2, MASKED, ALU.is_gt, ALU.mult))
            by_group = lambda a: a.rearrange("p a (g e) -> p a g e", g=GROUPS)
            then(nc.vector.tensor_tensor(by_group(choice), by_group(choice), gwork.unsqueeze(3).broadcast_to([P, TB, GROUPS, 8]), ALU.add))
            for tb in range(TB):
                last = nc.vector.max(gtop[:, tb, :], choice[:, tb, :])
            then(last)
            for tb in range(TB):
                last = nc.vector.match_replace(cwork[:, tb, :], gtop[:, tb, :], choice[:, tb, :], TAKEN)
            then(last)
            then(nc.vector.tensor_scalar(sel_e, cwork, TAKEN / 2, None, ALU.is_lt))
            then(nc.vector.tensor_tensor(sel_e, sel_e, score_e, ALU.mult))
            then(nc.vector.tensor_reduce(den, sel_e, AX_X, ALU.add))
            then(nc.vector.reciprocal(den, den))
            for tb in range(TB):
                last = nc.vector.tensor_scalar(sel_e[:, tb, :], sel_e[:, tb, :], den[:, tb:tb + 1], ROUTED_SCALE, ALU.mult, ALU.mult)
            last.then_inc(gates_ready, 1)
            done = 2 * FFN_CHUNKS
            for f in range(2):
                dve.wait_ge(sig_ready, done + f + 1)
                then(nc.vector.tensor_tensor(gated[:, f, :], B[4 + f][:, 0:T], sig_f[:, f, :], ALU.mult))
                nc.vector.tensor_tensor(act_f[:, f, :], gated[:, f, :], B[4 + f][:, T:2 * T], ALU.mult).then_inc(act_ready, 1)
            done += 2
            with dve.Fori(0, EXPERTS // UNITS) as i:
                for s in range(2 * UNITS):
                    gu = B[4 + s % 2]
                    dve.wait_ge(sig_ready, 2 * UNITS * i + (done + s + 1))
                    nc.vector.tensor_tensor(gated[:, s % 2, :], gu[:, 0:T], sig_f[:, s % 2, :], ALU.mult).then_inc(dve_step, 1)
                    dve.wait_ge(dve_step, 4 * UNITS * i + (steps[0] + 2 * s + 1))
                    nc.vector.tensor_tensor(weighted[:, s % 2, :], gated[:, s % 2, :], gu[:, T:2 * T], ALU.mult).then_inc(dve_step, 1)
                    if s % 2 == 0:
                        dve.wait_ge(wb_landed[s // 2], 16 * i + 16)
                    dve.wait_ge(dve_step, 4 * UNITS * i + (steps[0] + 2 * s + 2))
                    nc.vector.tensor_tensor(act_f[:, s % 2, :], weighted[:, s % 2, :], wb[:, s // 2, :], ALU.mult).then_inc(act_ready, 1)
            steps[0] += 4 * EXPERTS
            dve.wait_ge(unit_used, EXPERTS)
            gated_residual(None, None, 40)
            dve.wait_ge(rt_ready, 8)
            then(nc.vector.reciprocal(rinv[:], rt[:]))
            for c in range(KC):
                last = nc.vector.scalar_tensor_tensor(x[:, c, :], x[:, c, :], vcol("final_g", c), rinv[:], ALU.mult, ALU.mult)
            last.then_inc(out_ready, 1)


def tiles_of(w):
    k, n = w.shape
    return w.reshape(k // P, P, n // P, P).transpose(2, 1, 0, 3).reshape(n // P, P, k)


def slots_of(tiles):
    n = -(-len(tiles) // 3) * 3
    out = np.zeros((n, P, TILE), np.float32)
    for i, t in enumerate(tiles):
        out[i] = t
    return out.reshape(n // 3, 3, P, TILE).transpose(0, 2, 1, 3).reshape(n // 3, P, SLOT)


def ffN_SLOTS(gate_up, down):
    g = tiles_of(gate_up)
    d = down.reshape(FFN_CHUNKS, P, D)
    return np.concatenate([g[:FFN_CHUNKS], g[FFN_CHUNKS:], d], 2)


def half_tiles(w):
    t = tiles_of(w)
    return t.reshape(4, 2, P, 512).transpose(0, 2, 1, 3).reshape(4, P, TILE)


def columns(v):
    return np.asarray(v).reshape(-1, P).T


def layout(i):
    i = {k: np.asarray(v) for k, v in i.items()}
    vecs = {"norm_mixer0": i["norm_mixer"][0], "norm_mixer1": i["norm_mixer"][1], "norm_ffn0": i["norm_ffn"][0],
            "norm_ffn1": i["norm_ffn"][1], "pool_scale": i["pool_scale"][0], "kv_norm": i["kv_norm"], "final_norm": i["final_norm"],
            "norm1_g": i["norm1_g_2"][0], "norm2_g": i["norm2_g_2"][0], "final_g": i["final_g_2"], "c": i["c_2"][0], "ada_b": i["ada_b_2"][0],
            "tshift_mu": i["tshift_mu_2"][0], "decay_w0": i["decay_w0_2"][0], "iclr_a0": i["iclr_a0_2"][0], "k_k": i["k_k_2"][0], "k_a": i["k_a_2"][0],
            "r_k": i["r_k_2"][0].reshape(-1), "lnx_g": i["lnx_g_2"][0], "lnx_b": i["lnx_b_2"][0]}
    w_kv, w_in = i["w_kv"], i["w_in_2"][0]
    kvqo = [*tiles_of(w_kv[:, D:]), *tiles_of(w_kv[:, :D]), *tiles_of(i["w_q"][0]), *tiles_of(i["w_o"][0])]
    ada = i["ada_w_2"][0].reshape(KC, P, 2, SLOT).transpose(0, 2, 1, 3).reshape(16, P, SLOT)
    a = ATTN_W
    o = 3 * a
    iq, ik, iw = w_in[:, o:o + 512], w_in[:, o + 512:o + 544], w_in[:, o + 544:o + 560]
    zr, ga, gr = w_in[:, o + 560:o + 560 + ZR * P], w_in[:, o + 560 + ZR * P:o + 560 + ZR * P + D], w_in[:, o + 560 + ZR * P + D:]
    iw_tile = np.concatenate([iw, np.zeros((D, P - IDX_HEADS), np.float32)], 1)
    win = np.concatenate([w_in[:, 2 * a:3 * a], iw_tile, w_in[:, 0:2 * a], iq, ik, ik, ik, ik, zr, ga, gr], 1)
    br = [*half_tiles(i["w_attn_br_2"][0]), *half_tiles(i["w_rwkv_br_2"][0]), *tiles_of(i["w_out_2"][0])]
    ws = np.concatenate([ffN_SLOTS(i["w_gate_up"][0], i["w_down"][0]), slots_of(kvqo), ada, ffN_SLOTS(i["w_gate_up"][1], i["w_down"][1]),
                         slots_of(tiles_of(win)), slots_of(br)], 0)
    rel = np.concatenate([np.concatenate([i["rel_bias"], i["rel_bias_2"]], 1), np.ones((1, HEADS_1 + HEADS_2), np.float32)], 0)
    lora = np.concatenate([np.concatenate([i["decay_up_2"][0], i["iclr_up_2"][0]], 0), i["gate_up_2"][0]], 1)
    gate = np.concatenate([i["sh_gate_2"], i["exp_gate_2"][0]], 0)
    up = np.concatenate([i["sh_up_2"], i["exp_up_2"][0]], 0)
    dn = np.concatenate([i["sh_down_2"], i["exp_down_2"][0]], 0)
    n = EXPERTS + 1
    gu = np.concatenate([gate.reshape(n, KC, P, EXPERT_FF), up.reshape(n, KC, P, EXPERT_FF)], 3).transpose(0, 2, 1, 3).reshape(n, P, KC * 2 * EXPERT_FF)
    experts = np.concatenate([gu, dn.reshape(n, 2, P, D).transpose(0, 2, 1, 3).reshape(n, P, 2 * D)], 2)
    return {
        "xT": i["x"][0].T.reshape(KC, P, T).transpose(1, 0, 2),
        "vec": np.concatenate([columns(vecs[name]) for name, _ in VEC_PARTS], 1),
        "consts": constants(),
        "selector": bias_selector(),
        "inv_count": pool_inverse_counts(),
        "pool_w": i["pool_w"][0].reshape(4, 2, P, 256).transpose(2, 0, 1, 3),
        "ws": ws,
        "rel": rel,
        "lora": lora,
        "router": i["router_w_2"][0].reshape(KC, P, EXPERTS).transpose(1, 0, 2),
        "router_bias": i["router_bias_2"],
        "experts": experts,
    }


def kernel(**inputs):
    import concourse.bacc as bacc
    from concourse.bass_utils import run_bass_kernel_spmd

    nc = bacc.Bacc("TRN2", target_bir_lowering=False, num_devices=1)
    arrays = {name: np.ascontiguousarray(a) for name, a in layout(inputs).items()}
    aps = {name: nc.dram_tensor(name, a.shape, F32, kind="ExternalInput").ap() for name, a in arrays.items()}
    aps["out"] = nc.dram_tensor("out", (P, KC, T), F32, kind="ExternalOutput").ap()
    build(nc, **aps)
    result = run_bass_kernel_spmd(nc, [arrays], core_ids=[0]).results[0]["out"]
    return np.ascontiguousarray(result.transpose(1, 0, 2).reshape(D, T).T)[None]
```

```python
import math
from contextlib import ExitStack

import numpy as np
import concourse.bass as bass
from concourse import mybir

F32 = mybir.dt.float32
BF16 = mybir.dt.bfloat16
F32R = mybir.dt.float32r
I32 = mybir.dt.int32
ALU = mybir.AluOpType
ACT = mybir.ActivationFunctionType
AX_X = mybir.AxisListType.X

P = 128
T = 256
TB = T // P
D = 1024
KC = D // P
D_FF = 2816
FFN_CHUNKS = D_FF // P
HEADS_1, HEADS_2, HEAD = 16, 8, 64
ATTN_W = HEADS_2 * HEAD
AC = ATTN_W // P
IDX_HEADS, IDX_DIM, TOP_KEYS = 16, 32, 64
BUCKETS, MAX_DISTANCE = 32, 128
WINDOWS = (2, 4, 8, 16)
PAD = 16
CH = 64
NCH = T // CH
ZR = 14
EXPERTS, GROUPS, TOP_GROUPS, MOE_TOPK, EXPERT_FF = 64, 8, 4, 8, 256
ROUTED_SCALE = 2.5
EPS, GN_EPS = 1e-6, 64e-5
SHIFTS = 32
MASKED = -1e30
TAKEN = -3e38

TILE = KC * P
SLOT = 3 * TILE
RING = 11
S_FFN1 = 0
S_KVQ = S_FFN1 + FFN_CHUNKS
S_ADA = S_KVQ + 8
S_O = S_ADA + 16
S_FFN2 = S_O + 3
S_WIN = S_FFN2 + FFN_CHUNKS
S_BR = S_WIN + 16
N_SLOTS = S_BR + 6
S_TURNS = S_WIN + RING
PLACE = [n % RING for n in range(S_TURNS)] + [10, 0, 1, 2, 3] + [4, 10, 0, 1, 2, 3]
LOADS = [PLACE[:n + 1].count(PLACE[n]) for n in range(N_SLOTS)]
TENANT = [max((m for m in range(n) if PLACE[m] == PLACE[n]), default=None) for n in range(N_SLOTS)]
ZR_ORDER = (12, 13, *range(12))
UNIT = KC * 2 * EXPERT_FF + 2 * D
GATE_UP = KC * 2 * EXPERT_FF
UNITS = 4
CAP = 64
PAIRS = EXPERTS // 2
QUADS = EXPERTS // 4
NOT_CHOSEN = 1024

VEC_PARTS = [("norm_mixer0", 8), ("norm_mixer1", 8), ("norm_ffn0", 8), ("norm_ffn1", 8), ("pool_scale", 8),
             ("kv_norm", 8), ("final_norm", 8), ("norm1_g", 8), ("norm2_g", 8), ("final_g", 8), ("c", 8),
             ("ada_b", 48), ("tshift_mu", 14), ("decay_w0", 4), ("iclr_a0", 4), ("k_k", 4), ("k_a", 4),
             ("r_k", 4), ("lnx_g", 4), ("lnx_b", 4)]
VEC = {}
_n = 0
for _name, _w in VEC_PARTS:
    VEC[_name] = (_n, _n + _w)
    _n += _w
N_VEC = _n

LEVELS = [2, 4, 8, 16, 32]
CONST_PARTS = [("ident", 128), ("headones", 128), ("strict_t", 64), ("upto_t", 64), ("first", 64), ("first_t", 64),
               ("levels_t", 64 * len(LEVELS)), ("eye", 64), ("causal", 384),
               ("before", 128), ("slots", CAP), ("slot_of", 1)]
CONST = {}
_n = 0
for _name, _w in CONST_PARTS:
    CONST[_name] = (_n, _n + _w)
    _n += _w
N_CONST = _n


def constants():
    c = np.zeros((P, N_CONST), np.float32)

    def put(name, a):
        c[:, CONST[name][0]:CONST[name][1]] = a

    put("ident", np.eye(P))
    put("headones", np.kron(np.eye(2), np.ones((HEAD, HEAD))))
    s, t = np.meshgrid(np.arange(CH), np.arange(CH), indexing="ij")
    two = lambda m: np.concatenate([m, m], 0)
    put("strict_t", two(s < t))
    put("upto_t", two(s <= t))
    put("first", two((s // 2 == t // 2) & (s > t)))
    put("first_t", two((s // 2 == t // 2) & (s < t)))
    put("levels_t", np.concatenate([two((s // (2 * b) == t // (2 * b)) & (s // b % 2 == 0) & (t // b % 2 == 1)) for b in LEVELS], 1))
    put("eye", two(s == t))
    q = np.arange(P)[:, None]
    k = np.arange(T)[None, :]
    put("causal", np.concatenate([np.where(k <= q + P, 0.0, MASKED), np.where(k[:, :P] <= q, 0.0, MASKED)], 1))
    put("before", np.arange(P)[:, None] < np.arange(P)[None, :])
    put("slots", np.broadcast_to(np.arange(CAP) - NOT_CHOSEN, (P, CAP)))
    put("slot_of", (np.arange(P) % CAP - NOT_CHOSEN)[:, None])
    return c


def bias_selector():
    dist = 255 - np.arange(2 * T)
    n = np.maximum(dist, 0)
    half = BUCKETS // 2
    far = half + (np.log(np.maximum(n, half).astype(np.float32) / np.float32(half)) / np.float32(math.log(MAX_DISTANCE / half)) * half).astype(np.int32)
    bucket = np.where(n < half, n, np.minimum(far, BUCKETS - 1))
    m = np.zeros((BUCKETS + 1, 2 * T), np.float32)
    m[bucket, np.arange(2 * T)] = dist >= 0
    m[BUCKETS] = np.where(dist >= 0, 0.0, MASKED)
    return m


def pool_inverse_counts():
    t = np.arange(T)
    rows = [1.0 / np.minimum(t + 1, w).astype(np.float32) for w in WINDOWS]
    return np.broadcast_to(np.stack(rows).astype(np.float32)[None], (P, 4, T)).copy()


def build(nc, xT, vec, consts, selector, inv_count, pool_w, ws, rel, lora, router, router_bias, experts, out):
    bias_line = nc.dram_tensor("bias_line", (HEADS_1 + HEADS_2, SHIFTS, 2 * T), F32, kind="Internal").ap()
    mod_line = nc.dram_tensor("mod_line", (6 * D,), F32, kind="Internal").ap()
    route_rows = nc.dram_tensor("route_rows", (EXPERTS, 2 * T), F32, kind="Internal").ap()
    dense_rows = nc.dram_tensor("dense_rows", (EXPERTS, T), F32, kind="Internal").ap()

    with ExitStack() as ctx:
        def sb(name, shape, dt=F32):
            return ctx.enter_context(nc.sbuf_tensor(name, shape, dt))

        def sem(name):
            return ctx.enter_context(nc.semaphore(name))

        ring_at = -(-nc.sbuf_base // 32) * 32
        ring = sb("ring", [P, RING * SLOT])
        scr_at = -(-nc.sbuf_base // 32) * 32
        scr = sb("scr", [P, 14600])
        x = sb("x", [P, KC, T])
        vecs = sb("vecs", [P, N_VEC])
        con = sb("con", [P, N_CONST])
        ones = sb("ones", [P, P])
        zeros = sb("zeros", [P, 512], BF16)
        rt = sb("rt", [P, T])
        rinv = sb("rinv", [P, T])
        small = sb("small", [P, 64])
        mod = sb("mod", [P, 48])
        scale1 = sb("scale1", [P, KC])
        scale2 = sb("scale2", [P, KC])
        relw = sb("relw", [BUCKETS + 1, HEADS_1 + HEADS_2])
        banks = ctx.enter_context(nc.psum_tensor("banks", [P, 8, 512], F32))
        B = [banks[:, i, :] for i in range(8)]

        def view(lo, *dims, base=scr):
            n = int(np.prod(dims))
            v = base[:, lo:lo + n]
            if len(dims) == 2:
                return v.rearrange("p (a b) -> p a b", a=dims[0])
            if len(dims) == 3:
                return v.rearrange("p (a b c) -> p a b c", a=dims[0], b=dims[1])
            return v

        def rounded(name, at, cols):
            return nc.alloc_sbuf_tensor_at(name, [P, cols], F32R, offset=at)[:]

        def slot(n):
            return ring[:, PLACE[n] * SLOT:(PLACE[n] + 1) * SLOT]

        def vcol(name, c):
            return vecs[:, VEC[name][0] + c:VEC[name][0] + c + 1]

        def cst(name):
            return con[:, CONST[name][0]:CONST[name][1]]

        ident = cst("ident")
        headones = cst("headones")
        eps, gn_eps = small[:, 0:1], small[:, 1:2]

        h = view(0, KC, T)
        sq = view(2048, KC, T)
        hp, pw_b, pw_c = view(4352, KC, PAD + T), view(6528, KC, PAD + T), view(8704, KC, PAD + T)
        icnt, poolw = view(10880, 4, T), view(11904, 4, 2, T)
        sig_f, gated, act_f = view(4352, 2, T), view(4864, 2, T), view(5376, 2, T)
        hq = sq
        ex, pts = view(2048, 2, 384), view(2816, 2, 384)
        nmax, rsum, rrec = small[:, 8:12], small[:, 12:16], small[:, 16:20]
        q1, k1, v1, bias1 = view(4352, KC, T), view(6400, KC, T), view(8448, TB, D), view(10496, HEADS_1, T)
        csil, csig = small[:, 20:28], small[:, 28:36]
        modrow, mod48 = view(8448, 3, 512), view(10496, P)
        line_sb, sel_sb = view(13952, 2 * T), view(0, 2 * T)
        q2, k2, v2, iqT = view(2048, AC, T), view(3072, AC, T), view(4096, TB, ATTN_W), view(5120, AC, T)
        ikr, iw = view(6144, T), view(6400, TB, IDX_HEADS)
        zr = view(6432, ZR, T + 1)
        sig_a, sig_r = view(10030, KC, T), view(12078, KC, T)
        o2, rw = view(0, AC, T), view(1024, AC, T)

        def spare(lo, *dims):
            return view(5 * SLOT + lo, *dims, base=ring)

        bias2, relu_i, mask2 = spare(9728, HEADS_2, T), spare(11776, 8, T), spare(13824, 384)
        work, top8 = view(14126, 384), view(14510, 2, 8)
        ex2, pts2 = spare(11776, 2, 384), spare(12544, 2, 384)
        zs = spare(0, ZR, T)
        r_t, k_t, v_t, lo_t = zs[:, 0:4, :], zs[:, 4:8, :], zs[:, 8:12, :], zs[:, 12:14, :]
        b1, b2, b3, b4, b5, b6 = (spare(3584 + 1024 * i, AC, T) for i in range(6))
        vt, bt, kt = (spare(9728 + 1024 * i, NCH * AC, CH) for i in range(3))
        m_ab, m_lev = spare(12800, NCH * AC, CH), spare(13824, NCH * AC, CH)
        loraw = spare(14208, 2 * ATTN_W)
        m_ak, m_rb, m_rk, inv = (view(2048 + 1024 * i, NCH * AC, CH) for i in range(4))
        f0, f1 = (view(2048 + 1024 * i, AC, T) for i in range(2))
        inv_t, xm = view(6432, NCH * AC, CH), view(7456, NCH * AC, CH)
        gst, rhs_u, u_sb = view(8480, 2, AC, CH), view(8992, AC, CH), view(9248, AC, CH)
        p_end = small[:, 40:56].rearrange("p (a b) -> p a b", a=AC)
        mixed, mixed_r = view(6432, KC, T), view(4096, KC, T)
        score_e, choice, grp8, gsum, gtop, gwork, cwork, sel_e, den = (
            view(6432, TB, EXPERTS), view(6560, TB, EXPERTS), view(6688, TB, GROUPS, 8), view(6816, TB, GROUPS), view(6832, TB, 8),
            view(6848, TB, GROUPS), view(6864, TB, EXPERTS), view(6992, TB, EXPERTS), view(7120, TB))
        mask_e, rank_e, dense_e = view(7122, TB, EXPERTS), view(7250, TB, EXPERTS), view(7378, TB, EXPERTS)
        routerw, rbias = view(10030, KC, EXPERTS), view(10542, EXPERTS)
        beyond, flag = small[:, 58:59], small[:, 59:60].bitcast(I32)

        def unit(u):
            lo = (7, 9, 0, 2)[u] * SLOT
            return ring[:, lo:lo + UNIT]

        SHARED_UNIT = ring[:, 5 * SLOT:7 * SLOT]
        tok_hi = rounded("tok_hi", scr_at + 4 * 2048, TB * D).rearrange("p (a b) -> p a b", a=TB)
        tok_lo = rounded("tok_lo", ring_at + 4 * 4 * SLOT, TB * D).rearrange("p (a b) -> p a b", a=TB)
        rows_t, dense_t = view(4 * SLOT + 2048, 2 * T, base=ring), view(4 * SLOT + 2048 + 2 * T, T, base=ring)
        gathered_h = [view(7506 + 2048 * q, KC, 4 * CAP) for q in range(2)]
        pick = [rounded(f"pick{q}", scr_at + 4 * (11608 + 512 * q), TB * 4 * CAP).rearrange("p (a b) -> p a b", a=TB) for q in range(2)]
        rows_b = [view(12632 + 512 * q, 2 * T) for q in range(2)]
        spread = [rounded(f"spread{q}", scr_at + 4 * (13656 + T * q), T) for q in range(2)]
        slot_gate = [small[:, 56 + q:57 + q] for q in range(2)]
        sig_p, gated_p, act_p, act_pt = view(4352, T), view(4608, T), view(4864, T), view(5120, 2, P)
        out_hi = rounded("out_hi", ring_at + 4 * 5 * SLOT, D)
        out_lo = rounded("out_lo", ring_at + 4 * (5 * SLOT + D), D)
        gate_tmp = view(5 * SLOT + 2 * D, T, base=ring)
        wb = view(12632, UNITS, T)
        weighted = view(9216, 2, T)

        landed = [sem(f"weights_landed{i}") for i in range(RING)]
        w_used = sem("weights_used")
        x_loaded, vec_loaded, const_loaded, sel_loaded, pool_loaded = (sem(s) for s in ("x_loaded", "vec_loaded", "const_loaded", "sel_loaded", "pool_loaded"))
        sq_ready, ss_ready, rt_ready, h_ready, x_ready = (sem(s) for s in ("sq_ready", "ss_ready", "rt_ready", "h_ready", "x_ready"))
        ones_ready, line_ready, line_copied, line_stored, bias_loaded = (sem(s) for s in ("ones_ready", "line_ready", "line_copied", "line_stored", "bias_loaded"))
        pool_d, pool_y = sem("pool_d"), sem("pool_y")
        gu_ready, sig_ready, act_ready = sem("gu_ready"), sem("sig_ready"), sem("act_ready")
        proj_ready, proj_used, res_ready = sem("proj_ready"), sem("proj_used"), sem("res_ready")
        s_ready, s_used, max_ready, exp_ready, p_ready, pt_ready, pts_ready, o_ready, o_copied = (
            sem(s) for s in ("s_ready", "s_used", "max_ready", "exp_ready", "p_ready", "pt_ready", "pts_ready", "o_ready", "o_copied"))
        csig_ready, csil_ready, mod_copied, mod_stored, mod_back, mod_turned, mod_ready = (
            sem(s) for s in ("csig_ready", "csil_ready", "mod_copied", "mod_stored", "mod_back", "mod_turned", "mod_ready"))
        out_ready, out_done = sem("out_ready"), sem("out_done")
        bias2_loaded, lora_loaded, router_loaded = sem("bias2_loaded"), sem("lora_loaded"), sem("router_loaded")
        idx_ready, relu_ready, relu_used = sem("idx_ready"), sem("relu_ready"), sem("relu_used")
        shifted, lora_in, lora_out, decay_ready, iclr_ready, gate_ready = (
            sem(n) for n in ("shifted", "lora_in", "lora_out", "decay_ready", "iclr_ready", "gate_ready"))
        kk_sq, kk_sum, kk_norm, bonus_in, bonus_sum, bonus_used = (sem(n) for n in ("kk_sq", "kk_sum", "kk_norm", "bonus_in", "bonus_sum", "bonus_used"))
        v_ready, tilde_ready, turned, turned_used = (sem(n) for n in ("v_ready", "tilde_ready", "turned", "turned_used"))
        pair_ready, pair_used, level_m, level_x, x_copied, level_d, inv_ready = (
            sem(n) for n in ("pair_ready", "pair_used", "level_m", "level_x", "x_copied", "level_d", "inv_ready"))
        rhs_ready, rhs_copied, u_ready, u_copied, g_ready, state_ready, y_ready, y_copied = (
            sem(n) for n in ("rhs_ready", "rhs_copied", "u_ready", "u_copied", "g_ready", "state_ready", "y_ready", "y_copied"))
        gn_sum, gn_sq, gn_var, gn_rt, rw_ready = (sem(n) for n in ("gn_sum", "gn_sq", "gn_var", "gn_rt", "rw_ready"))
        br_ready, mixed_ready = sem("br_ready"), sem("mixed_ready")
        logits_ready, scores_ready, gates_ready, gates_turned, gates_copied, gates_stored = (
            sem(n) for n in ("logits_ready", "scores_ready", "gates_ready", "gates_turned", "gates_copied", "gates_stored"))
        shared_landed, tok_turned, tok_hi_ready, tok_lo_ready = (sem(n) for n in ("shared_landed", "tok_turned", "tok_hi_ready", "tok_lo_ready"))
        mask_ready, rank_ready, beyond_ready, beyond_sum, flag_ready = (sem(n) for n in ("mask_ready", "rank_ready", "beyond_ready", "beyond_sum", "flag_ready"))
        gu_landed, down_landed = [sem(f"gu_landed{u}") for u in range(UNITS)], [sem(f"down_landed{u}") for u in range(UNITS)]
        rows_landed, rows_used = [sem(f"rows_landed{u}") for u in range(2)], sem("rows_used")
        pick_ready, gather_ready, gather_copied = sem("pick_ready"), sem("gather_ready"), sem("gather_copied")
        pair_gu, pair_sig, pair_act, pair_turned, pair_act_t, pair_down, pair_hi, pair_lo, pair_spread = (
            sem(n) for n in ("pair_gu", "pair_sig", "pair_act", "pair_turned", "pair_act_t", "pair_down", "pair_hi", "pair_lo", "pair_spread"))
        unit_landed, wb_landed = [sem(f"unit_landed{u}") for u in range(UNITS)], [sem(f"wb_landed{u}") for u in range(UNITS)]
        unit_used, dense_gu, dense_sig, dense_step, dense_act = (sem(n) for n in ("unit_used", "dense_gu", "dense_sig", "dense_step", "dense_act"))
        dve_step, act_step = sem("dve_step"), sem("act_step")
        block = ctx.enter_context(nc.Block())

        H_BASE = [0, 8, 16, 32, 40, 40, 48, 56]

        PROJ_BANKS = [B[4], B[5], B[7]]
        U_V1, U_K1, U_Q1 = 0, 6, 14
        U_Z = 22
        IDX_AT, LO_AT, LORA_AT, DECAY_AT, KK_AT, KK_SQRT_AT, BONUS_AT = (18, 21, 24, 27), 30, 31, 33, 41, 42, 45
        VGROUPS1 = [(0, 3), (3, 3), (6, 2)]

        @block.sync
        def _(sp):
            sp.dma_start(x[:], xT).then_inc(x_loaded, 16)
            sp.dma_start(vecs[:], vec).then_inc(vec_loaded, 16)
            sp.dma_start(con[:], consts).then_inc(const_loaded, 16)
            sp.dma_start(poolw, pool_w).then_inc(pool_loaded, 16)
            sp.dma_start(icnt, inv_count).then_inc(pool_loaded, 16)
            sp.dma_start(sel_sb[0:BUCKETS + 1, :], selector).then_inc(sel_loaded, 16)
            sp.dma_start(relw[:], rel).then_inc(sel_loaded, 16)

            def load(n):
                sp.dma_start(slot(n), ws[n]).then_inc(landed[PLACE[n]], 16)

            for n in range(RING):
                load(n)
            with sp.Fori(1, S_TURNS // RING) as i:
                for s in range(RING):
                    sp.wait_ge(w_used, RING * i + (s + 1 - RING))
                    sp.dma_start(slot(s), ws[RING * i + s]).then_inc(landed[s], 16)
            for n in range(S_TURNS // RING * RING, N_SLOTS):
                sp.wait_ge(w_used, TENANT[n] + 1)
                load(n)
            sp.wait_ge(rw_ready, 1)
            sp.dma_start(SHARED_UNIT, experts[0]).then_inc(shared_landed, 16)

            def load_gate_up(u, e):
                sp.dma_start(unit(u)[:, 0:GATE_UP], experts[e, :, 0:GATE_UP]).then_inc(gu_landed[u], 16)

            def load_down(u, e):
                sp.dma_start(unit(u)[:, GATE_UP:], experts[e, :, GATE_UP:]).then_inc(down_landed[u], 16)

            for u in range(UNITS):
                if u == 1:
                    sp.wait_ge(x_ready, 24)
                load_gate_up(u, 1 + u)
                load_down(u, 1 + u)
            with sp.Fori(1, QUADS) as i:
                for k in range(2):
                    sp.wait_ge(pair_gu, 2 * i + (k - 1))
                    for u in (2 * k, 2 * k + 1):
                        load_gate_up(u, 4 * i + (1 + u))
                    sp.wait_ge(pair_down, 4 * i + 2 * (k - 1))
                    for u in (2 * k, 2 * k + 1):
                        load_down(u, 4 * i + (1 + u))
            sp.wait_ge(flag_ready, 1)
            overflow = sp.value_load(flag[0:1, :])
            with sp.If(overflow > 0):
                sp.wait_ge(pair_spread, PAIRS)
                for u in range(UNITS):
                    sp.dma_start(unit(u), experts[1 + u]).then_inc(unit_landed[u], 16)
                with sp.Fori(1, EXPERTS // UNITS) as i:
                    for u in range(UNITS):
                        sp.wait_ge(unit_used, UNITS * i + (u + 1 - UNITS))
                        sp.dma_start(unit(u), experts[UNITS * i + (1 + u)]).then_inc(unit_landed[u], 16)
            sp.wait_ge(out_ready, 1)
            sp.dma_start(out, x[:]).then_inc(out_done, 16)
            sp.wait_ge(out_done, 16)

        @block.gpsimd
        def _(pool):
            def load_toeplitz(dst, first, heads, signal):
                for a in range(P // SHIFTS):
                    start = first * SHIFTS * 2 * T + P - 1 - SHIFTS * a
                    src = bass.AP(bias_line.tensor, start, [[2 * T - 1, SHIFTS], [SHIFTS * 2 * T, heads], [1, T]])
                    pool.dma_start(dst[SHIFTS * a:SHIFTS * (a + 1)], src).then_inc(signal, 16)

            pool.wait_ge(line_copied, 1)
            pool.dma_start(bias_line, line_sb[0:HEADS_1 + HEADS_2, :].unsqueeze(1).broadcast_to([HEADS_1 + HEADS_2, SHIFTS, 2 * T])).then_inc(line_stored, 16)
            pool.wait_ge(line_stored, 16)
            pool.wait_ge(x_ready, 4)
            load_toeplitz(bias1, 0, HEADS_1, bias_loaded)
            pool.wait_ge(mod_copied, 4)
            by_row = mod_line.rearrange("(b q n) -> q b n", b=3, q=4)
            for q in range(4):
                pool.dma_start(by_row[q:q + 1], modrow[32 * q:32 * q + 1, :, :]).then_inc(mod_stored, 16)
            pool.wait_ge(mod_stored, 64)
            pool.dma_start(mod48[0:48, :], mod_line.rearrange("(r p) -> r p", p=P)).then_inc(mod_back, 16)
            pool.wait_ge(w_used, S_WIN + 5)
            load_toeplitz(bias2, HEADS_1, HEADS_2, bias2_loaded)
            pool.dma_start(loraw, lora).then_inc(lora_loaded, 16)
            pool.wait_ge(x_ready, 24)
            pool.dma_start(routerw, router).then_inc(router_loaded, 16)
            pool.dma_start(rbias, router_bias.partition_broadcast(P)).then_inc(router_loaded, 16)
            pool.wait_ge(gates_copied, 2)
            pool.dma_start(route_rows, rows_t[0:EXPERTS, :]).then_inc(gates_stored, 16)
            pool.dma_start(dense_rows, dense_t[0:EXPERTS, :]).then_inc(gates_stored, 16)
            pool.wait_ge(gates_stored, 32)

            def load_rows(k, e):
                for j in range(2):
                    row = route_rows[e + j:e + j + 1, :] if isinstance(e, int) else route_rows[bass.ds(e + j, 1), :]
                    pool.dma_start(rows_b[k][CAP * j:CAP * (j + 1), :], row.partition_broadcast(CAP)).then_inc(rows_landed[k], 16)

            for k in range(2):
                load_rows(k, 2 * k)
            with pool.Fori(1, QUADS) as i:
                for k in range(2):
                    pool.wait_ge(rows_used, 2 * i + (k - 1))
                    load_rows(k, 4 * i + 2 * k)
            pool.wait_ge(flag_ready, 1)
            overflow = pool.value_load(flag[0:1, :])
            with pool.If(overflow > 0):
                pool.wait_ge(rows_used, PAIRS)
                for u in range(UNITS):
                    pool.dma_start(wb[:, u, :], dense_rows[u:u + 1, :].partition_broadcast(P)).then_inc(wb_landed[u], 16)
                with pool.Fori(1, EXPERTS // UNITS) as i:
                    for u in range(UNITS):
                        pool.wait_ge(unit_used, UNITS * i + (u + 1 - UNITS))
                        pool.dma_start(wb[:, u, :], dense_rows[bass.ds(UNITS * i + u, 1), :].partition_broadcast(P)).then_inc(wb_landed[u], 16)

        @block.tensor
        def _(pe):
            def wait_slot(n):
                pe.wait_ge(landed[PLACE[n]], 16 * LOADS[n])

            def norm_sum(k):
                for g in range(4):
                    pe.wait_ge(sq_ready, 4 * k + g + 1)
                    for c in (2 * g, 2 * g + 1):
                        mm = nc.tensor.matmul(B[6][:, 0:T], ones[:], sq[:, c, :], start=(c == 0), stop=(c == KC - 1))
                mm.then_inc(ss_ready, 1)

            def clear_y():
                for b in range(4):
                    nc.tensor.matmul(B[b], zeros[:, 0:P], zeros[:], start=True, stop=False, skip_group_check=True)

            def gate_up(bank, gate, up, signal=gu_ready):
                for half, w in ((0, gate), (T, up)):
                    for c in range(KC):
                        mm = nc.tensor.matmul(bank[:, half:half + T], w(c), h[:, c, :], start=(c == 0), stop=(c == KC - 1))
                mm.then_inc(signal, 1)

            def down(w, a):
                for c in range(KC):
                    mm = nc.tensor.matmul(B[c // 2][:, c % 2 * T:c % 2 * T + T], w(c), a, start=False, stop=False, skip_group_check=True)
                return mm

            def ffn(base, k, done):
                clear_y()
                pe.wait_ge(h_ready, H_BASE[k] + KC)
                with pe.Fori(0, 2) as i:
                    for s in range(RING + 1):
                        if s < RING:
                            w = slot(base + s)
                            pe.wait_ge(landed[(base + s) % RING], 16 * ((base + s) // RING + 1) + 16 * i)
                            gate_up(B[4 + s % 2], lambda c: w[:, c * P:(c + 1) * P], lambda c: w[:, TILE + c * P:TILE + (c + 1) * P])
                        if s >= 1:
                            w2 = slot(base + s - 1)
                            pe.wait_ge(act_ready, RING * i + (done + s))
                            down(lambda c: w2[:, 2 * TILE + c * P:2 * TILE + (c + 1) * P], act_f[:, (s - 1) % 2, :]).then_inc(w_used, 1)

            def tile_w(base, i):
                return slot(base + i // 3)[:, i % 3 * TILE:(i % 3 + 1) * TILE]

            def proj(u, n, lhs, rhs, chunks=KC):
                bank = PROJ_BANKS[u % 3]
                if u >= 3:
                    pe.wait_ge(proj_used, u - 2)
                for c in range(chunks):
                    mm = nc.tensor.matmul(bank[:, 0:n], lhs(c), rhs(c), start=(c == 0), stop=(c == chunks - 1))
                return mm.then_inc(proj_ready, 1)

            def attention(heads, n0, qT, kT, v, ex, pts, o_banks, between=None):
                for j in range(heads + 2):
                    if j < heads:
                        r, b = j % 2 * HEAD, B[j % 2]
                        if n0 + j >= 2:
                            pe.wait_ge(s_used, n0 + j - 1)
                        lo = slice(r, r + HEAD)
                        nc.tensor.matmul(b[:, 0:T], qT[lo, j // 2, P:T], kT[lo, j // 2, :], start=True, stop=True)
                        nc.tensor.matmul(b[:, T:T + P], qT[lo, j // 2, 0:P], kT[lo, j // 2, 0:P], start=True, stop=True).then_inc(s_ready, 1)
                    if 1 <= j <= heads:
                        a = j - 1
                        pe.wait_ge(p_ready, n0 + a + 1)
                        b, e = B[2 + a % 2], ex[:, a % 2, :]
                        for d, s in ((0, T), (P, 0), (2 * P, P)):
                            mm = nc.tensor.transpose(b[:, d:d + P], e[:, s:s + P], ident)
                        mm.then_inc(pt_ready, 1)
                    if between is not None and j < heads:
                        between(j)
                    if j >= 2:
                        a = j - 2
                        pe.wait_ge(pts_ready, n0 + a + 1)
                        r, b, pt = a % 2 * HEAD, o_banks[a // 2 % len(o_banks)], pts[:, a % 2, :]
                        if a % 2 == 0 and (n0 + a) // 2 >= len(o_banks):
                            pe.wait_ge(o_copied, (n0 + a) // 2 - len(o_banks) + 1)
                        nc.tensor.matmul(b[r:r + HEAD, 0:T], v[:, 0, a * HEAD:(a + 1) * HEAD], pt[:, 0:T], start=True, stop=False, skip_group_check=True)
                        nc.tensor.matmul(b[r:r + HEAD, P:T], v[:, 1, a * HEAD:(a + 1) * HEAD], pt[:, T:T + P], start=False, stop=True, skip_group_check=True).then_inc(o_ready, 1)

            pe.wait_ge(ones_ready, 1)
            pe.wait_ge(sel_loaded, 32)
            nc.tensor.matmul(B[7][0:HEADS_1 + HEADS_2, :], relw[:], sel_sb[0:BUCKETS + 1, :], start=True, stop=True).then_inc(line_ready, 1)

            norm_sum(0)
            pe.wait_ge(pool_loaded, 32)
            pe.wait_ge(const_loaded, 16)
            for g in range(4):
                pe.wait_ge(pool_d, g + 1)
                for e in range(2):
                    for c in range(2):
                        mm = nc.tensor.matmul(B[g][:, e * T:(e + 1) * T], poolw[:, g, c, e * P:(e + 1) * P], h[:, 2 * g + c, :], start=(c == 0), stop=(c == 1))
                mm.then_inc(pool_y, 1)
            norm_sum(1)
            ffn(S_FFN1, 1, 0)
            def modulation(n):
                wait_slot(S_ADA + n)
                w = slot(S_ADA + n)
                for b in range(6):
                    c, j = divmod(6 * n + b, 12)
                    r = 32 * (j % 4)
                    mm = nc.tensor.matmul(B[5 + j // 4][r:r + 1, :], csil[:, c:c + 1], w[:, b * 512:(b + 1) * 512], start=(c == 0), stop=(c == KC - 1),
                                          skip_group_check=True, tile_position=(0, r))
                mm.then_inc(w_used, 1)

            norm_sum(2)
            pe.wait_ge(h_ready, H_BASE[2] + KC)
            for g, (t0, nt) in enumerate(VGROUPS1):
                wait_slot(S_KVQ + g)
                w = slot(S_KVQ + g)[:, 0:nt * TILE].rearrange("p (t c m) -> p t c m", t=nt, c=KC)
                for tb in range(TB):
                    proj(U_V1 + 2 * g + tb, nt * P, lambda c: h[:, c, tb * P:(tb + 1) * P], lambda c: w[:, :, c, :])
            used = 0
            for i in range(8, 24):
                if i == 16:
                    pe.wait_ge(h_ready, H_BASE[2] + 2 * KC)
                wait_slot(S_KVQ + i // 3)
                w = tile_w(S_KVQ, i)
                src = h if i < 16 else hq
                proj(U_K1 + i - 8, T, lambda c: w[:, c * P:(c + 1) * P], lambda c: src[:, c, :])
            pe.wait_ge(proj_ready, U_Z)
            pe.sem_inc(w_used, 8)
            pe.wait_ge(proj_used, U_Z)
            pe.wait_ge(csil_ready, 1)
            attention(HEADS_1, 0, q1, k1, v1, ex, pts, B[4:5], between=modulation)
            pe.wait_ge(o_copied, HEADS_1 // 2)
            for i in range(24, 32):
                dc = i - 24
                wait_slot(S_O + dc // 3)
                w = tile_w(S_O, dc)
                for c in range(KC):
                    mm = nc.tensor.matmul(B[dc // 2][:, dc % 2 * T:dc % 2 * T + T], w[:, c * P:(c + 1) * P], h[:, c, :], start=(c == 0), stop=(c == KC - 1))
                if dc % 2:
                    mm.then_inc(res_ready, 1)
            pe.wait_ge(res_ready, 4)
            pe.sem_inc(w_used, 3)
            pe.wait_ge(mod_copied, 4)
            norm_sum(3)
            ffn(S_FFN2, 3, FFN_CHUNKS)
            pe.wait_ge(mod_back, 16)
            nc.tensor.transpose(B[7][:, 0:48], mod48[0:48, :], ident[0:48, 0:48]).then_inc(mod_turned, 1)
            norm_sum(4)
            norm_sum(5)
            def u_of(i):
                return U_Z + 1 + i

            pe.wait_ge(h_ready, H_BASE[5] + KC)
            u = U_Z
            for t0, w0, nt in ((0, 0, 3 * P), (3, 3, P), (4, 4, IDX_HEADS)):
                wait_slot(S_WIN + t0 // 3)
                w = tile_w(S_WIN, t0)
                if t0 == 0:
                    w3 = slot(S_WIN).rearrange("p (t c m) -> p t c m", t=3, c=KC)
                for tb in range(TB):
                    proj(u, nt, lambda c: h[:, c, tb * P:(tb + 1) * P], (lambda c: w3[:, :, c, :]) if t0 == 0 else (lambda c: w[:, c * P:c * P + nt]))
                    u += 1
                if t0 == 0:
                    pe.wait_ge(proj_ready, u)
                    pe.sem_inc(w_used, 1)

            def head_sums(src, b0):
                for c in range(AC):
                    mm = nc.tensor.matmul(B[b0 + c // 2][:, c % 2 * T:c % 2 * T + T], headones, src[:, c, :], start=True, stop=True)
                return mm

            def low_rank(b0, lo, src, col):
                for c in range(AC):
                    mm = nc.tensor.matmul(B[b0 + c // 2][:, c % 2 * T:c % 2 * T + T], loraw[lo, col + c * P:col + (c + 1) * P], lo_t[lo, src, :], start=True, stop=True)
                mm.then_inc(lora_out, 1)

            def indexer(n):
                qb, cp = n // 2, n % 2
                nk = (qb + 1) * P
                if n:
                    pe.wait_ge(relu_ready, n)
                for cc in range(2):
                    for r in range(4):
                        mm = nc.tensor.matmul(B[r][:, cc * T:cc * T + nk], iqT[32 * r:32 * r + 32, 2 * cp + cc, qb * P:(qb + 1) * P],
                                              ikr[32 * r:32 * r + 32, 0:nk], start=True, stop=True)
                mm.then_inc(idx_ready, 1)

            for i in range(5, 48):
                if i in IDX_AT:
                    pe.wait_ge(proj_used, u_of(18))
                    indexer(IDX_AT.index(i))
                if i == LORA_AT:
                    pe.wait_ge(relu_ready, 4)
                    pe.wait_ge(lora_loaded, 16)
                    pe.wait_ge(lora_in, 2)
                    low_rank(0, slice(0, 64), 0, 0)
                    low_rank(2, slice(64, 128), 0, 0)
                if i == KK_AT:
                    pe.wait_ge(kk_sq, 1)
                    pe.wait_ge(decay_ready, 1)
                    head_sums(b2, 0).then_inc(kk_sum, 1)
                if i == BONUS_AT:
                    pe.wait_ge(iclr_ready, 1)
                    pe.wait_ge(bonus_in, 1)
                    head_sums(b2, 2).then_inc(bonus_sum, 1)
                wait_slot(S_WIN + i // 3)
                w = tile_w(S_WIN, i)
                proj(u, T, lambda c: w[:, c * P:(c + 1) * P], lambda c: h[:, c, :])
                u += 1
                if i % 3 == 0:
                    pe.wait_ge(proj_ready, u - 1)
                    pe.sem_inc(w_used, 1)
            pe.wait_ge(proj_ready, u)
            pe.sem_inc(w_used, 1)
            pe.wait_ge(proj_used, u)
            low_rank(6, slice(0, 128), 1, ATTN_W)
            pe.wait_ge(bonus_used, 1)
            attention(HEADS_2, HEADS_1, q2, k2, v2, ex2, pts2, B[4:6])

            pe.wait_ge(o_copied, (HEADS_1 + HEADS_2) // 2)

            def pairs(fn):
                for c in range(NCH):
                    for hp in range(AC):
                        for p in range(2):
                            mm = fn(c, hp, slice(p * HEAD, (p + 1) * HEAD))
                return mm

            def block_of(b0, c, hp, rows):
                n = (c * AC + hp) * CH
                return B[b0 + n // 512][rows, n % 512:n % 512 + CH]

            pe.wait_ge(tilde_ready, 1)
            for n, src in enumerate((v_t, b5, k_t)):
                pairs(lambda c, hp, rows: nc.tensor.matmul(block_of(2 * n, c, hp, rows), src[rows, hp, c * CH:(c + 1) * CH], ident[rows, rows], start=True, stop=True)).then_inc(turned, 1)

            pair_list = [(b5, b4, 6), (b4, b5, 0), (k_t, b4, 2), (b5, b3, 4), (k_t, b3, 6)]
            for n, (lhs, rhs, b0) in enumerate(pair_list):
                if n in (1, 2, 3):
                    pe.wait_ge(turned_used, n)
                if n == 4:
                    pe.wait_ge(pair_used, 1)

                def product(c, hp, rows):
                    t = slice(c * CH, (c + 1) * CH)
                    return nc.tensor.matmul(block_of(b0, c, hp, rows), lhs[rows, hp, t], rhs[rows, hp, t], start=True, stop=True)

                pairs(product).then_inc(pair_ready, 1)
            pe.wait_ge(pair_used, 5)
            for n in range(len(LEVELS)):
                blk = lambda a, c, hp, rows: a[rows, c * AC + hp, :]
                pe.wait_ge(level_m, n + 1)
                pairs(lambda c, hp, rows: nc.tensor.matmul(block_of(0, c, hp, rows), blk(m_lev, c, hp, rows), blk(inv, c, hp, rows), start=True, stop=True)).then_inc(level_x, 1)
                pe.wait_ge(x_copied, n + 1)
                pairs(lambda c, hp, rows: nc.tensor.matmul(block_of(2, c, hp, rows), blk(inv_t, c, hp, rows), blk(xm, c, hp, rows), start=True, stop=True))
                pairs(lambda c, hp, rows: nc.tensor.matmul(block_of(4, c, hp, rows), blk(xm, c, hp, rows), blk(inv_t, c, hp, rows), start=True, stop=True)).then_inc(level_d, 1)
            pe.wait_ge(inv_ready, 1)
            halves = [(hp, slice(p * HEAD, (p + 1) * HEAD)) for hp in range(AC) for p in range(2)]
            for c in range(NCH):
                t = slice(c * CH, (c + 1) * CH)
                g_in = gst[:, (c - 1) % 2]
                if c:
                    pe.wait_ge(state_ready, c)
                for hp, rows in halves:
                    o, n = B[0][rows, hp * CH:(hp + 1) * CH], c * AC + hp
                    if c:
                        nc.tensor.matmul(o, b4[rows, hp, t], g_in[rows, hp, :], start=True, stop=False)
                    mm = nc.tensor.matmul(o, m_ak[rows, n, :], vt[rows, n, :], start=(c == 0), stop=True)
                mm.then_inc(rhs_ready, 1)
                pe.wait_ge(rhs_copied, c + 1)
                for hp, rows in halves:
                    n = c * AC + hp
                    mm = nc.tensor.matmul(B[1][rows, hp * CH:(hp + 1) * CH], inv_t[rows, n, :], rhs_u[rows, hp, :], start=True, stop=True)
                mm.then_inc(u_ready, 1)
                pe.wait_ge(u_copied, c + 1)
                for hp, rows in halves:
                    o, n = B[2][rows, hp * CH:(hp + 1) * CH], c * AC + hp
                    nc.tensor.matmul(o, bt[rows, n, :], u_sb[rows, hp, :], start=True, stop=False)
                    mm = nc.tensor.matmul(o, kt[rows, n, :], vt[rows, n, :], start=False, stop=True)
                mm.then_inc(g_ready, 1)
                if c >= 2:
                    pe.wait_ge(y_copied, c - 1)
                for hp, rows in halves:
                    o, n = B[3 + c % 2][rows, hp * CH:(hp + 1) * CH], c * AC + hp
                    if c:
                        nc.tensor.matmul(o, g_in[rows, hp, :], b3[rows, hp, t], start=True, stop=False)
                    nc.tensor.matmul(o, u_sb[rows, hp, :], m_rb[rows, n, :], start=(c == 0), stop=False)
                    mm = nc.tensor.matmul(o, vt[rows, n, :], m_rk[rows, n, :], start=False, stop=True)
                mm.then_inc(y_ready, 1)
            pe.wait_ge(y_copied, NCH)
            head_sums(b1, 6).then_inc(gn_sum, 1)
            pe.wait_ge(gn_sq, 1)
            head_sums(f0, 0).then_inc(gn_var, 1)
            pe.wait_ge(rw_ready, 1)
            for n, (src, b0) in enumerate(((o2, 0), (rw, 4))):
                for i in range(4):
                    k = 4 * n + i
                    wait_slot(S_BR + k // 3)
                    w = tile_w(S_BR, k)
                    for e in range(2):
                        for c in range(AC):
                            mm = nc.tensor.matmul(B[b0 + i][:, e * T:(e + 1) * T], w[:, (e * AC + c) * P:(e * AC + c + 1) * P], src[:, c, :], start=(c == 0), stop=(c == AC - 1))
                    mm.then_inc(br_ready, 1)
            for dc in range(KC):
                k = 8 + dc
                wait_slot(S_BR + k // 3)
                w = tile_w(S_BR, k)
                if dc == 0:
                    pe.wait_ge(mixed_ready, 4)
                for c in range(KC):
                    mm = nc.tensor.matmul(B[dc // 2][:, dc % 2 * T:dc % 2 * T + T], w[:, c * P:(c + 1) * P], mixed[:, c, :], start=(c == 0), stop=(c == KC - 1))
                if dc % 2:
                    mm.then_inc(res_ready, 1)
            norm_sum(6)
            pe.wait_ge(h_ready, H_BASE[6] + KC)
            for b in range(4):
                for c in range(4):
                    lo = (b // 2) * P
                    mm = nc.tensor.transpose(B[4 + b][:, c * P:(c + 1) * P], h[:, b % 2 * 4 + c, lo:lo + P], ident)
                mm.then_inc(tok_turned, 1)
            pe.wait_ge(router_loaded, 32)
            for tb in range(TB):
                for c in range(KC):
                    mm = nc.tensor.matmul(B[0][:, tb * EXPERTS:(tb + 1) * EXPERTS], h[:, c, tb * P:(tb + 1) * P], routerw[:, c, :], start=(c == 0), stop=(c == KC - 1))
            mm.then_inc(logits_ready, 1)

            def expert_gate_up(w, f, bank, signal):
                gate_up(bank, lambda c: w[:, c * 512 + f * P:c * 512 + (f + 1) * P], lambda c: w[:, c * 512 + EXPERT_FF + f * P:c * 512 + EXPERT_FF + (f + 1) * P], signal)

            def expert_down(w, f):
                return down(lambda c: w[:, GATE_UP + f * D + c * P:GATE_UP + f * D + (c + 1) * P], act_f[:, f, :])

            done = 2 * FFN_CHUNKS
            pe.wait_ge(shared_landed, 16)
            for f in range(2):
                pe.wait_ge(tok_lo_ready, f + 1)
                expert_gate_up(SHARED_UNIT, f, B[4 + f], gu_ready)
            pe.wait_ge(scores_ready, 1)
            clear_y()
            for f in range(2):
                pe.wait_ge(act_ready, done + f + 1)
                expert_down(SHARED_UNIT, f)
            pe.wait_ge(tok_lo_ready, 4)
            pe.wait_ge(mask_ready, 1)
            before = cst("before")
            nc.tensor.matmul(B[6][:, 0:EXPERTS], before, mask_e[:, 0, :], start=True, stop=True)
            nc.tensor.matmul(B[6][:, EXPERTS:2 * EXPERTS], before, mask_e[:, 1, :], start=True, stop=False, skip_group_check=True)
            nc.tensor.matmul(B[6][:, EXPERTS:2 * EXPERTS], ones[:], mask_e[:, 0, :], start=False, stop=True, skip_group_check=True).then_inc(rank_ready, 1)
            pe.wait_ge(gates_ready, 1)
            for n, a in enumerate((rank_e, sel_e)):
                for tb in range(TB):
                    mm = nc.tensor.transpose(B[7][0:EXPERTS, n * T + tb * P:n * T + (tb + 1) * P], a[:, tb, :], ident)
            mm.then_inc(gates_turned, 1)
            pe.wait_ge(beyond_ready, 1)
            for tb in range(TB):
                mm = nc.tensor.transpose(B[5][0:EXPERTS, tb * P:(tb + 1) * P], dense_e[:, tb, :], ident)
            mm.then_inc(gates_turned, 1)
            nc.tensor.matmul(B[6][:, T:T + 1], ones[:], beyond, start=True, stop=True).then_inc(beyond_sum, 1)

            def gather(q, step, bank):
                for c in range(2):
                    kc = 2 * step + c
                    for n, tok in enumerate((tok_hi, tok_lo)):
                        for tb in range(TB):
                            mm = nc.tensor.matmul(bank[:, c * 4 * CAP:(c + 1) * 4 * CAP], tok[:, tb, kc * P:(kc + 1) * P], pick[q % 2][:, tb, :],
                                                  start=(n == 0 and tb == 0), stop=(n == 1 and tb == TB - 1))
                mm.then_inc(gather_ready, 1)

            def spread_out(k):
                for c in range(KC):
                    for part in (out_hi, out_lo):
                        mm = nc.tensor.matmul(B[c // 2][:, c % 2 * T:c % 2 * T + T], part[:, c * P:(c + 1) * P], spread[k % 2], start=False, stop=False, skip_group_check=True)
                mm.then_inc(pair_spread, 1)

            pe.wait_ge(pick_ready, 1)
            pe.wait_ge(gates_copied, 2)
            pe.wait_ge(flag_ready, 1)
            for step in range(4):
                gather(0, step, B[4 + step])

            def two_quads(i, first=False, last=False):
                for k in range(4):
                    q, hs = k // 2, gathered_h[k // 2]
                    us = [k % 2 * 2, k % 2 * 2 + 1]
                    pe.wait_ge(gather_copied, 8 * i + (2 * k + 4) if not last or k < 3 else 8 * i + 8)
                    for u in us:
                        pe.wait_ge(gu_landed[u], 32 * i + 16 * (q + 1))
                    for c in range(KC):
                        for j, u in enumerate(us):
                            mm = nc.tensor.matmul(B[4][CAP * j:CAP * (j + 1), :], hs[:, c, CAP * u:CAP * (u + 1)], unit(u)[:, c * 512:(c + 1) * 512],
                                                  start=(c == 0), stop=(c == KC - 1), skip_group_check=True)
                    mm.then_inc(pair_gu, 1)
                    more = not (last and k >= 2)
                    if more:
                        pe.wait_ge(pick_ready, 2 * i + (q + 2))
                        gather(q + 1, 2 * (k % 2), B[5])
                    if not (first and k == 0):
                        pe.wait_ge(pair_lo, 4 * i + k)
                        spread_out(k - 1)
                    pe.wait_ge(pair_act, 4 * i + (k + 1))
                    for f in range(2):
                        mm = nc.tensor.transpose(B[7][:, f * P:(f + 1) * P], act_p[:, f * P:(f + 1) * P], ident)
                    mm.then_inc(pair_turned, 1)
                    if more:
                        gather(q + 1, 2 * (k % 2) + 1, B[4])
                    pe.wait_ge(pair_act_t, 4 * i + (k + 1))
                    for u in us:
                        pe.wait_ge(down_landed[u], 32 * i + 16 * (q + 1))
                    for half in range(2):
                        for f in range(2):
                            for j, u in enumerate(us):
                                lo = GATE_UP + f * D + half * 512
                                mm = nc.tensor.matmul(B[6 + half][CAP * j:CAP * (j + 1), :], act_pt[:, f, CAP * j:CAP * (j + 1)], unit(u)[:, lo:lo + 512],
                                                      start=(f == 0), stop=(f == 1), skip_group_check=True)
                        mm.then_inc(pair_down, 1)

            two_quads(0, first=True)
            with pe.Fori(1, QUADS // 2 - 1) as i:
                two_quads(i)
            two_quads(QUADS // 2 - 1, last=True)
            pe.wait_ge(pair_lo, PAIRS)
            spread_out(3)
            overflow = pe.value_load(flag[0:1, :])
            with pe.If(overflow > 0):
                with pe.Fori(0, EXPERTS // UNITS) as i:
                    for s in range(2 * UNITS + 1):
                        if s < 2 * UNITS:
                            if s % 2 == 0:
                                pe.wait_ge(unit_landed[s // 2], 16 * i + 16)
                            expert_gate_up(unit(s // 2), s % 2, B[4 + s % 2], dense_gu)
                        if s >= 1:
                            pe.wait_ge(dense_act, 2 * UNITS * i + s)
                            mm = expert_down(unit((s - 1) // 2), (s - 1) % 2)
                            if s % 2 == 0:
                                mm.then_inc(unit_used, 1)
            norm_sum(7)

        @block.scalar
        def _(act):
            def norm_squares(k):
                for g in range(4):
                    if k == 0:
                        act.wait_ge(x_loaded, 16)
                    else:
                        act.wait_ge(x_ready, 4 * (k - 1) + g + 1)
                    nc.scalar.activation(sq[:, 2 * g:2 * g + 2, :], x[:, 2 * g:2 * g + 2, :], ACT.Square).then_inc(sq_ready, 1)
                act.wait_ge(ss_ready, k + 1)
                nc.scalar.activation(rt[:], B[6][:, 0:T], ACT.Sqrt, scale=1.0 / D, bias=eps).then_inc(rt_ready, 1)

            def ffn(done):
                with act.Fori(0, 2) as i:
                    for s in range(RING):
                        act.wait_ge(gu_ready, RING * i + (done + s + 1))
                        nc.scalar.activation(sig_f[:, s % 2, :], B[4 + s % 2][:, 0:T], ACT.Sigmoid).then_inc(sig_ready, 1)

            def evacuate(u, dst, n=T, func=ACT.Copy):
                act.wait_ge(proj_ready, u + 1)
                nc.scalar.activation(dst, PROJ_BANKS[u % 3][:, 0:n], func).then_inc(proj_used, 1)

            def attention(heads, n0, oT, ex, pts, o_banks):
                for j in range(heads + 2):
                    if j < heads:
                        act.wait_ge(max_ready, n0 + j + 1)
                        e, k = ex[:, j % 2, :], 2 * (j % 2)
                        nc.scalar.activation(e[:, 0:T], e[:, 0:T], ACT.Exp, bias=nmax[:, k:k + 1], accum_out=rsum[:, k:k + 1])
                        nc.scalar.activation(e[:, T:T + P], e[:, T:T + P], ACT.Exp, bias=nmax[:, k + 1:k + 2], accum_out=rsum[:, k + 1:k + 2]).then_inc(exp_ready, 1)
                    if 1 <= j <= heads:
                        a = j - 1
                        act.wait_ge(pt_ready, n0 + a + 1)
                        if a >= 2:
                            act.wait_ge(o_ready, n0 + a - 1)
                        nc.scalar.activation(pts[:, a % 2, :], B[2 + a % 2][:, 0:384], ACT.Copy).then_inc(pts_ready, 1)
                    if j >= 2 and j % 2:
                        a = (j - 2) // 2
                        act.wait_ge(o_ready, n0 + 2 * a + 2)
                        nc.scalar.activation(oT[:, a, :], o_banks[a % len(o_banks)][:, 0:T], ACT.Copy).then_inc(o_copied, 1)

            act.wait_ge(line_ready, 1)
            nc.scalar.activation(line_sb[0:HEADS_1 + HEADS_2, :], B[7][0:HEADS_1 + HEADS_2, :], ACT.Copy).then_inc(line_copied, 1)
            act.wait_ge(ones_ready, 1)
            norm_squares(0)
            norm_squares(1)
            act.wait_ge(vec_loaded, 16)
            nc.scalar.activation(csig, vecs[:, VEC["c"][0]:VEC["c"][1]], ACT.Sigmoid).then_inc(csig_ready, 1)
            ffn(0)
            norm_squares(2)
            for g, (t0, nt) in enumerate(VGROUPS1):
                for tb in range(TB):
                    evacuate(U_V1 + 2 * g + tb, v1[:, tb, t0 * P:(t0 + nt) * P], nt * P)
            for c in range(KC):
                evacuate(U_K1 + c, k1[:, c, :])
            for c in range(KC):
                evacuate(U_Q1 + c, q1[:, c, :])
            attention(HEADS_1, 0, h, ex, pts, B[4:5])
            act.wait_ge(w_used, S_O)
            for q in range(4):
                nc.scalar.activation(modrow[32 * q:32 * q + 1, :, :], banks[32 * q:32 * q + 1, 5:8, :], ACT.Copy).then_inc(mod_copied, 1)
            norm_squares(3)
            ffn(FFN_CHUNKS)
            norm_squares(4)
            norm_squares(5)
            u = U_Z
            for t0, nt in ((0, 3 * P), (3, P)):
                for tb in range(TB):
                    evacuate(u, v2[:, tb, t0 * P:t0 * P + nt], nt)
                    u += 1
            for tb in range(TB):
                evacuate(u, iw[:, tb, :], IDX_HEADS)
                u += 1
            dsts = [q2[:, c, :] for c in range(AC)] + [k2[:, c, :] for c in range(AC)] + [iqT[:, c, :] for c in range(AC)] + [ikr]
            dsts += [zr[:, c, 1:] for c in ZR_ORDER]
            dsts += [d[:, c, :] for d in (sig_a, sig_r) for c in range(KC)]

            def indexer(n):
                nk = (n // 2 + 1) * P
                act.wait_ge(idx_ready, n + 1)
                if n:
                    act.wait_ge(relu_used, n)
                for r in range(4):
                    src = B[r].rearrange("p (a t) -> p a t", a=2)[:, :, 0:nk]
                    mm = nc.scalar.activation(relu_i[:, 2 * r:2 * r + 2, 0:nk], src, ACT.Relu)
                mm.then_inc(relu_ready, 1)

            for i, d in enumerate(dsts, 5):
                if i in IDX_AT:
                    indexer(IDX_AT.index(i))
                if i == LO_AT:
                    act.wait_ge(shifted, 2)
                    nc.scalar.activation(lo_t[0:64, 0, :], lo_t[0:64, 0, :], ACT.Tanh).then_inc(lora_in, 1)
                    nc.scalar.activation(lo_t[:, 1, :], lo_t[:, 1, :], ACT.Sigmoid).then_inc(lora_in, 1)
                if i == DECAY_AT:
                    act.wait_ge(lora_out, 1)
                    for c in range(AC):
                        nc.scalar.activation(b1[:, c, :], B[c // 2][:, c % 2 * T:c % 2 * T + T], ACT.Sigmoid, bias=vcol("decay_w0", c)).then_inc(act_step, 1)
                    act.wait_ge(lora_out, 2)
                    for c in range(AC):
                        mm = nc.scalar.activation(b5[:, c, :], B[2 + c // 2][:, c % 2 * T:c % 2 * T + T], ACT.Sigmoid, bias=vcol("iclr_a0", c))
                    mm.then_inc(iclr_ready, 1)
                    act.wait_ge(act_step, AC)
                    nc.scalar.activation(b1, b1, ACT.Exp, scale=-math.exp(-0.5)).then_inc(decay_ready, 1)
                if i == KK_SQRT_AT:
                    act.wait_ge(kk_sum, 1)
                    nc.scalar.activation(b6, banks[:, 0:2, :].rearrange("p a (b t) -> p (a b) t", b=2), ACT.Sqrt).then_inc(kk_norm, 1)
                evacuate(u, d, func=ACT.Copy if i < 32 else ACT.Sigmoid)
                u += 1
            act.wait_ge(lora_out, 3)
            act.wait_ge(tilde_ready, 1)
            nc.scalar.activation(b6, banks[:, 6:8, :].rearrange("p a (b t) -> p (a b) t", b=2), ACT.Copy).then_inc(gate_ready, 1)
            attention(HEADS_2, HEADS_1, o2, ex2, pts2, B[4:6])

            def pair_bank(b0):
                return banks[:, b0:b0 + 2, :].rearrange("p a (b t) -> p (a b) t", t=CH)

            for n, dst in enumerate((vt, bt, kt)):
                act.wait_ge(turned, n + 1)
                nc.scalar.activation(dst, pair_bank(2 * n), ACT.Copy).then_inc(turned_used, 1)
            for n in range(len(LEVELS)):
                act.wait_ge(level_x, n + 1)
                nc.scalar.activation(xm, pair_bank(0), ACT.Copy).then_inc(x_copied, 1)

            def quarter(b):
                return B[b][:, 0:T].rearrange("p (a t) -> p a t", a=AC)

            for c in range(NCH):
                act.wait_ge(rhs_ready, c + 1)
                nc.scalar.activation(rhs_u, quarter(0), ACT.Copy).then_inc(rhs_copied, 1)
                act.wait_ge(u_ready, c + 1)
                if c:
                    act.wait_ge(y_ready, c)
                nc.scalar.activation(u_sb, quarter(1), ACT.Copy).then_inc(u_copied, 1)
                act.wait_ge(y_ready, c + 1)
                nc.scalar.activation(b1[:, :, c * CH:(c + 1) * CH], quarter(3 + c % 2), ACT.Copy).then_inc(y_copied, 1)
            act.wait_ge(gn_var, 1)
            nc.scalar.activation(f1, banks[:, 0:2, :].rearrange("p a (b t) -> p (a b) t", b=2), ACT.Sqrt, scale=1.0 / HEAD, bias=gn_eps).then_inc(gn_rt, 1)
            norm_squares(6)
            for b in range(4):
                act.wait_ge(tok_turned, b + 1)
                nc.scalar.activation(tok_hi[:, b // 2, b % 2 * 512:(b % 2 + 1) * 512], B[4 + b], ACT.Copy).then_inc(tok_hi_ready, 1)
            act.wait_ge(logits_ready, 1)
            nc.scalar.activation(score_e, B[0][:, 0:TB * EXPERTS].rearrange("p (a e) -> p a e", a=TB), ACT.Sigmoid).then_inc(scores_ready, 1)
            done = 2 * FFN_CHUNKS
            for f in range(2):
                act.wait_ge(gu_ready, done + f + 1)
                nc.scalar.activation(sig_f[:, f, :], B[4 + f][:, 0:T], ACT.Sigmoid).then_inc(sig_ready, 1)
            act.wait_ge(gates_turned, 1)
            nc.scalar.activation(rows_t[0:EXPERTS, :], B[7][0:EXPERTS, :], ACT.Copy).then_inc(gates_copied, 1)
            act.wait_ge(gates_turned, 2)
            nc.scalar.activation(dense_t[0:EXPERTS, :], B[5][0:EXPERTS, 0:T], ACT.Copy).then_inc(gates_copied, 1)

            def copy_gathered(q, step, bank):
                nc.scalar.activation(gathered_h[q % 2][:, 2 * step:2 * step + 2, :], bank.rearrange("p (c s) -> p c s", c=2), ACT.Copy).then_inc(gather_copied, 1)

            for step in range(4):
                act.wait_ge(gather_ready, step + 1)
                copy_gathered(0, step, B[4 + step])

            def two_quads(i, last=False):
                for k in range(4):
                    q, more = k // 2, not (last and k >= 2)
                    act.wait_ge(pair_gu, 4 * i + (k + 1))
                    nc.scalar.activation(sig_p, B[4][:, 0:T], ACT.Sigmoid).then_inc(pair_sig, 1)
                    if more:
                        act.wait_ge(gather_ready, 8 * i + (2 * k + 5))
                        copy_gathered(q + 1, 2 * (k % 2), B[5])
                    act.wait_ge(pair_turned, 4 * i + (k + 1))
                    nc.scalar.activation(act_pt, B[7][:, 0:2 * P].rearrange("p (f s) -> p f s", f=2), ACT.Copy).then_inc(pair_act_t, 1)
                    if more:
                        act.wait_ge(gather_ready, 8 * i + (2 * k + 6))
                        copy_gathered(q + 1, 2 * (k % 2) + 1, B[4])
                    for half in range(2):
                        act.wait_ge(pair_down, 8 * i + (2 * k + half + 1))
                        nc.scalar.activation(out_hi[:, half * 512:(half + 1) * 512], B[6 + half], ACT.Copy).then_inc(pair_hi, 1)

            with act.Fori(0, QUADS // 2 - 1) as i:
                two_quads(i)
            two_quads(QUADS // 2 - 1, last=True)
            act.wait_ge(flag_ready, 1)
            overflow = act.value_load(flag[0:1, :])
            with act.If(overflow > 0):
                with act.Fori(0, EXPERTS // UNITS) as i:
                    for s in range(2 * UNITS):
                        act.wait_ge(dense_gu, 2 * UNITS * i + (s + 1))
                        nc.scalar.activation(sig_f[:, s % 2, :], B[4 + s % 2][:, 0:T], ACT.Sigmoid).then_inc(dense_sig, 1)
            norm_squares(7)

        @block.vector
        def _(dve):
            steps = [0]

            def then(ins):
                steps[0] += 1
                ins.then_inc(dve_step, 1)
                dve.wait_ge(dve_step, steps[0])

            def norm_scale(k, weight, dst):
                dve.wait_ge(rt_ready, k + 1)
                then(nc.vector.reciprocal(rinv[:], rt[:]))
                for c in range(KC):
                    nc.vector.scalar_tensor_tensor(dst(c), x[:, c, :], weight(c), rinv[:], ALU.mult, ALU.mult).then_inc(h_ready, 1)

            def ffn(base, done, k):
                with dve.Fori(0, 2) as i:
                    for s in range(RING):
                        dve.wait_ge(sig_ready, RING * i + (done + s + 1))
                        gu = B[4 + s % 2]
                        nc.vector.tensor_tensor(gated[:, s % 2, :], gu[:, 0:T], sig_f[:, s % 2, :], ALU.mult).then_inc(dve_step, 1)
                        dve.wait_ge(dve_step, RING * i + (steps[0] + s + 1))
                        nc.vector.tensor_tensor(act_f[:, s % 2, :], gated[:, s % 2, :], gu[:, T:2 * T], ALU.mult).then_inc(act_ready, 1)
                steps[0] += FFN_CHUNKS
                dve.wait_ge(w_used, base + FFN_CHUNKS)
                for b in range(4):
                    xb = x[:, 2 * b:2 * b + 2, :]
                    nc.vector.tensor_tensor(xb, B[b].rearrange("p (a t) -> p a t", a=2), xb, ALU.add).then_inc(x_ready, 1)

            def attention(heads, n0, bias, extra, ex):
                for j in range(heads + 1):
                    if j < heads:
                        b, e, k = B[j % 2], ex[:, j % 2, :], 2 * (j % 2)
                        dve.wait_ge(s_ready, n0 + j + 1)
                        if j >= 2:
                            dve.wait_ge(pt_ready, n0 + j - 1)
                        nc.vector.scalar_tensor_tensor(e[:, 0:T], b[:, 0:T], HEAD ** -0.5, bias[:, j, :], ALU.mult, ALU.add)
                        m = nc.vector.scalar_tensor_tensor(e[:, T:T + P], b[:, T:T + P], HEAD ** -0.5, bias[:, j, P:T], ALU.mult, ALU.add)
                        m.then_inc(s_used, 1)
                        dve.wait_ge(s_used, n0 + j + 1)
                        if extra is not None:
                            then(nc.vector.tensor_tensor(e, e, extra, ALU.add))
                        nc.vector.tensor_reduce(nmax[:, k:k + 1], e[:, 0:T], AX_X, ALU.max, negate=True)
                        nc.vector.tensor_reduce(nmax[:, k + 1:k + 2], e[:, T:T + P], AX_X, ALU.max, negate=True).then_inc(max_ready, 1)
                    if j >= 1:
                        a = j - 1
                        e, k = ex[:, a % 2, :], 2 * (a % 2)
                        dve.wait_ge(exp_ready, n0 + a + 1)
                        then(nc.vector.reciprocal(rrec[:, k:k + 2], rsum[:, k:k + 2]))
                        nc.vector.tensor_scalar(e[:, 0:T], e[:, 0:T], rrec[:, k:k + 1], None, ALU.mult)
                        nc.vector.tensor_scalar(e[:, T:T + P], e[:, T:T + P], rrec[:, k + 1:k + 2], None, ALU.mult).then_inc(p_ready, 1)

            def residual(first):
                for b in range(4):
                    dve.wait_ge(res_ready, first + b + 1)
                    xb = x[:, 2 * b:2 * b + 2, :]
                    nc.vector.tensor_tensor(xb, B[b].rearrange("p (a t) -> p a t", a=2), xb, ALU.add).then_inc(x_ready, 1)

            nc.vector.memset(ones[:], 1.0)
            nc.vector.memset(zeros[:], 0.0)
            nc.vector.memset(eps, EPS)
            then(nc.vector.memset(gn_eps, GN_EPS))
            nc.vector.memset(hp[:, :, 0:PAD], 0.0).then_inc(ones_ready, 1)

            dve.wait_ge(vec_loaded, 16)
            norm_scale(0, lambda c: vcol("norm_mixer0", c), lambda c: hp[:, c, PAD:])
            dve.wait_ge(h_ready, KC)
            W = PAD + T
            then(nc.vector.tensor_tensor(pw_b[:, :, 1:W], hp[:, :, 1:W], hp[:, :, 0:W - 1], ALU.add))
            then(nc.vector.tensor_tensor(pw_c[:, 2:, 3:W], pw_b[:, 2:, 3:W], pw_b[:, 2:, 1:W - 2], ALU.add))
            then(nc.vector.tensor_tensor(pw_b[:, 4:, 7:W], pw_c[:, 4:, 7:W], pw_c[:, 4:, 3:W - 4], ALU.add))
            then(nc.vector.tensor_tensor(pw_c[:, 6:, 15:W], pw_b[:, 6:, 15:W], pw_b[:, 6:, 7:W - 8], ALU.add))
            dve.wait_ge(pool_loaded, 32)
            for g in range(4):
                win = (pw_b, pw_c)[g % 2][:, 2 * g:2 * g + 2, PAD:]
                hg = h[:, 2 * g:2 * g + 2, :]
                then(nc.vector.tensor_tensor(hg, win, icnt[:, g:g + 1, :].broadcast_to([P, 2, T]), ALU.mult))
                nc.vector.tensor_tensor(hg, hg, hp[:, 2 * g:2 * g + 2, PAD:], ALU.subtract).then_inc(pool_d, 1)
            for g in range(4):
                dve.wait_ge(pool_y, g + 1)
                for e in range(2):
                    c = 2 * g + e
                    last = nc.vector.scalar_tensor_tensor(x[:, c, :], B[g][:, e * T:(e + 1) * T], vcol("pool_scale", c), x[:, c, :], ALU.mult, ALU.add)
                last.then_inc(x_ready, 1)
            norm_scale(1, lambda c: vcol("norm_ffn0", c), lambda c: h[:, c, :])
            dve.wait_ge(csig_ready, 1)
            nc.vector.tensor_tensor(csil, csig, vecs[:, VEC["c"][0]:VEC["c"][1]], ALU.mult).then_inc(csil_ready, 1)
            ffn(S_FFN1, 0, 1)
            norm_scale(2, lambda c: vcol("kv_norm", c), lambda c: h[:, c, :])
            for c in range(KC):
                nc.vector.scalar_tensor_tensor(hq[:, c, :], x[:, c, :], vcol("norm_mixer1", c), rinv[:], ALU.mult, ALU.mult).then_inc(h_ready, 1)
            dve.wait_ge(bias_loaded, 16 * P // SHIFTS)
            attention(HEADS_1, 0, bias1, None, ex)
            residual(0)
            norm_scale(3, lambda c: vcol("norm_ffn1", c), lambda c: h[:, c, :])
            ffn(S_FFN2, FFN_CHUNKS, 3)
            dve.wait_ge(mod_turned, 1)
            then(nc.vector.tensor_tensor(mod[:], B[7][:, 0:48], vecs[:, VEC["ada_b"][0]:VEC["ada_b"][1]], ALU.add))
            for dst, col, g in ((scale1, 8, "norm1_g"), (scale2, 32, "norm2_g")):
                last = nc.vector.scalar_tensor_tensor(dst[:], mod[:, col:col + 8], 1.0, vecs[:, VEC[g][0]:VEC[g][1]], ALU.add, ALU.mult)
            then(last)
            dve.wait_ge(rt_ready, 5)
            then(nc.vector.reciprocal(rinv[:], rt[:]))
            for c in range(KC):
                last = nc.vector.scalar_tensor_tensor(x[:, c, :], x[:, c, :], vcol("final_norm", c), rinv[:], ALU.mult, ALU.mult)
                if c % 2:
                    last.then_inc(x_ready, 1)
            def norm_modulated(k, scale, shift):
                dve.wait_ge(rt_ready, k + 1)
                then(nc.vector.reciprocal(rinv[:], rt[:]))
                for c in range(KC):
                    last = nc.vector.scalar_tensor_tensor(h[:, c, :], x[:, c, :], scale[:, c:c + 1], rinv[:], ALU.mult, ALU.mult)
                then(last)
                for c in range(KC):
                    nc.vector.tensor_scalar(h[:, c, :], h[:, c, :], mod[:, shift + c:shift + c + 1], None, ALU.add).then_inc(h_ready, 1)

            norm_modulated(5, scale1, 0)
            dve.wait_ge(proj_used, U_Z + 6)
            then(nc.vector.tensor_scalar(iw, iw, IDX_HEADS ** -0.5 * IDX_DIM ** -0.5, None, ALU.mult))
            causal = cst("causal")
            parts = {1: slice(0, T), 0: slice(T, T + P)}
            dve.wait_ge(bias2_loaded, 16 * P // SHIFTS)
            then(nc.vector.memset(zr[:, :, 0:1], 0.0))

            def token_shift(lo, hi):
                first = U_Z + 1 + 18
                dve.wait_ge(proj_used, first + (ZR_ORDER.index(hi - 1) + 1))
                then(nc.vector.tensor_tensor(zs[:, lo:hi, :], zr[:, lo:hi, 0:T], zr[:, lo:hi, 1:], ALU.subtract))
                for c in range(lo, hi):
                    nc.vector.scalar_tensor_tensor(zs[:, c, :], zs[:, c, :], vcol("tshift_mu", c), zr[:, c, 1:], ALU.mult, ALU.add).then_inc(shifted, 1)

            for n in range(4):
                qb, cp = n // 2, n % 2
                nk = (qb + 1) * P
                dve.wait_ge(relu_ready, n + 1)
                for r in range(4):
                    for cc in range(2):
                        head = (2 * cp + cc) * 4 + r
                        acc, rl, w = work[:, parts[qb]], relu_i[:, 2 * r + cc, 0:nk], iw[:, qb, head:head + 1]
                        prev = causal[:, parts[qb]] if cp == 0 and r == 0 and cc == 0 else acc
                        then(nc.vector.scalar_tensor_tensor(acc, rl, w, prev, ALU.mult, ALU.add))
                dve.sem_inc(relu_used, 1)
                if n == 1:
                    token_shift(12, 14)
            for it in range(TOP_KEYS // 8):
                for qb in range(2):
                    last = nc.vector.max(top8[:, qb, :], work[:, parts[qb]])
                then(last)
                for qb in range(2):
                    last = nc.vector.match_replace(work[:, parts[qb]], top8[:, qb, :], work[:, parts[qb]], TAKEN)
                then(last)
            then(nc.vector.tensor_scalar(mask2, work, TAKEN / 2, MASKED, ALU.is_gt, ALU.mult))
            then(nc.vector.tensor_tensor(mask2, mask2, causal, ALU.add))
            token_shift(0, 12)
            dve.wait_ge(shifted, ZR)

            def per_chunk(fn):
                for c in range(AC):
                    last = fn(c)
                then(last)

            per_chunk(lambda c: nc.vector.tensor_scalar(b4[:, c, :], k_t[:, c, :], vcol("k_k", c), None, ALU.mult))
            nc.vector.tensor_tensor(b2, b4, b4, ALU.mult).then_inc(kk_sq, 1)
            dve.wait_ge(iclr_ready, 1)
            per_chunk(lambda c: nc.vector.tensor_scalar(b3[:, c, :], b5[:, c, :], 1.0, vcol("k_a", c), ALU.subtract, ALU.mult))
            then(nc.vector.scalar_tensor_tensor(k_t, b3, 1.0, k_t, ALU.add, ALU.mult))
            then(nc.vector.tensor_tensor(b3, r_t, k_t, ALU.mult))
            dve.wait_ge(kk_norm, 1)
            for c in range(AC):
                last = nc.vector.tensor_scalar(b2[:, c, :], b3[:, c, :], vcol("r_k", c), None, ALU.mult)
            last.then_inc(bonus_in, 1)
            then(nc.vector.tensor_scalar(b6, b6, 1e-12, None, ALU.max))
            then(nc.vector.reciprocal(b6, b6))
            then(nc.vector.tensor_tensor(b4, b4, b6, ALU.mult))
            starts = lambda a: a.rearrange("p a (c t) -> p a c t", t=CH)
            dve.wait_ge(decay_ready, 1)
            then(nc.vector.memset(b3, 0.0))
            then(nc.vector.tensor_copy(starts(b3)[:, :, :, 0], starts(b1)[:, :, :, 0]))
            then(nc.vector.memset(starts(b1)[:, :, :, 0:1], 0.0))
            dve.wait_ge(bonus_sum, 1)
            per_chunk(lambda c: nc.vector.tensor_tensor_scan(b2[:, c, :], b1[:, c, :], b3[:, c, :], 0.0, ALU.mult, ALU.add))
            nc.vector.tensor_copy(p_end, starts(b2)[:, :, :, CH - 1])
            then(nc.vector.tensor_copy(b3[:, :, 1:], b2[:, :, 0:T - 1]))
            then(nc.vector.memset(starts(b3)[:, :, :, 0:1], 1.0))
            then(nc.vector.reciprocal(b1, b2))
            then(nc.vector.tensor_tensor(b5, b4, b5, ALU.mult))
            then(nc.vector.scalar_tensor_tensor(b4, b4, -1.0, b3, ALU.mult, ALU.mult))
            nc.vector.tensor_tensor(b5, b5, b1, ALU.mult)
            nc.vector.tensor_tensor(b3, r_t, b2, ALU.mult)
            then(nc.vector.tensor_tensor(k_t, k_t, b1, ALU.mult))
            dve.sem_inc(tilde_ready, 1)
            nc.vector.tensor_tensor(b2, banks[:, 2:4, :].rearrange("p a (b t) -> p (a b) t", b=2), v_t, ALU.mult).then_inc(bonus_used, 1)

            attention(HEADS_2, HEADS_1, bias2, mask2, ex2)

            def pair_bank(b0):
                return banks[:, b0:b0 + 2, :].rearrange("p a (b t) -> p (a b) t", t=CH)

            def every(name, lo=0):
                a = CONST[name][0] + lo
                return con[:, a:a + CH].unsqueeze(1).broadcast_to([P, NCH * AC, CH])

            dve.wait_ge(pair_ready, 1)
            nc.vector.tensor_tensor(m_ab, pair_bank(6), every("strict_t"), ALU.mult).then_inc(pair_used, 1)
            dve.wait_ge(pair_used, 1)
            then(nc.vector.tensor_tensor(inv_t, m_ab, every("first_t"), ALU.mult))
            then(nc.vector.tensor_tensor(inv_t, inv_t, every("eye"), ALU.add))
            dve.wait_ge(pair_ready, 2)
            nc.vector.tensor_tensor(inv, pair_bank(0), every("first"), ALU.mult).then_inc(pair_used, 1)
            dve.wait_ge(pair_used, 2)
            then(nc.vector.tensor_tensor(inv, inv, every("eye"), ALU.add))
            for n, (dst, b0, m) in enumerate(((m_ak, 2, "strict_t"), (m_rb, 4, "upto_t"), (m_rk, 6, "upto_t"))):
                dve.wait_ge(pair_ready, n + 3)
                nc.vector.tensor_tensor(dst, pair_bank(b0), every(m), ALU.mult).then_inc(pair_used, 1)
            for n in range(len(LEVELS)):
                if n:
                    dve.wait_ge(level_x, n)
                nc.vector.tensor_tensor(m_lev, m_ab, every("levels_t", CH * n), ALU.mult).then_inc(level_m, 1)
                dve.wait_ge(level_d, n + 1)
                nc.vector.tensor_tensor(inv, inv, pair_bank(2), ALU.add)
                last = nc.vector.tensor_tensor(inv_t, inv_t, pair_bank(4), ALU.add)
                then(last)
            dve.sem_inc(inv_ready, 1)
            for c in range(NCH):
                dve.wait_ge(g_ready, c + 1)
                g_new, g_old = gst[:, c % 2], gst[:, (c - 1) % 2]
                add = B[2][:, 0:T].rearrange("p (a t) -> p a t", a=AC)
                pc = p_end[:, :, c:c + 1].broadcast_to([P, AC, CH])
                if c:
                    dve.wait_ge(y_ready, c)
                    then(nc.vector.tensor_tensor(g_new, add, g_old, ALU.add))
                    nc.vector.tensor_tensor(g_new, g_new, pc, ALU.mult).then_inc(state_ready, 1)
                else:
                    nc.vector.tensor_tensor(g_new, add, pc, ALU.mult).then_inc(state_ready, 1)
                dve.wait_ge(state_ready, c + 1)
            dve.wait_ge(gn_sum, 1)
            full = lambda b0: banks[:, b0:b0 + 2, :].rearrange("p a (b t) -> p (a b) t", b=2)
            then(nc.vector.scalar_tensor_tensor(b1, full(6), -1.0 / HEAD, b1, ALU.mult, ALU.add))
            nc.vector.tensor_tensor(f0, b1, b1, ALU.mult).then_inc(gn_sq, 1)
            dve.wait_ge(gn_rt, 1)
            then(nc.vector.reciprocal(f1, f1))
            then(nc.vector.tensor_tensor(b1, b1, f1, ALU.mult))
            per_chunk(lambda c: nc.vector.tensor_scalar(b1[:, c, :], b1[:, c, :], vcol("lnx_g", c), vcol("lnx_b", c), ALU.mult, ALU.add))
            then(nc.vector.tensor_tensor(b1, b1, b2, ALU.add))
            nc.vector.tensor_tensor(rw, b1, b6, ALU.mult).then_inc(rw_ready, 1)
            for b in range(4):
                dve.wait_ge(br_ready, b + 1)
                two = lambda a: a[:, 2 * b:2 * b + 2, :]
                pair = lambda k: B[k].rearrange("p (a t) -> p a t", a=2)
                nc.vector.tensor_tensor(two(mixed), pair(b), two(sig_a), ALU.mult)
            for b in range(4):
                dve.wait_ge(br_ready, b + 5)
                then(nc.vector.tensor_tensor(two(mixed_r), pair(4 + b), two(sig_r), ALU.mult))
                nc.vector.tensor_tensor(two(mixed), two(mixed), two(mixed_r), ALU.add).then_inc(mixed_ready, 1)

            def gated_residual(first, sem_of, gate):
                for b in range(4):
                    dve.wait_ge(sem_of, first + b + 1) if first is not None else None
                    for c in (2 * b, 2 * b + 1):
                        last = nc.vector.scalar_tensor_tensor(x[:, c, :], B[b][:, c % 2 * T:c % 2 * T + T], mod[:, gate + c:gate + c + 1], x[:, c, :], ALU.mult, ALU.add)
                    last.then_inc(x_ready, 1)

            gated_residual(4, res_ready, 16)
            norm_modulated(6, scale2, 24)
            for b in range(4):
                dve.wait_ge(tok_hi_ready, b + 1)
                part = (slice(None), b // 2, slice(b % 2 * 512, (b % 2 + 1) * 512))
                nc.vector.tensor_tensor(tok_lo[part], B[4 + b], tok_hi[part].bitcast(F32), ALU.subtract).then_inc(tok_lo_ready, 1)
            dve.wait_ge(scores_ready, 1)
            dve.wait_ge(router_loaded, 32)
            then(nc.vector.tensor_tensor(choice, score_e, rbias.unsqueeze(1).broadcast_to([P, TB, EXPERTS]), ALU.add))
            nc.vector.memset(gtop, 3e38)
            for tb in range(TB):
                for g in range(GROUPS):
                    last = nc.vector.max(grp8[:, tb, g, :], choice[:, tb, g * 8:(g + 1) * 8])
            then(last)
            then(nc.vector.tensor_tensor(gsum, grp8[:, :, :, 0], grp8[:, :, :, 1], ALU.add))
            for tb in range(TB):
                last = nc.vector.max(gwork[:, tb, :], gsum[:, tb, :])
            then(last)
            then(nc.vector.tensor_copy(gtop[:, :, 0:TOP_GROUPS], gwork[:, :, 0:TOP_GROUPS]))
            for tb in range(TB):
                last = nc.vector.match_replace(gwork[:, tb, :], gtop[:, tb, :], gsum[:, tb, :], TAKEN)
            then(last)
            then(nc.vector.tensor_scalar(gwork, gwork, TAKEN / 2, MASKED, ALU.is_gt, ALU.mult))
            by_group = lambda a: a.rearrange("p a (g e) -> p a g e", g=GROUPS)
            then(nc.vector.tensor_tensor(by_group(choice), by_group(choice), gwork.unsqueeze(3).broadcast_to([P, TB, GROUPS, 8]), ALU.add))
            for tb in range(TB):
                last = nc.vector.max(gtop[:, tb, :], choice[:, tb, :])
            then(last)
            for tb in range(TB):
                last = nc.vector.match_replace(cwork[:, tb, :], gtop[:, tb, :], choice[:, tb, :], TAKEN)
            then(last)
            nc.vector.tensor_scalar(mask_e, cwork, TAKEN / 2, None, ALU.is_lt).then_inc(mask_ready, 1)
            dve.wait_ge(mask_ready, 1)
            then(nc.vector.tensor_tensor(sel_e, mask_e, score_e, ALU.mult))
            then(nc.vector.tensor_reduce(den, sel_e, AX_X, ALU.add))
            then(nc.vector.reciprocal(den, den))
            for tb in range(TB):
                last = nc.vector.tensor_scalar(sel_e[:, tb, :], sel_e[:, tb, :], den[:, tb:tb + 1], ROUTED_SCALE, ALU.mult, ALU.mult)
            then(last)
            done = 2 * FFN_CHUNKS
            for f in range(2):
                dve.wait_ge(sig_ready, done + f + 1)
                then(nc.vector.tensor_tensor(gated[:, f, :], B[4 + f][:, 0:T], sig_f[:, f, :], ALU.mult))
                nc.vector.tensor_tensor(act_f[:, f, :], gated[:, f, :], B[4 + f][:, T:2 * T], ALU.mult).then_inc(act_ready, 1)
            dve.wait_ge(rank_ready, 1)
            nc.vector.scalar_tensor_tensor(rank_e, mask_e, -NOT_CHOSEN, B[6][:, 0:2 * EXPERTS].rearrange("p (a e) -> p a e", a=TB), ALU.mult, ALU.add).then_inc(gates_ready, 1)
            dve.wait_ge(gates_ready, 1)

            def build_pick(buf, e):
                by_token = rank_e[:, :, e] if isinstance(e, slice) else rank_e[:, :, bass.ds(e, 4)]
                slots = cst("slots").unsqueeze(1).unsqueeze(1).broadcast_to([P, TB, 4, CAP])
                dst = pick[buf].rearrange("p a (e s) -> p a e s", e=4)
                nc.vector.tensor_tensor(dst, slots, by_token.unsqueeze(3).broadcast_to([P, TB, 4, CAP]), ALU.is_equal).then_inc(pick_ready, 1)

            build_pick(0, slice(0, 4))
            then(nc.vector.scalar_tensor_tensor(mask_e, rank_e, CAP - NOT_CHOSEN, mask_e, ALU.is_ge, ALU.mult))
            nc.vector.tensor_tensor(dense_e, mask_e, sel_e, ALU.mult)
            nc.vector.tensor_reduce(beyond, mask_e.rearrange("p a e -> p (a e)"), AX_X, ALU.add).then_inc(beyond_ready, 1)
            dve.wait_ge(beyond_sum, 1)
            nc.vector.tensor_copy(flag, B[6][:, T:T + 1]).then_inc(flag_ready, 1)

            def two_quads(i, first=False, last=False):
                for k in range(4):
                    b = k % 2
                    dve.wait_ge(rows_landed[b], 64 * i + 32 * (k // 2 + 1))
                    if not (first and k < 2):
                        dve.wait_ge(pair_spread, 4 * i + (k - 1))
                    then_k(i, 2 * k, nc.vector.tensor_scalar(spread[b], rows_b[b][:, 0:T], cst("slot_of"), None, ALU.is_equal))
                    nc.vector.tensor_tensor_reduce(gate_tmp, spread[b].bitcast(F32), rows_b[b][:, T:2 * T], 1.0, 0.0, ALU.mult, ALU.add, slot_gate[b]).then_inc(rows_used, 1)
                    if k % 2 == 0 and not (last and k == 2):
                        if not (first and k == 0):
                            dve.wait_ge(gather_ready, 8 * i + 2 * k + 4)
                        build_pick((k // 2 + 1) % 2, 8 * i + (4 * (k // 2) + 4))
                    dve.wait_ge(pair_sig, 4 * i + (k + 1))
                    then_k(i, 2 * k + 1, nc.vector.tensor_tensor(gated_p, B[4][:, 0:T], sig_p, ALU.mult))
                    dve.wait_ge(rows_used, 4 * i + (k + 1))
                    nc.vector.scalar_tensor_tensor(act_p, gated_p, slot_gate[b], B[4][:, T:2 * T], ALU.mult, ALU.mult).then_inc(pair_act, 1)
                    for half in range(2):
                        dve.wait_ge(pair_hi, 8 * i + (2 * k + half + 1))
                        part = (slice(None), slice(half * 512, (half + 1) * 512))
                        ins = nc.vector.tensor_tensor(out_lo[part], B[6 + half], out_hi[part].bitcast(F32), ALU.subtract)
                    ins.then_inc(pair_lo, 1)

            base = steps[0]

            def then_k(i, n, ins):
                ins.then_inc(dve_step, 1)
                dve.wait_ge(dve_step, 8 * i + (base + n + 1))

            two_quads(0, first=True)
            with dve.Fori(1, QUADS // 2 - 1) as i:
                two_quads(i)
            two_quads(QUADS // 2 - 1, last=True)
            steps[0] += 2 * PAIRS
            dve.wait_ge(pair_spread, PAIRS)
            overflow = dve.value_load(flag[0:1, :])
            with dve.If(overflow > 0):
                with dve.Fori(0, EXPERTS // UNITS) as i:
                    for s in range(2 * UNITS):
                        gu = B[4 + s % 2]
                        dve.wait_ge(dense_sig, 2 * UNITS * i + (s + 1))
                        nc.vector.tensor_tensor(gated[:, s % 2, :], gu[:, 0:T], sig_f[:, s % 2, :], ALU.mult).then_inc(dense_step, 1)
                        dve.wait_ge(dense_step, 4 * UNITS * i + (2 * s + 1))
                        nc.vector.tensor_tensor(weighted[:, s % 2, :], gated[:, s % 2, :], gu[:, T:2 * T], ALU.mult).then_inc(dense_step, 1)
                        if s % 2 == 0:
                            dve.wait_ge(wb_landed[s // 2], 16 * i + 16)
                        dve.wait_ge(dense_step, 4 * UNITS * i + (2 * s + 2))
                        nc.vector.tensor_tensor(act_f[:, s % 2, :], weighted[:, s % 2, :], wb[:, s // 2, :], ALU.mult).then_inc(dense_act, 1)
                dve.wait_ge(unit_used, EXPERTS)
            gated_residual(None, None, 40)
            dve.wait_ge(rt_ready, 8)
            then(nc.vector.reciprocal(rinv[:], rt[:]))
            for c in range(KC):
                last = nc.vector.scalar_tensor_tensor(x[:, c, :], x[:, c, :], vcol("final_g", c), rinv[:], ALU.mult, ALU.mult)
            last.then_inc(out_ready, 1)


def tiles_of(w):
    k, n = w.shape
    return w.reshape(k // P, P, n // P, P).transpose(2, 1, 0, 3).reshape(n // P, P, k)


def slots_of(tiles):
    n = -(-len(tiles) // 3) * 3
    out = np.zeros((n, P, TILE), np.float32)
    for i, t in enumerate(tiles):
        out[i] = t
    return out.reshape(n // 3, 3, P, TILE).transpose(0, 2, 1, 3).reshape(n // 3, P, SLOT)


def ffn_slots(gate_up, down):
    g = tiles_of(gate_up)
    d = down.reshape(FFN_CHUNKS, P, D)
    return np.concatenate([g[:FFN_CHUNKS], g[FFN_CHUNKS:], d], 2)


def half_tiles(w):
    t = tiles_of(w)
    return t.reshape(4, 2, P, 512).transpose(0, 2, 1, 3).reshape(4, P, TILE)


def columns(v):
    return np.asarray(v).reshape(-1, P).T


def layout(i):
    i = {k: np.asarray(v) for k, v in i.items()}
    vecs = {"norm_mixer0": i["norm_mixer"][0], "norm_mixer1": i["norm_mixer"][1], "norm_ffn0": i["norm_ffn"][0],
            "norm_ffn1": i["norm_ffn"][1], "pool_scale": i["pool_scale"][0], "kv_norm": i["kv_norm"], "final_norm": i["final_norm"],
            "norm1_g": i["norm1_g_2"][0], "norm2_g": i["norm2_g_2"][0], "final_g": i["final_g_2"], "c": i["c_2"][0], "ada_b": i["ada_b_2"][0],
            "tshift_mu": i["tshift_mu_2"][0], "decay_w0": i["decay_w0_2"][0], "iclr_a0": i["iclr_a0_2"][0], "k_k": i["k_k_2"][0], "k_a": i["k_a_2"][0],
            "r_k": i["r_k_2"][0].reshape(-1), "lnx_g": i["lnx_g_2"][0], "lnx_b": i["lnx_b_2"][0]}
    w_kv, w_in = i["w_kv"], i["w_in_2"][0]
    kvq = [*tiles_of(w_kv[:, D:]), *tiles_of(w_kv[:, :D]), *tiles_of(i["w_q"][0])]
    ada = i["ada_w_2"][0].reshape(KC, P, 2, SLOT).transpose(0, 2, 1, 3).reshape(16, P, SLOT)
    a = ATTN_W
    o = 3 * a
    iq, ik, iw = w_in[:, o:o + 512], w_in[:, o + 512:o + 544], w_in[:, o + 544:o + 560]
    zr, ga, gr = w_in[:, o + 560:o + 560 + ZR * P], w_in[:, o + 560 + ZR * P:o + 560 + ZR * P + D], w_in[:, o + 560 + ZR * P + D:]
    zr = zr.reshape(D, ZR, P)[:, ZR_ORDER, :].reshape(D, ZR * P)
    iw_tile = np.concatenate([iw, np.zeros((D, P - IDX_HEADS), np.float32)], 1)
    win = np.concatenate([w_in[:, 2 * a:3 * a], iw_tile, w_in[:, 0:2 * a], iq, ik, ik, ik, ik, zr, ga, gr], 1)
    br = [*half_tiles(i["w_attn_br_2"][0]), *half_tiles(i["w_rwkv_br_2"][0]), *tiles_of(i["w_out_2"][0])]
    ws = np.concatenate([ffn_slots(i["w_gate_up"][0], i["w_down"][0]), slots_of(kvq), ada, slots_of(tiles_of(i["w_o"][0])), ffn_slots(i["w_gate_up"][1], i["w_down"][1]),
                         slots_of(tiles_of(win)), slots_of(br)], 0)
    rel = np.concatenate([np.concatenate([i["rel_bias"], i["rel_bias_2"]], 1), np.ones((1, HEADS_1 + HEADS_2), np.float32)], 0)
    lora = np.concatenate([np.concatenate([i["decay_up_2"][0], i["iclr_up_2"][0]], 0), i["gate_up_2"][0]], 1)
    gate = np.concatenate([i["sh_gate_2"], i["exp_gate_2"][0]], 0)
    up = np.concatenate([i["sh_up_2"], i["exp_up_2"][0]], 0)
    dn = np.concatenate([i["sh_down_2"], i["exp_down_2"][0]], 0)
    n = EXPERTS + 1
    gu = np.concatenate([gate.reshape(n, KC, P, EXPERT_FF), up.reshape(n, KC, P, EXPERT_FF)], 3).transpose(0, 2, 1, 3).reshape(n, P, KC * 2 * EXPERT_FF)
    experts = np.concatenate([gu, dn.reshape(n, 2, P, D).transpose(0, 2, 1, 3).reshape(n, P, 2 * D)], 2)
    return {
        "xT": i["x"][0].T.reshape(KC, P, T).transpose(1, 0, 2),
        "vec": np.concatenate([columns(vecs[name]) for name, _ in VEC_PARTS], 1),
        "consts": constants(),
        "selector": bias_selector(),
        "inv_count": pool_inverse_counts(),
        "pool_w": i["pool_w"][0].reshape(4, 2, P, 256).transpose(2, 0, 1, 3),
        "ws": ws,
        "rel": rel,
        "lora": lora,
        "router": i["router_w_2"][0].reshape(KC, P, EXPERTS).transpose(1, 0, 2),
        "router_bias": i["router_bias_2"],
        "experts": experts,
    }


def kernel(**inputs):
    import concourse.bacc as bacc
    from concourse.bass_utils import run_bass_kernel_spmd

    nc = bacc.Bacc("TRN2", target_bir_lowering=False, num_devices=1)
    arrays = {name: np.ascontiguousarray(a) for name, a in layout(inputs).items()}
    aps = {name: nc.dram_tensor(name, a.shape, F32, kind="ExternalInput").ap() for name, a in arrays.items()}
    aps["out"] = nc.dram_tensor("out", (P, KC, T), F32, kind="ExternalOutput").ap()
    build(nc, **aps)
    result = run_bass_kernel_spmd(nc, [arrays], core_ids=[0]).results[0]["out"]
    return np.ascontiguousarray(result.transpose(1, 0, 2).reshape(D, T).T)[None]
```

```python
import math
from contextlib import ExitStack

import numpy as np
import concourse.bass as bass
from concourse import mybir

F32 = mybir.dt.float32
BF16 = mybir.dt.bfloat16
F32R = mybir.dt.float32r
I32 = mybir.dt.int32
ALU = mybir.AluOpType
ACT = mybir.ActivationFunctionType
AX_X = mybir.AxisListType.X

P = 128
T = 256
TB = T // P
D = 1024
KC = D // P
D_FF = 2816
FFN_CHUNKS = D_FF // P
HEADS_1, HEADS_2, HEAD = 16, 8, 64
ATTN_W = HEADS_2 * HEAD
AC = ATTN_W // P
IDX_HEADS, IDX_DIM, TOP_KEYS = 16, 32, 64
BUCKETS, MAX_DISTANCE = 32, 128
WINDOWS = (2, 4, 8, 16)
PAD = 16
CH = 64
NCH = T // CH
ZR = 14
EXPERTS, GROUPS, TOP_GROUPS, MOE_TOPK, EXPERT_FF = 64, 8, 4, 8, 256
ROUTED_SCALE = 2.5
EPS, GN_EPS = 1e-6, 64e-5
SHIFTS = 32
MASKED = -1e30
TAKEN = -3e38

TILE = KC * P
SLOT = 3 * TILE
RING = 11
S_FFN1 = 0
S_KVQ = S_FFN1 + FFN_CHUNKS
S_ADA = S_KVQ + 8
S_O = S_ADA + 16
S_FFN2 = S_O + 3
S_WIN = S_FFN2 + FFN_CHUNKS
S_BR = S_WIN + 16
N_SLOTS = S_BR + 6
S_TURNS = S_WIN + RING - 1
PLACE = [n % RING for n in range(S_TURNS)] + [10, 0, 1, 2, 3, 10] + [10, 0, 1, 4, 2, 3]
LOADS = [PLACE[:n + 1].count(PLACE[n]) for n in range(N_SLOTS)]
TENANT = [max((m for m in range(n) if PLACE[m] == PLACE[n]), default=None) for n in range(N_SLOTS)]
ZR_ORDER = (12, 13, *range(12))
UNIT = KC * 2 * EXPERT_FF + 2 * D
GATE_UP = KC * 2 * EXPERT_FF
UNITS = 4
CAP = 64
PAIRS = EXPERTS // 2
QUADS = EXPERTS // 4
SHARED_GATE_UP = {0: {2: 0}, 1: {2: 1}}
SHARED_DOWN = {1: {0: 0}, QUADS // 2 - 1: {2: 1}}
NOT_CHOSEN = 1024

VEC_PARTS = [("norm_mixer0", 8), ("norm_mixer1", 8), ("norm_ffn0", 8), ("norm_ffn1", 8), ("pool_scale", 8),
             ("kv_norm", 8), ("final_norm", 8), ("norm1_g", 8), ("norm2_g", 8), ("final_g", 8), ("c", 8),
             ("ada_b", 48), ("tshift_mu", 14), ("decay_w0", 4), ("iclr_a0", 4), ("k_k", 4), ("k_a", 4),
             ("r_k", 4), ("lnx_g", 4), ("lnx_b", 4)]
VEC = {}
_n = 0
for _name, _w in VEC_PARTS:
    VEC[_name] = (_n, _n + _w)
    _n += _w
N_VEC = _n

LEVELS = [2, 4, 8, 16, 32]
CONST_PARTS = [("ident", 128), ("headones", 128), ("strict_t", 64), ("upto_t", 64), ("first", 64), ("first_t", 64),
               ("levels_t", 64 * len(LEVELS)), ("eye", 64), ("causal", 384),
               ("before", 128), ("slots", CAP), ("slot_of", 1)]
CONST = {}
_n = 0
for _name, _w in CONST_PARTS:
    CONST[_name] = (_n, _n + _w)
    _n += _w
N_CONST = _n


def constants():
    c = np.zeros((P, N_CONST), np.float32)

    def put(name, a):
        c[:, CONST[name][0]:CONST[name][1]] = a

    put("ident", np.eye(P))
    put("headones", np.kron(np.eye(2), np.ones((HEAD, HEAD))))
    s, t = np.meshgrid(np.arange(CH), np.arange(CH), indexing="ij")
    two = lambda m: np.concatenate([m, m], 0)
    put("strict_t", two(s < t))
    put("upto_t", two(s <= t))
    put("first", two((s // 2 == t // 2) & (s > t)))
    put("first_t", two((s // 2 == t // 2) & (s < t)))
    put("levels_t", np.concatenate([two((s // (2 * b) == t // (2 * b)) & (s // b % 2 == 0) & (t // b % 2 == 1)) for b in LEVELS], 1))
    put("eye", two(s == t))
    q = np.arange(P)[:, None]
    k = np.arange(T)[None, :]
    put("causal", np.concatenate([np.where(k <= q + P, 0.0, MASKED), np.where(k[:, :P] <= q, 0.0, MASKED)], 1))
    put("before", np.arange(P)[:, None] < np.arange(P)[None, :])
    put("slots", np.broadcast_to(np.arange(CAP) - NOT_CHOSEN, (P, CAP)))
    put("slot_of", (np.arange(P) % CAP - NOT_CHOSEN)[:, None])
    return c


def bias_selector():
    dist = 255 - np.arange(2 * T)
    n = np.maximum(dist, 0)
    half = BUCKETS // 2
    far = half + (np.log(np.maximum(n, half).astype(np.float32) / np.float32(half)) / np.float32(math.log(MAX_DISTANCE / half)) * half).astype(np.int32)
    bucket = np.where(n < half, n, np.minimum(far, BUCKETS - 1))
    m = np.zeros((BUCKETS + 1, 2 * T), np.float32)
    m[bucket, np.arange(2 * T)] = dist >= 0
    m[BUCKETS] = np.where(dist >= 0, 0.0, MASKED)
    return m


def pool_inverse_counts():
    t = np.arange(T)
    rows = [1.0 / np.minimum(t + 1, w).astype(np.float32) for w in WINDOWS]
    return np.broadcast_to(np.stack(rows).astype(np.float32)[None], (P, 4, T)).copy()


def build(nc, xT, vec, consts, selector, inv_count, pool_w, ws, rel, lora, router, router_bias, experts, out):
    bias_line = nc.dram_tensor("bias_line", (HEADS_1 + HEADS_2, SHIFTS, 2 * T), F32, kind="Internal").ap()
    dense_rows = nc.dram_tensor("dense_rows", (EXPERTS, T), F32, kind="Internal").ap()

    with ExitStack() as ctx:
        def sb(name, shape, dt=F32):
            return ctx.enter_context(nc.sbuf_tensor(name, shape, dt))

        def sem(name):
            return ctx.enter_context(nc.semaphore(name))

        ring_at = -(-nc.sbuf_base // 32) * 32
        ring = sb("ring", [P, RING * SLOT])
        scr_at = -(-nc.sbuf_base // 32) * 32
        scr = sb("scr", [P, 14600])
        x = sb("x", [P, KC, T])
        vecs = sb("vecs", [P, N_VEC])
        con = sb("con", [P, N_CONST])
        ones = sb("ones", [P, P])
        zeros = sb("zeros", [P, 512], BF16)
        rt = sb("rt", [P, T])
        rinv = sb("rinv", [P, T])
        small = sb("small", [P, 64])
        mod = sb("mod", [P, 48])
        scale1 = sb("scale1", [P, KC])
        scale2 = sb("scale2", [P, KC])
        relw = sb("relw", [BUCKETS + 1, HEADS_1 + HEADS_2])
        banks = ctx.enter_context(nc.psum_tensor("banks", [P, 8, 512], F32))
        B = [banks[:, i, :] for i in range(8)]

        def view(lo, *dims, base=scr):
            n = int(np.prod(dims))
            v = base[:, lo:lo + n]
            if len(dims) == 2:
                return v.rearrange("p (a b) -> p a b", a=dims[0])
            if len(dims) == 3:
                return v.rearrange("p (a b c) -> p a b c", a=dims[0], b=dims[1])
            return v

        def rounded(name, at, cols):
            return nc.alloc_sbuf_tensor_at(name, [P, cols], F32R, offset=at)[:]

        def slot(n):
            return ring[:, PLACE[n] * SLOT:(PLACE[n] + 1) * SLOT]

        def vcol(name, c):
            return vecs[:, VEC[name][0] + c:VEC[name][0] + c + 1]

        def cst(name):
            return con[:, CONST[name][0]:CONST[name][1]]

        ident = cst("ident")
        headones = cst("headones")
        eps, gn_eps = small[:, 0:1], small[:, 1:2]

        h = view(0, KC, T)
        sq = view(2048, KC, T)
        hp, pw_b, pw_c = view(4352, KC, PAD + T), view(6528, KC, PAD + T), view(8704, KC, PAD + T)
        icnt, poolw = view(10880, 4, T), view(11904, 4, 2, T)
        sig_f, gated, act_f = view(4352, 2, T), view(4864, 2, T), view(5376, 2, T)
        h_hi = rounded("h_hi", scr_at + 4 * 5888, KC * T).rearrange("p (c t) -> p c t", c=KC)
        h_lo = rounded("h_lo", scr_at + 4 * 2048, KC * T).rearrange("p (c t) -> p c t", c=KC)
        gu_hi = [rounded(f"gu_hi{q}", scr_at + 4 * (7936 + 2 * TILE * q), 2 * TILE) for q in range(2)]
        down_hi = [rounded(f"down_hi{q}", scr_at + 4 * (12032 + TILE * q), TILE) for q in range(2)]
        act_hi = [rounded(f"act_hi{q}", scr_at + 4 * (14080 + T * q), T) for q in range(2)]
        act_lo = [rounded(f"act_lo{q}", scr_at + 4 * (4096 + T * q), T) for q in range(1)] + [rounded("act_lo1", scr_at + 4 * 5632, T)]
        slot_lo = [rounded(f"slot_lo{q}", ring_at + 4 * SLOT * q, SLOT) for q in range(RING)]
        hq = sq
        ex, pts = view(2048, 3, 384), view(3200, 2, 384)
        nmax, rsum, rrec = small[:, 2:8], small[:, 8:14], small[:, 14:20]
        q1, k1, v1, bias1 = view(4352, KC, T), view(6400, KC, T), view(8448, TB, D), view(10496, HEADS_1, T)
        kv_hi = rounded("kv_hi", scr_at + 4 * 4352, KC * T).rearrange("p (c t) -> p c t", c=KC)
        kv_lo = rounded("kv_lo", scr_at, KC * T).rearrange("p (c t) -> p c t", c=KC)
        hq_hi = slot_lo[PLACE[S_KVQ + 1]][:, 0:KC * T].rearrange("p (c t) -> p c t", c=KC)
        hq_lo = h_lo
        v_hi = [rounded(f"v_hi{q}", scr_at + 4 * at, 2 * TILE) for q, at in enumerate((6400, 10496))]
        v_lo = [rounded(f"v_lo{g}", ring_at + 4 * (SLOT * PLACE[S_KVQ] + 2 * TILE * g), 2 * TILE) for g in range(KC // 2)]
        kq_hi = [slot_lo[PLACE[S_KVQ]][:, q * TILE:(q + 1) * TILE] for q in range(3)]
        csil, csig = small[:, 20:28], small[:, 28:36]
        modrow = view(12032, 3, 512)
        line_sb, sel_sb = view(13952, 2 * T), view(0, 2 * T)
        q2, k2, v2, iqT = view(2048, AC, T), view(3072, AC, T), view(4096, TB, ATTN_W), view(5120, AC, T)
        ikr, iw = view(6144, T), view(6400, TB, IDX_HEADS)
        zr = view(6432, ZR, T + 1)
        sig_a, sig_r = view(10032, KC, T), view(12080, KC, T)
        o2, rw = view(0, AC, T), view(1024, AC, T)
        in_hi = slot_lo[4][:, 0:KC * T].rearrange("p (c t) -> p c t", c=KC)
        in_lo = kv_lo
        win_hi = [rounded(f"win_hi{q}", scr_at + 4 * (10032 + TILE * q), TILE) for q in range(4)]
        win_hi3 = rounded("win_hi_three", scr_at + 4 * 10032, 3 * TILE)
        win_hi2 = rounded("win_hi_two", scr_at + 4 * 2048, 2 * TILE)
        win_late = [slot_lo[4][:, 2 * TILE:], rounded("win_late1", scr_at + 4 * 5120, TILE)]
        win_late += [rounded(f"win_late{q}", ring_at + 4 * (5 * SLOT + 8704 + TILE * (q - 2)), TILE) for q in (2, 3)]

        def spare(lo, *dims):
            return view(5 * SLOT + lo, *dims, base=ring)

        bias2, relu_i, mask2 = spare(4608, HEADS_2, T), spare(8704, 8, T), spare(11776, 384)
        work, top8 = view(14128, 384), view(14512, 2, 8)
        ex2, pts2 = spare(8704, 3, 384), spare(9856, 2, 384)
        zs = spare(0, ZR, T)
        r_t, k_t, v_t, lo_t = zs[:, 0:4, :], zs[:, 4:8, :], zs[:, 8:12, :], zs[:, 12:14, :]
        b5, b3, b4, b1, b2, b6 = (spare(at, AC, T) for at in (3584, 6656, 7680, 12288, 13312, 14336))
        m_ab, m_lev = spare(4608, NCH * AC, CH), spare(5632, NCH * AC, CH)
        vt, bt, kt = (spare(8704 + 1024 * i, NCH * AC, CH) for i in range(3))
        loraw = spare(10752, 2 * ATTN_W)
        m_ak, m_rb, m_rk, inv = (view(2048 + 1024 * i, NCH * AC, CH) for i in range(4))
        f0, f1 = (view(2048 + 1024 * i, AC, T) for i in range(2))
        inv_t, xm = view(6432, NCH * AC, CH), view(7456, NCH * AC, CH)
        gst, rhs_u, u_sb = view(8480, 2, AC, CH), view(8992, AC, CH), view(9248, AC, CH)
        p_end = small[:, 40:56].rearrange("p (a b) -> p a b", a=AC)
        mixed, mixed_r = sig_a, sig_r
        o2_hi = rounded("o2_hi", scr_at + 4 * 8480, AC * T)
        rw_hi = rounded("rw_hi", scr_at + 4 * 2048, AC * T)
        o2_lo, rw_lo = rounded("o2_lo", scr_at, AC * T), rounded("rw_lo", scr_at + 4 * 1024, AC * T)
        mixed_hi = rounded("mixed_hi", scr_at + 4 * 6432, KC * T).rearrange("p (c t) -> p c t", c=KC)
        mixed_lo = rounded("mixed_lo", scr_at + 4 * 10032, KC * T).rearrange("p (c t) -> p c t", c=KC)
        br_places = [rounded(f"br_hi{q}", scr_at + 4 * at, TILE) for q, at in enumerate((5120, 7456, 4096, 6432))] + [o2_hi]
        BR_HI = [br_places[q] for q in (0, 1, 2, 3) + (0, 2, 4) * 4]
        score_e, choice, grp8, gsum, gtop, gwork, cwork, sel_e, den = (
            view(6432, TB, EXPERTS), view(6560, TB, EXPERTS), view(6688, TB, GROUPS, 8), view(6816, TB, GROUPS), view(6832, TB, 8),
            view(6848, TB, GROUPS), view(6864, TB, EXPERTS), view(6992, TB, EXPERTS), view(7120, TB))
        mask_e, rank_e, dense_e = view(7122, TB, EXPERTS), view(7250, TB, EXPERTS), view(7378, TB, EXPERTS)
        routerw, rbias = view(12080, KC, EXPERTS), view(12592, EXPERTS)
        beyond, flag = small[:, 58:59], small[:, 59:60].bitcast(I32)

        def unit(u):
            lo = (7, 9, 0, 2)[u] * SLOT
            return ring[:, lo:lo + UNIT]

        SHARED_UNIT = ring[:, 5 * SLOT:7 * SLOT]
        tok_hi = rounded("tok_hi", scr_at + 4 * 2048, TB * D).rearrange("p (a b) -> p a b", a=TB)
        tok_lo = rounded("tok_lo", ring_at + 4 * 4 * SLOT, TB * D).rearrange("p (a b) -> p a b", a=TB)
        dense_t = view(4 * SLOT + 2048, T, base=ring)
        gathered_h = [view(7506 + 2048 * q, KC, 4 * CAP) for q in range(2)]
        pick = [rounded(f"pick{q}", scr_at + 4 * (11608 + 512 * q), TB * 4 * CAP).rearrange("p (a b) -> p a b", a=TB) for q in range(2)]
        spread = [rounded(f"spread{q}", scr_at + 4 * (13656 + T * q), T) for q in range(2)]
        ident_r = rounded("ident_r", scr_at + 4 * 14168, P)
        gate_hi, gate_lo = (rounded(n, scr_at + 4 * at, TB * EXPERTS).rearrange("p (a e) -> p a e", a=TB) for n, at in (("gate_hi", 14296), ("gate_lo", 14424)))
        slot_gate = [small[:, 56 + q:57 + q] for q in range(2)]
        sig_p, gated_p, act_p, act_pt = view(4352, T), view(4608, T), view(4864, T), view(5120, 2, P)
        out_hi = rounded("out_hi", scr_at + 4 * 5376, D)
        out_lo = rounded("out_lo", scr_at + 4 * 12632, D)
        sig_s, act_s = view(6432, T), view(6688, T)
        wb = view(5 * SLOT, UNITS, T, base=ring)
        weighted = view(9216, 2, T)

        landed = [sem(f"weights_landed{i}") for i in range(RING)]
        w_used = sem("weights_used")
        x_loaded, vec_loaded, const_loaded, sel_loaded, pool_loaded = (sem(s) for s in ("x_loaded", "vec_loaded", "const_loaded", "sel_loaded", "pool_loaded"))
        sq_ready, ss_ready, rt_ready, h_ready, x_ready = (sem(s) for s in ("sq_ready", "ss_ready", "rt_ready", "h_ready", "x_ready"))
        ones_ready, line_ready, line_copied, line_stored, bias_loaded = (sem(s) for s in ("ones_ready", "line_ready", "line_copied", "line_stored", "bias_loaded"))
        pool_d, pool_y = sem("pool_d"), sem("pool_y")
        gu_ready, sig_ready, act_ready = sem("gu_ready"), sem("sig_ready"), sem("act_ready")
        proj_ready, proj_used, res_ready = sem("proj_ready"), sem("proj_used"), sem("res_ready")
        s_ready, s_used, max_ready, exp_ready, p_ready, pt_ready, pts_ready, o_ready, o_copied = (
            sem(s) for s in ("s_ready", "s_used", "max_ready", "exp_ready", "p_ready", "pt_ready", "pts_ready", "o_ready", "o_copied"))
        csig_ready, csil_ready, mod_copied, mod_turned, mod_ready = (
            sem(s) for s in ("csig_ready", "csil_ready", "mod_copied", "mod_turned", "mod_ready"))
        out_ready, out_done = sem("out_ready"), sem("out_done")
        bias2_loaded, lora_loaded, router_loaded = sem("bias2_loaded"), sem("lora_loaded"), sem("router_loaded")
        idx_ready, relu_ready, relu_used = sem("idx_ready"), sem("relu_ready"), sem("relu_used")
        shifted, lora_in, lora_out, decay_ready, iclr_ready = (
            sem(n) for n in ("shifted", "lora_in", "lora_out", "decay_ready", "iclr_ready"))
        kk_sq, kk_sum, kk_norm, bonus_in, bonus_sum, bonus_used = (sem(n) for n in ("kk_sq", "kk_sum", "kk_norm", "bonus_in", "bonus_sum", "bonus_used"))
        tilde_ready, turned, turned_used = (sem(n) for n in ("tilde_ready", "turned", "turned_used"))
        pair_ready, pair_used, level_m, level_x, x_copied, level_d, inv_ready = (
            sem(n) for n in ("pair_ready", "pair_used", "level_m", "level_x", "x_copied", "level_d", "inv_ready"))
        rhs_ready, rhs_copied, u_ready, u_copied, g_ready, state_ready, y_ready, y_copied = (
            sem(n) for n in ("rhs_ready", "rhs_copied", "u_ready", "u_copied", "g_ready", "state_ready", "y_ready", "y_copied"))
        gn_sum, gn_sq, gn_var, gn_rt, rw_ready = (sem(n) for n in ("gn_sum", "gn_sq", "gn_var", "gn_rt", "rw_ready"))
        br_ready, mixed_ready = sem("br_ready"), sem("mixed_ready")
        logits_ready, scores_ready, gates_ready, gates_turned, gates_copied, gates_stored = (
            sem(n) for n in ("logits_ready", "scores_ready", "gates_ready", "gates_turned", "gates_copied", "gates_stored"))
        shared_landed, shared_gated, tok_turned, tok_hi_ready, tok_lo_ready = (sem(n) for n in ("shared_landed", "shared_gated", "tok_turned", "tok_hi_ready", "tok_lo_ready"))
        mask_ready, rank_ready, beyond_ready, beyond_sum, flag_ready = (sem(n) for n in ("mask_ready", "rank_ready", "beyond_ready", "beyond_sum", "flag_ready"))
        gu_landed, down_landed = [sem(f"gu_landed{u}") for u in range(UNITS)], [sem(f"down_landed{u}") for u in range(UNITS)]
        pick_turned, spread_ready = sem("pick_turned"), sem("spread_ready")
        pick_ready, gather_ready, gather_copied = sem("pick_ready"), sem("gather_ready"), sem("gather_copied")
        pair_gu, pair_sig, pair_act, pair_turned, pair_act_t, pair_down, pair_hi, pair_lo, pair_spread = (
            sem(n) for n in ("pair_gu", "pair_sig", "pair_act", "pair_turned", "pair_act_t", "pair_down", "pair_hi", "pair_lo", "pair_spread"))
        unit_landed, wb_landed = [sem(f"unit_landed{u}") for u in range(UNITS)], [sem(f"wb_landed{u}") for u in range(UNITS)]
        unit_used, dense_gu, dense_sig, dense_step, dense_act = (sem(n) for n in ("unit_used", "dense_gu", "dense_sig", "dense_step", "dense_act"))
        h_hi_ready, h_lo_ready = sem("h_hi_ready"), sem("h_lo_ready")
        kvq_w_hi, kvq_w_lo, win_w_hi, win_w_lo = (sem(n) for n in ("kvq_weights_hi", "kvq_weights_lo", "win_weights_hi", "win_weights_lo"))
        gu_hi_ready, gu_lo_ready, down_hi_ready, down_lo_ready = (sem(n) for n in ("gu_hi_ready", "gu_lo_ready", "down_hi_ready", "down_lo_ready"))
        dve_step, act_step = sem("dve_step"), sem("act_step")
        block = ctx.enter_context(nc.Block())

        LHALF = NCH * AC // 2

        def level_bank(b0, half, col):
            return banks[:, b0 + 2 * half:b0 + 2 * half + 2, col:col + LHALF // 2 * CH].rearrange("p a (j t) -> p a j t", t=CH)

        def level_half(a, half):
            return a[:, half * LHALF:(half + 1) * LHALF, :].rearrange("p (j a) t -> p a j t", a=2)

        def four_heads(b0):
            return banks[:, b0:b0 + 2, 0:2 * CH].rearrange("p a (b t) -> p a b t", t=CH)

        def by_bank(a):
            return a.rearrange("p (a b) t -> p a b t", a=2)

        H_BASE = [0, 8, 16, 32, 40, 40, 48, 56]
        H_PARTS = {1: 0, 3: 3 * KC}
        KV_PARTS, HQ_PARTS, IN_PARTS = KC, 2 * KC, 4 * KC
        O2_PARTS, RW_PARTS, MIXED_PARTS = 5 * KC, 5 * KC + AC, 6 * KC

        PROJ_BANKS = [B[4], B[5], B[7]]
        U_V1, U_K1, U_Q1 = 0, 8, 16
        U_Z = 24
        def win_group(i):
            return 2 + i - 5

        BR_GROUP = win_group(48)

        def win_hi_of(i):
            return (win_hi if i < 32 else win_late)[i % 4]

        def win_tile(i):
            return PLACE[S_WIN + i // 3], slice(i % 3 * TILE, (i % 3 + 1) * TILE)

        IDX_AT, LO_AT, LORA_AT, DECAY_AT, KK_AT, KK_SQRT_AT, BONUS_AT = (18, 21, 24, 27), 30, 31, 33, 36, 37, 40
        V_PAIRS = KC // 2
        KQ_TILES = 2 * KC

        def load_toeplitz(eng, dst, first, heads, signal):
            for a in range(P // SHIFTS):
                start = first * SHIFTS * 2 * T + P - 1 - SHIFTS * a
                src = bass.AP(bias_line.tensor, start, [[2 * T - 1, SHIFTS], [SHIFTS * 2 * T, heads], [1, T]])
                eng.dma_start(dst[SHIFTS * a:SHIFTS * (a + 1)], src).then_inc(signal, 16)

        @block.sync
        def _(sp):
            sp.dma_start(sel_sb[0:BUCKETS + 1, :], selector).then_inc(sel_loaded, 16)
            sp.dma_start(relw[:], rel).then_inc(sel_loaded, 16)
            sp.dma_start(x[:], xT).then_inc(x_loaded, 16)
            sp.dma_start(vecs[:], vec).then_inc(vec_loaded, 16)
            sp.dma_start(icnt, inv_count).then_inc(pool_loaded, 16)
            sp.dma_start(poolw, pool_w).then_inc(pool_loaded, 16)

            def load(n):
                sp.dma_start(slot(n), ws[n]).then_inc(landed[PLACE[n]], 16)

            for n in range(RING):
                if n == 2:
                    sp.wait_ge(line_copied, 1)
                    heads = HEADS_1 + HEADS_2
                    sp.dma_start(bias_line, line_sb[0:heads, :].unsqueeze(1).broadcast_to([heads, SHIFTS, 2 * T])).then_inc(line_stored, 16)
                    sp.dma_start(con[:], consts).then_inc(const_loaded, 16)
                load(n)
            with sp.Fori(1, S_TURNS // RING) as i:
                for s in range(RING):
                    sp.wait_ge(w_used, RING * i + (s + 1 - RING))
                    sp.dma_start(slot(s), ws[RING * i + s]).then_inc(landed[s], 16)
            for n in range(S_TURNS // RING * RING, N_SLOTS):
                sp.wait_ge(w_used, TENANT[n] + 1)
                load(n)
                if n == S_WIN + 10:
                    load_toeplitz(sp, bias2, HEADS_1, HEADS_2, bias2_loaded)
                    sp.dma_start(loraw, lora).then_inc(lora_loaded, 16)
            def load_gate_up(u, e):
                sp.dma_start(unit(u)[:, 0:GATE_UP], experts[e, :, 0:GATE_UP]).then_inc(gu_landed[u], 16)

            def load_down(u, e):
                sp.dma_start(unit(u)[:, GATE_UP:], experts[e, :, GATE_UP:]).then_inc(down_landed[u], 16)

            sp.wait_ge(inv_ready, 1)
            sp.dma_start(SHARED_UNIT, experts[0]).then_inc(shared_landed, 16)
            for u, (done, count) in enumerate(((y_ready, NCH), (br_ready, 3), (res_ready, 4 + 2), (res_ready, 4 + KC))):
                if u == 1:
                    sp.wait_ge(rw_ready, 1)
                sp.wait_ge(done, count)
                load_gate_up(u, 1 + u)
                load_down(u, 1 + u)
            with sp.Fori(1, QUADS) as i:
                for k in range(2):
                    sp.wait_ge(pair_gu, 2 * i + (k - 1))
                    for u in (2 * k, 2 * k + 1):
                        load_gate_up(u, 4 * i + (1 + u))
                    sp.wait_ge(pair_down, 4 * i + 2 * (k - 1))
                    for u in (2 * k, 2 * k + 1):
                        load_down(u, 4 * i + (1 + u))
            sp.wait_ge(flag_ready, 1)
            overflow = sp.value_load(flag[0:1, :])
            with sp.If(overflow > 0):
                sp.wait_ge(pair_spread, PAIRS)
                for u in range(UNITS):
                    sp.dma_start(unit(u), experts[1 + u]).then_inc(unit_landed[u], 16)
                with sp.Fori(1, EXPERTS // UNITS) as i:
                    for u in range(UNITS):
                        sp.wait_ge(unit_used, UNITS * i + (u + 1 - UNITS))
                        sp.dma_start(unit(u), experts[UNITS * i + (1 + u)]).then_inc(unit_landed[u], 16)
            for b in range(4):
                sp.wait_ge(out_ready, b + 1)
                sp.dma_start(out[:, 2 * b:2 * b + 2, :], x[:, 2 * b:2 * b + 2, :]).then_inc(out_done, 16)
            sp.wait_ge(out_done, 64)

        @block.gpsimd
        def _(pool):
            pool.wait_ge(line_stored, 16)
            pool.wait_ge(proj_ready, U_K1)
            load_toeplitz(pool, bias1, 0, HEADS_1, bias_loaded)
            def second_part(n, dst, src, hi):
                pool.wait_ge(win_w_hi, n + 1)
                nc.gpsimd.tensor_tensor(dst, src, hi.bitcast(F32), ALU.subtract).then_inc(win_w_lo, 1)

            second_part(0, slot_lo[PLACE[S_WIN]], slot(S_WIN), win_hi3)
            second_part(1, slot_lo[PLACE[S_WIN + 1]][:, 0:2 * TILE], slot(S_WIN + 1)[:, 0:2 * TILE], win_hi2)
            for i in range(5, 48):
                place, cols = win_tile(i)
                second_part(win_group(i), slot_lo[place][:, cols], slot(S_WIN + i // 3)[:, cols], win_hi_of(i))
            for k in range(16):
                cols = slice(k % 3 * TILE, (k % 3 + 1) * TILE)
                if k == 2:
                    pool.wait_ge(h_hi_ready, (O2_PARTS + AC) // 2)
                    flat = o2.rearrange("p a t -> p (a t)")
                    nc.gpsimd.tensor_tensor(o2_lo, flat, o2_hi.bitcast(F32), ALU.subtract).then_inc(h_lo_ready, AC)
                second_part(BR_GROUP + k, slot_lo[PLACE[S_BR + k // 3]][:, cols], slot(S_BR + k // 3)[:, cols], BR_HI[k])
            pool.wait_ge(mixed_ready, 4)
            pool.dma_start(routerw, router).then_inc(router_loaded, 16)
            pool.dma_start(rbias, router_bias.partition_broadcast(P)).then_inc(router_loaded, 16)
            pool.wait_ge(gates_copied, 1)
            pool.dma_start(dense_rows, dense_t[0:EXPERTS, :]).then_inc(gates_stored, 16)
            pool.wait_ge(gates_stored, 16)
            pool.wait_ge(flag_ready, 1)
            overflow = pool.value_load(flag[0:1, :])
            with pool.If(overflow > 0):
                pool.wait_ge(pair_spread, PAIRS)
                for u in range(UNITS):
                    pool.dma_start(wb[:, u, :], dense_rows[u:u + 1, :].partition_broadcast(P)).then_inc(wb_landed[u], 16)
                with pool.Fori(1, EXPERTS // UNITS) as i:
                    for u in range(UNITS):
                        pool.wait_ge(unit_used, UNITS * i + (u + 1 - UNITS))
                        pool.dma_start(wb[:, u, :], dense_rows[bass.ds(UNITS * i + u, 1), :].partition_broadcast(P)).then_inc(wb_landed[u], 16)

        @block.tensor
        def _(pe):
            def wait_slot(n):
                pe.wait_ge(landed[PLACE[n]], 16 * LOADS[n])

            def norm_sum(k):
                for g in range(4):
                    pe.wait_ge(sq_ready, 4 * k + g + 1)
                    for c in (2 * g, 2 * g + 1):
                        mm = nc.tensor.matmul(B[6][:, 0:T], ones[:], sq[:, c, :], start=(c == 0), stop=(c == KC - 1))
                mm.then_inc(ss_ready, 1)

            def clear_y():
                for b in range(4):
                    nc.tensor.matmul(B[b], zeros[:, 0:P], zeros[:], start=True, stop=False, skip_group_check=True)

            def gate_up(bank, gate, up, signal=gu_ready):
                for half, w in ((0, gate), (T, up)):
                    for c in range(KC):
                        mm = nc.tensor.matmul(bank[:, half:half + T], w(c), h[:, c, :], start=(c == 0), stop=(c == KC - 1))
                mm.then_inc(signal, 1)

            def down(w, a):
                for c in range(KC):
                    mm = nc.tensor.matmul(B[c // 2][:, c % 2 * T:c % 2 * T + T], w(c), a, start=False, stop=False, skip_group_check=True)
                return mm

            def three(out, hi, lo, move_hi, move_lo, start, stop):
                nc.tensor.matmul(out, hi, move_hi, start=start, stop=False, skip_group_check=True)
                nc.tensor.matmul(out, hi, move_lo, start=False, stop=False, skip_group_check=True)
                return nc.tensor.matmul(out, lo, move_hi, start=False, stop=stop, skip_group_check=True)

            def ffn(base, k, done):
                clear_y()
                with pe.Fori(0, 2) as i:
                    for s in range(RING + 1):
                        if s < RING:
                            w, lo, bank = gu_hi[s % 2], slot_lo[PLACE[base + s]], B[4 + s % 2]
                            pe.wait_ge(gu_lo_ready, RING * i + (done + s + 1))
                            for half in range(2):
                                for c in range(KC):
                                    part = slice(half * TILE + c * P, half * TILE + (c + 1) * P)
                                    if s == 0 and half == 0:
                                        pe.wait_ge(h_lo_ready, H_PARTS[k] + c + 1)
                                    mm = three(bank[:, half * T:(half + 1) * T], w[:, part], lo[:, part], h_hi[:, c, :], h_lo[:, c, :], c == 0, c == KC - 1)
                            mm.then_inc(gu_ready, 1)
                        if s >= 1:
                            a = (s - 1) % 2
                            w, lo = down_hi[a], slot_lo[PLACE[base + s - 1]][:, 2 * TILE:]
                            pe.wait_ge(act_ready, RING * i + (done + s))
                            pe.wait_ge(down_lo_ready, RING * i + (done + s))
                            for c in range(KC):
                                part = slice(c * P, (c + 1) * P)
                                mm = three(B[c // 2][:, c % 2 * T:c % 2 * T + T], w[:, part], lo[:, part], act_hi[a], act_lo[a], False, False)
                            mm.then_inc(w_used, 1)

            def tile_w(base, i):
                return slot(base + i // 3)[:, i % 3 * TILE:(i % 3 + 1) * TILE]

            def attention(heads, n0, qT, kT, v, ex, pts, o_banks, between=None):
                for j in range(heads + 3):
                    if j < heads:
                        r, b = j % 2 * HEAD, B[j % 2]
                        if n0 + j >= 2:
                            pe.wait_ge(s_used, n0 + j - 1)
                        lo = slice(r, r + HEAD)
                        nc.tensor.matmul(b[:, 0:T], qT[lo, j // 2, P:T], kT[lo, j // 2, :], start=True, stop=True)
                        nc.tensor.matmul(b[:, T:T + P], qT[lo, j // 2, 0:P], kT[lo, j // 2, 0:P], start=True, stop=True).then_inc(s_ready, 1)
                    if 2 <= j <= heads + 1:
                        a = j - 2
                        pe.wait_ge(p_ready, n0 + a + 1)
                        b, e = B[2 + a % 2], ex[:, a % 3, :]
                        for d, s in ((0, T), (P, 0), (2 * P, P)):
                            mm = nc.tensor.transpose(b[:, d:d + P], e[:, s:s + P], ident)
                        mm.then_inc(pt_ready, 1)
                    if between is not None and j < heads:
                        between(j)
                    if j >= 3:
                        a = j - 3
                        pe.wait_ge(pts_ready, n0 + a + 1)
                        r, b, pt = a % 2 * HEAD, o_banks[a // 2 % len(o_banks)], pts[:, a % 2, :]
                        if a % 2 == 0 and (n0 + a) // 2 >= len(o_banks):
                            pe.wait_ge(o_copied, (n0 + a) // 2 - len(o_banks) + 1)
                        nc.tensor.matmul(b[r:r + HEAD, 0:T], v[:, 0, a * HEAD:(a + 1) * HEAD], pt[:, 0:T], start=True, stop=False, skip_group_check=True)
                        nc.tensor.matmul(b[r:r + HEAD, P:T], v[:, 1, a * HEAD:(a + 1) * HEAD], pt[:, T:T + P], start=False, stop=True, skip_group_check=True).then_inc(o_ready, 1)

            pe.wait_ge(ones_ready, 1)
            pe.wait_ge(sel_loaded, 32)
            nc.tensor.matmul(B[7][0:HEADS_1 + HEADS_2, :], relw[:], sel_sb[0:BUCKETS + 1, :], start=True, stop=True).then_inc(line_ready, 1)

            norm_sum(0)
            pe.wait_ge(pool_loaded, 32)
            for g in range(4):
                pe.wait_ge(pool_d, g + 1)
                for e in range(2):
                    for c in range(2):
                        mm = nc.tensor.matmul(B[g][:, e * T:(e + 1) * T], poolw[:, g, c, e * P:(e + 1) * P], h[:, 2 * g + c, :], start=(c == 0), stop=(c == 1))
                mm.then_inc(pool_y, 1)
            norm_sum(1)
            ffn(S_FFN1, 1, 0)
            def modulation(n):
                wait_slot(S_ADA + n)
                w = slot(S_ADA + n)
                for b in range(6):
                    c, j = divmod(6 * n + b, 12)
                    r = 32 * (j % 4)
                    mm = nc.tensor.matmul(B[5 + j // 4][r:r + 1, :], csil[:, c:c + 1], w[:, b * 512:(b + 1) * 512], start=(c == 0), stop=(c == KC - 1),
                                          skip_group_check=True, tile_position=(0, r))
                mm.then_inc(w_used, 1)

            pe.wait_ge(const_loaded, 16)
            norm_sum(2)
            def proj_three(u, stationary, moving, ready=None, n=T):
                bank = PROJ_BANKS[u % 3]
                if u >= 3:
                    pe.wait_ge(proj_used, u - 2)
                for c in range(KC):
                    if ready is not None:
                        pe.wait_ge(h_lo_ready, ready + c + 1)
                    mm = three(bank[:, 0:n], *stationary(c), *moving(c), c == 0, c == KC - 1)
                mm.then_inc(proj_ready, 1)

            for g in range(V_PAIRS):
                pe.wait_ge(kvq_w_lo, g + 1)
                w_hi, w_lo = (w.rearrange("p (t c m) -> p t c m", t=2, c=KC) for w in (v_hi[g % 2], v_lo[g]))
                for tb in range(TB):
                    tokens = slice(tb * P, (tb + 1) * P)
                    proj_three(U_V1 + 2 * g + tb, lambda c: (kv_hi[:, c, tokens], kv_lo[:, c, tokens]), lambda c: (w_hi[:, :, c, :], w_lo[:, :, c, :]),
                               KV_PARTS if g == tb == 0 else None)
            for n in range(KQ_TILES):
                pe.wait_ge(kvq_w_lo, V_PAIRS + n + 1)
                i = KC + n
                w_hi, w_lo = kq_hi[n % 3], slot_lo[PLACE[S_KVQ + i // 3]][:, i % 3 * TILE:(i % 3 + 1) * TILE]
                of_hi, of_lo = (kv_hi, kv_lo) if n < KC else (hq_hi, hq_lo)
                proj_three(U_K1 + n, lambda c: (w_hi[:, c * P:(c + 1) * P], w_lo[:, c * P:(c + 1) * P]), lambda c: (of_hi[:, c, :], of_lo[:, c, :]),
                           HQ_PARTS if n == KC else None)
            pe.wait_ge(proj_ready, U_Z)
            pe.sem_inc(w_used, 8)
            pe.wait_ge(proj_used, U_Z)
            pe.wait_ge(csil_ready, 1)
            attention(HEADS_1, 0, q1, k1, v1, ex, pts, B[4:5], between=modulation)
            pe.wait_ge(o_copied, HEADS_1 // 2)
            for i in range(24, 32):
                dc = i - 24
                wait_slot(S_O + dc // 3)
                w = tile_w(S_O, dc)
                for c in range(KC):
                    mm = nc.tensor.matmul(B[dc // 2][:, dc % 2 * T:dc % 2 * T + T], w[:, c * P:(c + 1) * P], h[:, c, :], start=(c == 0), stop=(c == KC - 1))
                if dc % 2:
                    mm.then_inc(res_ready, 1)
            pe.wait_ge(res_ready, 4)
            pe.sem_inc(w_used, 3)
            pe.wait_ge(mod_copied, 4)
            for q in range(4):
                for j in range(3):
                    for t in range(4):
                        row = slice(32 * q, 32 * q + 1)
                        mm = nc.tensor.matmul(B[4 + q][:, 4 * j + t:4 * j + t + 1], modrow[row, j, t * P:(t + 1) * P], ones[row, 0:1], start=True, stop=True)
            mm.then_inc(mod_turned, 1)
            pe.wait_ge(mod_ready, 1)
            norm_sum(3)
            ffn(S_FFN2, 3, FFN_CHUNKS)
            norm_sum(4)
            norm_sum(5)
            def u_of(i):
                return U_Z + 4 + i - 5

            u = U_Z
            for g, (nt, w_hi, w_lo) in enumerate(((3, win_hi3, slot_lo[PLACE[S_WIN]]), (2, win_hi2, slot_lo[PLACE[S_WIN + 1]][:, 0:2 * TILE]))):
                pe.wait_ge(win_w_lo, g + 1)
                w_hi, w_lo = (w.rearrange("p (t c m) -> p t c m", t=nt, c=KC) for w in (w_hi, w_lo))
                for tb in range(TB):
                    tokens = slice(tb * P, (tb + 1) * P)
                    proj_three(u, lambda c: (in_hi[:, c, tokens], in_lo[:, c, tokens]), lambda c: (w_hi[:, :, c, :], w_lo[:, :, c, :]),
                               IN_PARTS if g == tb == 0 else None, nt * P)
                    u += 1
                if g == 0:
                    pe.wait_ge(proj_ready, u)
                    pe.sem_inc(w_used, 1)

            def head_sums(src, b0):
                for c in range(AC):
                    mm = nc.tensor.matmul(B[b0 + c // 2][:, c % 2 * T:c % 2 * T + T], headones, src[:, c, :], start=True, stop=True)
                return mm

            def low_rank(b0, lo, src, col):
                for c in range(AC):
                    mm = nc.tensor.matmul(B[b0 + c // 2][:, c % 2 * T:c % 2 * T + T], loraw[lo, col + c * P:col + (c + 1) * P], lo_t[lo, src, :], start=True, stop=True)
                mm.then_inc(lora_out, 1)

            def indexer(n):
                qb, cp = n // 2, n % 2
                nk = (qb + 1) * P
                if n:
                    pe.wait_ge(relu_ready, n)
                for cc in range(2):
                    for r in range(4):
                        mm = nc.tensor.matmul(B[r][:, cc * T:cc * T + nk], iqT[32 * r:32 * r + 32, 2 * cp + cc, qb * P:(qb + 1) * P],
                                              ikr[32 * r:32 * r + 32, 0:nk], start=True, stop=True)
                mm.then_inc(idx_ready, 1)

            for i in range(5, 48):
                if i in IDX_AT:
                    pe.wait_ge(proj_used, u_of(18))
                    indexer(IDX_AT.index(i))
                if i == LORA_AT:
                    pe.wait_ge(relu_ready, 4)
                    pe.wait_ge(lora_loaded, 16)
                    pe.wait_ge(lora_in, 2)
                    low_rank(0, slice(0, 64), 0, 0)
                    low_rank(2, slice(64, 128), 0, 0)
                if i == KK_AT:
                    pe.wait_ge(kk_sq, 1)
                    pe.wait_ge(decay_ready, 1)
                    head_sums(b2, 0).then_inc(kk_sum, 1)
                if i == BONUS_AT:
                    pe.wait_ge(iclr_ready, 1)
                    pe.wait_ge(bonus_in, 1)
                    head_sums(b2, 2).then_inc(bonus_sum, 1)
                pe.wait_ge(win_w_lo, win_group(i) + 1)
                place_i, cols = win_tile(i)
                w_hi, w_lo = win_hi_of(i), slot_lo[place_i][:, cols]
                proj_three(u, lambda c: (w_hi[:, c * P:(c + 1) * P], w_lo[:, c * P:(c + 1) * P]), lambda c: (in_hi[:, c, :], in_lo[:, c, :]))
                u += 1
                if i % 3 == 0:
                    pe.wait_ge(proj_ready, u - 1)
                    pe.sem_inc(w_used, 1)
            pe.wait_ge(proj_ready, u)
            pe.sem_inc(w_used, 1)
            pe.wait_ge(proj_used, u)
            low_rank(6, slice(0, 128), 1, ATTN_W)
            pe.wait_ge(bonus_used, 1)
            attention(HEADS_2, HEADS_1, q2, k2, v2, ex2, pts2, B[4:6])

            pe.wait_ge(o_copied, (HEADS_1 + HEADS_2) // 2)

            def pairs(fn):
                for i in range(NCH * AC):
                    for p in range(2):
                        c, hp = divmod((i + p * NCH * AC // 2) % (NCH * AC), AC)
                        mm = fn(c, hp, slice(p * HEAD, (p + 1) * HEAD))
                return mm

            def block_of(b0, c, hp, rows):
                n = (c * AC + hp) * CH
                return B[b0 + n // 512][rows, n % 512:n % 512 + CH]

            pe.wait_ge(tilde_ready, 1)
            for n, src in enumerate((v_t, b5, k_t)):
                pairs(lambda c, hp, rows: nc.tensor.matmul(block_of(2 * n, c, hp, rows), src[rows, hp, c * CH:(c + 1) * CH], ident[rows, rows], start=True, stop=True)).then_inc(turned, 1)

            pair_list = [(b5, b4, 6), (b4, b5, 0), (k_t, b4, 2), (b5, b3, 4), (k_t, b3, 6)]
            for n, (lhs, rhs, b0) in enumerate(pair_list):
                if n in (1, 2, 3):
                    pe.wait_ge(turned_used, n)
                if n == 4:
                    pe.wait_ge(pair_used, 1)

                def product(c, hp, rows):
                    t = slice(c * CH, (c + 1) * CH)
                    return nc.tensor.matmul(block_of(b0, c, hp, rows), lhs[rows, hp, t], rhs[rows, hp, t], start=True, stop=True)

                pairs(product).then_inc(pair_ready, 1)
            pe.wait_ge(pair_used, 5)
            def half_level(half, b0, col, stationary, moving):
                for j in range(LHALF):
                    for p in range(2):
                        k, rows = j ^ p, slice(p * HEAD, (p + 1) * HEAD)
                        n = half * LHALF + k
                        lo = col + k // 2 * CH
                        mm = nc.tensor.matmul(B[b0 + 2 * half + k % 2][rows, lo:lo + CH], stationary[rows, n, :], moving[rows, n, :], start=True, stop=True, skip_group_check=True)
                return mm

            for n in range(len(LEVELS)):
                for half in range(2):
                    pe.wait_ge(level_m, 2 * n + half + 1)
                    half_level(half, 0, 0, m_lev, inv).then_inc(level_x, 1)
                for half in range(2):
                    pe.wait_ge(x_copied, 2 * n + half + 1)
                    if n < len(LEVELS) - 1:
                        half_level(half, 4, 0, inv_t, xm)
                    half_level(half, 4, T, xm, inv_t).then_inc(level_d, 1)
            pe.wait_ge(inv_ready, 1)
            halves = [((i + 2 * p) % AC, slice(p * HEAD, (p + 1) * HEAD)) for i in range(AC) for p in range(2)]

            def place(b0, hp, rows):
                return B[b0 + hp // 2][rows, hp % 2 * CH:(hp % 2 + 1) * CH]

            def products(b0, lhs, rhs, start, stop):
                for hp, rows in halves:
                    mm = nc.tensor.matmul(place(b0, hp, rows), lhs(hp, rows), rhs(hp, rows), start=start and hp % 2 == 0, stop=stop, skip_group_check=True)
                return mm

            def of_chunk(a, c):
                return lambda hp, rows: a[rows, c * AC + hp, :]

            def of_heads(a):
                return lambda hp, rows: a[rows, hp, :]

            def of_tokens(a, c):
                return lambda hp, rows: a[rows, hp, c * CH:(c + 1) * CH]

            rhs_part = products(0, of_chunk(m_ak, 0), of_chunk(vt, 0), True, True)
            for c in range(NCH):
                g_in = gst[:, (c - 1) % 2]
                if c:
                    pe.wait_ge(state_ready, c)
                    rhs_part = products(0, of_tokens(b4, c), of_heads(g_in), False, True)
                rhs_part.then_inc(rhs_ready, 1)
                if c:
                    pe.wait_ge(y_copied, c)
                    products(6, of_heads(g_in), of_tokens(b3, c), True, False)
                pe.wait_ge(rhs_copied, c + 1)
                products(2, of_chunk(inv_t, c), of_heads(rhs_u), True, True).then_inc(u_ready, 1)
                products(4, of_chunk(kt, c), of_chunk(vt, c), True, False)
                products(6, of_chunk(vt, c), of_chunk(m_rk, c), c == 0, False)
                pe.wait_ge(u_copied, c + 1)
                products(4, of_chunk(bt, c), of_heads(u_sb), False, True).then_inc(g_ready, 1)
                products(6, of_heads(u_sb), of_chunk(m_rb, c), False, True).then_inc(y_ready, 1)
                if c + 1 < NCH:
                    products(0, of_chunk(m_ak, c + 1), of_chunk(vt, c + 1), True, False)
            pe.wait_ge(y_copied, NCH)
            head_sums(b1, 6).then_inc(gn_sum, 1)
            pe.wait_ge(gn_sq, 1)
            head_sums(f0, 0).then_inc(gn_var, 1)
            def branch_tile(k):
                pe.wait_ge(win_w_lo, BR_GROUP + k + 1)
                return BR_HI[k], slot_lo[PLACE[S_BR + k // 3]][:, k % 3 * TILE:(k % 3 + 1) * TILE]

            for n, (src_hi, src_lo, b0, parts) in enumerate(((o2_hi, o2_lo, 0, O2_PARTS), (rw_hi, rw_lo, 4, RW_PARTS))):
                pe.wait_ge(rw_ready if n else gn_rt, 1)
                pe.wait_ge(h_lo_ready, parts + AC)
                for i in range(4):
                    w_hi, w_lo = branch_tile(4 * n + i)
                    for e in range(2):
                        for c in range(AC):
                            w, t = slice((e * AC + c) * P, (e * AC + c + 1) * P), slice(c * T, (c + 1) * T)
                            mm = three(B[b0 + i][:, e * T:(e + 1) * T], w_hi[:, w], w_lo[:, w], src_hi[:, t], src_lo[:, t], c == 0, c == AC - 1)
                    mm.then_inc(br_ready, 1)
            for dc in range(KC):
                w_hi, w_lo = branch_tile(8 + dc)
                if dc == 0:
                    pe.wait_ge(mixed_ready, 4)
                for c in range(KC):
                    if dc == 0:
                        pe.wait_ge(h_lo_ready, MIXED_PARTS + c + 1)
                    w = slice(c * P, (c + 1) * P)
                    mm = three(B[dc // 2][:, dc % 2 * T:dc % 2 * T + T], w_hi[:, w], w_lo[:, w], mixed_hi[:, c, :], mixed_lo[:, c, :], c == 0, c == KC - 1)
                mm.then_inc(res_ready, 1)
            norm_sum(6)
            pe.wait_ge(router_loaded, 32)
            for tb in range(TB):
                for c in range(KC):
                    if tb == 0:
                        pe.wait_ge(h_ready, H_BASE[6] + c + 1)
                    mm = nc.tensor.matmul(B[0][:, tb * EXPERTS:(tb + 1) * EXPERTS], h[:, c, tb * P:(tb + 1) * P], routerw[:, c, :], start=(c == 0), stop=(c == KC - 1))
            mm.then_inc(logits_ready, 1)
            for b in range(4):
                for c in range(4):
                    lo = (b // 2) * P
                    mm = nc.tensor.transpose(B[4 + b][:, c * P:(c + 1) * P], h[:, b % 2 * 4 + c, lo:lo + P], ident)
                mm.then_inc(tok_turned, 1)

            def expert_gate_up(w, f, bank, signal):
                gate_up(bank, lambda c: w[:, c * 512 + f * P:c * 512 + (f + 1) * P], lambda c: w[:, c * 512 + EXPERT_FF + f * P:c * 512 + EXPERT_FF + (f + 1) * P], signal)

            def expert_down(w, f, a):
                return down(lambda c: w[:, GATE_UP + f * D + c * P:GATE_UP + f * D + (c + 1) * P], a)

            pe.wait_ge(scores_ready, 1)
            clear_y()
            pe.wait_ge(tok_lo_ready, 4)
            pe.wait_ge(mask_ready, 1)
            before = cst("before")
            nc.tensor.matmul(B[6][:, 0:EXPERTS], before, mask_e[:, 0, :], start=True, stop=True)
            nc.tensor.matmul(B[6][:, EXPERTS:2 * EXPERTS], before, mask_e[:, 1, :], start=True, stop=False, skip_group_check=True)
            nc.tensor.matmul(B[6][:, EXPERTS:2 * EXPERTS], ones[:], mask_e[:, 0, :], start=False, stop=True, skip_group_check=True).then_inc(rank_ready, 1)
            pe.wait_ge(beyond_ready, 1)
            for tb in range(TB):
                mm = nc.tensor.transpose(B[5][0:EXPERTS, tb * P:(tb + 1) * P], dense_e[:, tb, :], ident)
            mm.then_inc(gates_turned, 1)
            nc.tensor.matmul(B[6][:, T:T + 1], ones[:], beyond, start=True, stop=True).then_inc(beyond_sum, 1)

            def gather(q, step, bank):
                for c in range(2):
                    kc = 2 * step + c
                    for n, tok in enumerate((tok_hi, tok_lo)):
                        for tb in range(TB):
                            mm = nc.tensor.matmul(bank[:, c * 4 * CAP:(c + 1) * 4 * CAP], tok[:, tb, kc * P:(kc + 1) * P], pick[q % 2][:, tb, :],
                                                  start=(n == 0 and tb == 0), stop=(n == 1 and tb == TB - 1))
                mm.then_inc(gather_ready, 1)

            def spread_out(k):
                for c in range(KC):
                    for part in (out_hi, out_lo):
                        mm = nc.tensor.matmul(B[c // 2][:, c % 2 * T:c % 2 * T + T], part[:, c * P:(c + 1) * P], spread[k % 2], start=False, stop=False, skip_group_check=True)
                mm.then_inc(pair_spread, 1)

            def turn_pick(k, e):
                for tb in range(TB):
                    nc.tensor.matmul(B[6][:, tb * P:(tb + 1) * P], pick[k // 2][:, tb, k % 2 * P:(k % 2 + 1) * P], ident_r, start=True, stop=True)
                for n, gate in enumerate((gate_hi, gate_lo)):
                    for tb in range(TB):
                        mm = nc.tensor.matmul(B[6][:, 2 * P:2 * P + 2], pick[k // 2][:, tb, k % 2 * P:(k % 2 + 1) * P], gate[:, tb, bass.ds(e, 2)],
                                              start=(n == 0 and tb == 0), stop=(n == 1 and tb == TB - 1))
                mm.then_inc(pick_turned, 1)

            done = 2 * FFN_CHUNKS


            pe.wait_ge(pick_ready, 1)
            pe.wait_ge(gates_copied, 1)
            pe.wait_ge(flag_ready, 1)
            for step in range(4):
                gather(0, step, B[4 + step])

            def two_quads(i, n=None):
                first, last = n == 0, n == QUADS // 2 - 1
                shared_gu, shared_down = SHARED_GATE_UP.get(n, {}), SHARED_DOWN.get(n, {})
                for k in range(4):
                    q, hs = k // 2, gathered_h[k // 2]
                    us = [k % 2 * 2, k % 2 * 2 + 1]
                    pe.wait_ge(gather_copied, 8 * i + (2 * k + 4) if not last or k < 3 else 8 * i + 8)
                    for u in us:
                        pe.wait_ge(gu_landed[u], 32 * i + 16 * (q + 1))
                    for c in range(KC):
                        for j, u in enumerate(us):
                            mm = nc.tensor.matmul(B[4][CAP * j:CAP * (j + 1), :], hs[:, c, CAP * u:CAP * (u + 1)], unit(u)[:, c * 512:(c + 1) * 512],
                                                  start=(c == 0), stop=(c == KC - 1), skip_group_check=True)
                    mm.then_inc(pair_gu, 1)
                    more = not (last and k >= 2)
                    if not (first and k == 0):
                        pe.wait_ge(pair_lo, 4 * i + k)
                    turn_pick(k, 8 * i + 2 * k)
                    if more:
                        pe.wait_ge(pick_ready, 2 * i + (q + 2))
                        if k - 1 in shared_gu:
                            pe.wait_ge(act_ready, done + shared_gu[k - 1] + 1)
                        gather(q + 1, 2 * (k % 2), B[5])
                    if not (first and k == 0):
                        spread_out(k - 1)
                    pe.wait_ge(pair_act, 4 * i + (k + 1))
                    for f in range(2):
                        mm = nc.tensor.transpose(B[7][:, f * P:(f + 1) * P], act_p[:, f * P:(f + 1) * P], ident)
                    mm.then_inc(pair_turned, 1)
                    if more:
                        gather(q + 1, 2 * (k % 2) + 1, B[4])
                    pe.wait_ge(pair_act_t, 4 * i + (k + 1))
                    for u in us:
                        pe.wait_ge(down_landed[u], 32 * i + 16 * (q + 1))
                    for half in range(2):
                        for f in range(2):
                            for j, u in enumerate(us):
                                lo = GATE_UP + f * D + half * 512
                                mm = nc.tensor.matmul(B[6 + half][CAP * j:CAP * (j + 1), :], act_pt[:, f, CAP * j:CAP * (j + 1)], unit(u)[:, lo:lo + 512],
                                                      start=(f == 0), stop=(f == 1), skip_group_check=True)
                        mm.then_inc(pair_down, 1)
                    if k in shared_gu:
                        pe.wait_ge(shared_landed, 16)
                        pe.wait_ge(gather_copied, 8 * i + 2 * k + 5)
                        expert_gate_up(SHARED_UNIT, shared_gu[k], B[5], gu_ready)
                    if k in shared_down:
                        pe.wait_ge(act_ready, done + shared_down[k] + 1)
                        expert_down(SHARED_UNIT, shared_down[k], act_s)

            for n in range(2):
                two_quads(n, n)
            with pe.Fori(2, QUADS // 2 - 1) as i:
                two_quads(i)
            two_quads(QUADS // 2 - 1, QUADS // 2 - 1)
            pe.wait_ge(pair_lo, PAIRS)
            spread_out(3)
            overflow = pe.value_load(flag[0:1, :])
            with pe.If(overflow > 0):
                with pe.Fori(0, EXPERTS // UNITS) as i:
                    for s in range(2 * UNITS + 1):
                        if s < 2 * UNITS:
                            if s % 2 == 0:
                                pe.wait_ge(unit_landed[s // 2], 16 * i + 16)
                            expert_gate_up(unit(s // 2), s % 2, B[4 + s % 2], dense_gu)
                        if s >= 1:
                            pe.wait_ge(dense_act, 2 * UNITS * i + s)
                            mm = expert_down(unit((s - 1) // 2), (s - 1) % 2, act_f[:, (s - 1) % 2, :])
                            if s % 2 == 0:
                                mm.then_inc(unit_used, 1)
            norm_sum(7)

        @block.scalar
        def _(act):
            def load_table(func):
                nc.scalar.activation(small[:, 60:61], eps, func)

            def norm_squares(k):
                if k:
                    load_table(ACT.Sqrt)
                for g in range(4):
                    if k == 0:
                        act.wait_ge(x_loaded, 16)
                    else:
                        act.wait_ge(x_ready, 4 * (k - 1) + g + 1)
                    nc.scalar.activation(sq[:, 2 * g:2 * g + 2, :], x[:, 2 * g:2 * g + 2, :], ACT.Square).then_inc(sq_ready, 1)
                act.wait_ge(ss_ready, k + 1)
                nc.scalar.activation(rt[:], B[6][:, 0:T], ACT.Sqrt, scale=1.0 / D, bias=eps).then_inc(rt_ready, 1)
                if k in (1, 3, 6):
                    load_table(ACT.Sigmoid)

            def ffn_start(base):
                act.wait_ge(landed[PLACE[base]], 16 * LOADS[base])
                nc.scalar.activation(gu_hi[0], slot(base)[:, 0:2 * TILE], ACT.Copy).then_inc(gu_hi_ready, 1)

            def ffn(base, k, done):
                def first_part(dst, s, lo, hi, signal):
                    nc.scalar.activation(dst, slot(base + s)[:, lo:hi], ACT.Copy).then_inc(signal, 1)

                def split_gate_up(s, i):
                    act.wait_ge(landed[PLACE[base + s]], 16 * i + 16 * LOADS[base + s])
                    first_part(gu_hi[s % 2], s, 0, 2 * TILE, gu_hi_ready)

                for c in range(0, KC, 2):
                    act.wait_ge(h_ready, H_BASE[k] + c + 2)
                    nc.scalar.activation(h_hi[:, c:c + 2, :], h[:, c:c + 2, :], ACT.Copy).then_inc(h_hi_ready, 1)
                with act.Fori(0, 2) as i:
                    for s in range(RING):
                        if s + 1 < RING:
                            split_gate_up(s + 1, i)
                        act.wait_ge(gu_ready, RING * i + (done + s + 1))
                        nc.scalar.activation(sig_f[:, s % 2, :], B[4 + s % 2][:, 0:T], ACT.Sigmoid).then_inc(sig_ready, 1)
                        first_part(down_hi[s % 2], s, 2 * TILE, SLOT, down_hi_ready)
                    with act.If(i < 1):
                        split_gate_up(0, 1)

            def evacuate(u, dst, n=T, func=ACT.Copy):
                act.wait_ge(proj_ready, u + 1)
                nc.scalar.activation(dst, PROJ_BANKS[u % 3][:, 0:n], func).then_inc(proj_used, 1)

            def attention(heads, n0, oT, ex, pts, o_banks):
                for j in range(heads + 3):
                    if j < heads:
                        act.wait_ge(max_ready, n0 + j + 1)
                        e, k = ex[:, j % 3, :], 2 * (j % 3)
                        nc.scalar.activation(e[:, 0:T], e[:, 0:T], ACT.Exp, bias=nmax[:, k:k + 1], accum_out=rsum[:, k:k + 1])
                        nc.scalar.activation(e[:, T:T + P], e[:, T:T + P], ACT.Exp, bias=nmax[:, k + 1:k + 2], accum_out=rsum[:, k + 1:k + 2]).then_inc(exp_ready, 1)
                    if 2 <= j <= heads + 1:
                        a = j - 2
                        act.wait_ge(pt_ready, n0 + a + 1)
                        if a >= 2:
                            act.wait_ge(o_ready, n0 + a - 1)
                        nc.scalar.activation(pts[:, a % 2, :], B[2 + a % 2][:, 0:384], ACT.Copy).then_inc(pts_ready, 1)
                    if j >= 3 and j % 2 == 0:
                        a = (j - 3) // 2
                        act.wait_ge(o_ready, n0 + 2 * a + 2)
                        nc.scalar.activation(oT[:, a, :], o_banks[a % len(o_banks)][:, 0:T], ACT.Copy).then_inc(o_copied, 1)

            act.wait_ge(ones_ready, 1)
            load_table(ACT.Sqrt)
            act.wait_ge(line_ready, 1)
            nc.scalar.activation(line_sb[0:HEADS_1 + HEADS_2, :], B[7][0:HEADS_1 + HEADS_2, :], ACT.Copy).then_inc(line_copied, 1)
            norm_squares(0)
            act.wait_ge(pool_d, 4)
            ffn_start(S_FFN1)
            norm_squares(1)
            act.wait_ge(vec_loaded, 16)
            nc.scalar.activation(csig, vecs[:, VEC["c"][0]:VEC["c"][1]], ACT.Sigmoid).then_inc(csig_ready, 1)
            ffn(S_FFN1, 1, 0)

            def first_parts(dst, t0, nt):
                for n in range(t0, t0 + nt):
                    if n % 3 == 0:
                        act.wait_ge(landed[PLACE[S_KVQ + n // 3]], 16 * LOADS[S_KVQ + n // 3])
                lo = SLOT * PLACE[S_KVQ] + t0 * TILE
                nc.scalar.activation(dst, ring[:, lo:lo + nt * TILE], ACT.Copy).then_inc(kvq_w_hi, 1)

            first_parts(v_hi[0], 0, 2)
            norm_squares(2)
            for c in range(0, KC, 2):
                act.wait_ge(h_ready, H_BASE[2] + c + 2)
                nc.scalar.activation(kv_hi[:, c:c + 2, :], h[:, c:c + 2, :], ACT.Copy).then_inc(h_hi_ready, 1)
            first_parts(v_hi[1], 2, 2)

            def keys_queries_parts(n):
                first_parts(kq_hi[n % 3], KC + n, 1)

            for g in range(V_PAIRS):
                for tb in range(TB):
                    evacuate(U_V1 + 2 * g + tb, v1[:, tb, 2 * g * P:(2 * g + 2) * P])
                if g + 2 < V_PAIRS:
                    first_parts(v_hi[g % 2], 2 * g + 4, 2)
                if g == V_PAIRS - 2:
                    keys_queries_parts(0)
                    keys_queries_parts(1)
                    act.wait_ge(h_ready, H_BASE[2] + 2 * KC)
                    for c in range(0, KC, 2):
                        nc.scalar.activation(hq_hi[:, c:c + 2, :], hq[:, c:c + 2, :], ACT.Copy).then_inc(h_hi_ready, 1)
            for n in range(KQ_TILES):
                if n + 2 < KQ_TILES:
                    keys_queries_parts(n + 2)
                evacuate(U_K1 + n, k1[:, n, :] if n < KC else q1[:, n - KC, :])
            attention(HEADS_1, 0, h, ex, pts, B[4:5])
            act.wait_ge(w_used, S_O)
            for q in range(4):
                nc.scalar.activation(modrow[32 * q:32 * q + 1, :, :], banks[32 * q:32 * q + 1, 5:8, :], ACT.Copy).then_inc(mod_copied, 1)
            ffn_start(S_FFN2)
            norm_squares(3)
            act.wait_ge(mod_turned, 1)
            ffn(S_FFN2, 3, FFN_CHUNKS)
            norm_squares(4)

            def first_part(dst, n, lo, hi):
                act.wait_ge(landed[PLACE[n]], 16 * LOADS[n])
                nc.scalar.activation(dst, slot(n)[:, lo:hi], ACT.Copy).then_inc(win_w_hi, 1)

            def tile_part(i):
                first_part(win_hi_of(i), S_WIN + i // 3, i % 3 * TILE, (i % 3 + 1) * TILE)

            first_part(win_hi3, S_WIN, 0, 3 * TILE)
            norm_squares(5)
            for c in range(0, KC, 2):
                act.wait_ge(h_ready, H_BASE[5] + c + 2)
                nc.scalar.activation(in_hi[:, c:c + 2, :], h[:, c:c + 2, :], ACT.Copy).then_inc(h_hi_ready, 1)
            first_part(win_hi2, S_WIN + 1, 0, 2 * TILE)
            u = U_Z
            for tb in range(TB):
                evacuate(u, v2[:, tb, 0:3 * P], 3 * P)
                u += 1
            for i in range(5, 8):
                tile_part(i)
            for tb in range(TB):
                act.wait_ge(proj_ready, u + 1)
                bank = PROJ_BANKS[u % 3]
                nc.scalar.activation(v2[:, tb, 3 * P:], bank[:, 0:P], ACT.Copy)
                nc.scalar.activation(iw[:, tb, :], bank[:, P:P + IDX_HEADS], ACT.Copy).then_inc(proj_used, 1)
                u += 1
            dsts = [q2[:, c, :] for c in range(AC)] + [k2[:, c, :] for c in range(AC)] + [iqT[:, c, :] for c in range(AC)] + [ikr]
            dsts += [zr[:, c, 1:] for c in ZR_ORDER]
            dsts += [d[:, c, :] for d in (sig_a, sig_r) for c in range(KC)]

            def indexer(n):
                nk = (n // 2 + 1) * P
                act.wait_ge(idx_ready, n + 1)
                if n:
                    act.wait_ge(relu_used, n)
                for r in range(4):
                    src = B[r].rearrange("p (a t) -> p a t", a=2)[:, :, 0:nk]
                    mm = nc.scalar.activation(relu_i[:, 2 * r:2 * r + 2, 0:nk], src, ACT.Relu)
                mm.then_inc(relu_ready, 1)

            for i, d in enumerate(dsts, 5):
                if i + 3 < 48:
                    if i + 3 == 34:
                        act.wait_ge(relu_used, 4)
                    tile_part(i + 3)
                if i in IDX_AT:
                    indexer(IDX_AT.index(i))
                if i == LO_AT:
                    act.wait_ge(shifted, 2)
                    nc.scalar.activation(lo_t[0:64, 0, :], lo_t[0:64, 0, :], ACT.Tanh).then_inc(lora_in, 1)
                    nc.scalar.activation(lo_t[:, 1, :], lo_t[:, 1, :], ACT.Sigmoid).then_inc(lora_in, 1)
                if i == DECAY_AT:
                    act.wait_ge(lora_out, 1)
                    for c in range(AC):
                        nc.scalar.activation(b1[:, c, :], B[c // 2][:, c % 2 * T:c % 2 * T + T], ACT.Sigmoid, bias=vcol("decay_w0", c)).then_inc(act_step, 1)
                    act.wait_ge(lora_out, 2)
                    for c in range(AC):
                        mm = nc.scalar.activation(b5[:, c, :], B[2 + c // 2][:, c % 2 * T:c % 2 * T + T], ACT.Sigmoid, bias=vcol("iclr_a0", c))
                    mm.then_inc(iclr_ready, 1)
                    act.wait_ge(act_step, AC)
                    nc.scalar.activation(b1, b1, ACT.Exp, scale=-math.exp(-0.5)).then_inc(decay_ready, 1)
                if i == KK_SQRT_AT:
                    act.wait_ge(kk_sum, 1)
                    nc.scalar.activation(b6, banks[:, 0:2, :].rearrange("p a (b t) -> p (a b) t", b=2), ACT.Sqrt).then_inc(kk_norm, 1)
                evacuate(u, d, func=ACT.Copy if i < 32 else ACT.Sigmoid)
                u += 1
            act.wait_ge(lora_out, 3)
            act.wait_ge(tilde_ready, 1)
            nc.scalar.activation(b6, banks[:, 6:8, :].rearrange("p a (b t) -> p (a b) t", b=2), ACT.Copy)
            attention(HEADS_2, HEADS_1, o2, ex2, pts2, B[4:6])

            def pair_bank(b0):
                return banks[:, b0:b0 + 2, :].rearrange("p a (b t) -> p (a b) t", t=CH)

            for n, dst in enumerate((vt, bt, kt)):
                act.wait_ge(turned, n + 1)
                nc.scalar.activation(dst, pair_bank(2 * n), ACT.Copy).then_inc(turned_used, 1)
            for n in range(len(LEVELS)):
                for half in range(2):
                    act.wait_ge(level_x, 2 * n + half + 1)
                    nc.scalar.activation(level_half(xm, half), level_bank(0, half, 0), ACT.Copy).then_inc(x_copied, 1)

            def branch_part(k):
                first_part(BR_HI[k], S_BR + k // 3, k % 3 * TILE, (k % 3 + 1) * TILE)

            branch_part(0)
            for c in range(NCH):
                act.wait_ge(rhs_ready, c + 1)
                nc.scalar.activation(by_bank(rhs_u), four_heads(0), ACT.Copy).then_inc(rhs_copied, 1)
                act.wait_ge(u_ready, c + 1)
                if c:
                    act.wait_ge(y_ready, c)
                nc.scalar.activation(by_bank(u_sb), four_heads(2), ACT.Copy).then_inc(u_copied, 1)
                act.wait_ge(y_ready, c + 1)
                nc.scalar.activation(by_bank(b1[:, :, c * CH:(c + 1) * CH]), four_heads(6), ACT.Copy).then_inc(y_copied, 1)
            branch_part(1)
            nc.scalar.activation(o2_hi, o2.rearrange("p a t -> p (a t)"), ACT.Copy).then_inc(h_hi_ready, AC // 2)
            branch_part(2)
            branch_part(3)
            act.wait_ge(gn_var, 1)
            nc.scalar.activation(f1, banks[:, 0:2, :].rearrange("p a (b t) -> p (a b) t", b=2), ACT.Sqrt, scale=1.0 / HEAD, bias=gn_eps).then_inc(gn_rt, 1)
            act.wait_ge(br_ready, 1)
            branch_part(4)
            act.wait_ge(br_ready, 3)
            branch_part(5)
            act.wait_ge(rw_ready, 1)
            nc.scalar.activation(rw_hi, rw.rearrange("p a t -> p (a t)"), ACT.Copy).then_inc(h_hi_ready, AC // 2)
            act.wait_ge(br_ready, 4)
            branch_part(6)
            for b in range(4):
                act.wait_ge(br_ready, b + 5)
                branch_part(b + 7)
                act.wait_ge(mixed_ready, b + 1)
                nc.scalar.activation(mixed_hi[:, 2 * b:2 * b + 2, :], mixed[:, 2 * b:2 * b + 2, :], ACT.Copy).then_inc(h_hi_ready, 1)
            for k in range(11, 16):
                act.wait_ge(res_ready, 4 + k - 10)
                branch_part(k)
            norm_squares(6)
            act.wait_ge(logits_ready, 1)
            nc.scalar.activation(score_e, B[0][:, 0:TB * EXPERTS].rearrange("p (a e) -> p a e", a=TB), ACT.Sigmoid).then_inc(scores_ready, 1)
            for b in range(4):
                act.wait_ge(tok_turned, b + 1)
                nc.scalar.activation(tok_hi[:, b // 2, b % 2 * 512:(b % 2 + 1) * 512], B[4 + b], ACT.Copy).then_inc(tok_hi_ready, 1)
            act.wait_ge(gates_turned, 1)
            nc.scalar.activation(dense_t[0:EXPERTS, :], B[5][0:EXPERTS, 0:T], ACT.Copy).then_inc(gates_copied, 1)

            def copy_gathered(q, step, bank):
                nc.scalar.activation(gathered_h[q % 2][:, 2 * step:2 * step + 2, :], bank.rearrange("p (c s) -> p c s", c=2), ACT.Copy).then_inc(gather_copied, 1)

            for step in range(4):
                act.wait_ge(gather_ready, step + 1)
                copy_gathered(0, step, B[4 + step])

            def two_quads(i, n=None):
                first, last = n == 0, n == QUADS // 2 - 1
                shared_gu = SHARED_GATE_UP.get(n, {})
                for k in range(4):
                    q, more = k // 2, not (last and k >= 2)
                    act.wait_ge(pair_gu, 4 * i + (k + 1))
                    nc.scalar.activation(sig_p, B[4][:, 0:T], ACT.Sigmoid).then_inc(pair_sig, 1)
                    act.wait_ge(pick_turned, 4 * i + (k + 1))
                    nc.scalar.activation(spread[k % 2], B[6][:, 0:T], ACT.Copy)
                    for j in range(2):
                        ins = nc.scalar.activation(slot_gate[k % 2][CAP * j:CAP * (j + 1), :], B[6][CAP * j:CAP * (j + 1), T + j:T + j + 1], ACT.Copy)
                    ins.then_inc(spread_ready, 1)
                    if more:
                        act.wait_ge(gather_ready, 8 * i + (2 * k + 5))
                        copy_gathered(q + 1, 2 * (k % 2), B[5])
                    act.wait_ge(pair_turned, 4 * i + (k + 1))
                    nc.scalar.activation(act_pt, B[7][:, 0:2 * P].rearrange("p (f s) -> p f s", f=2), ACT.Copy).then_inc(pair_act_t, 1)
                    if more:
                        act.wait_ge(gather_ready, 8 * i + (2 * k + 6))
                        copy_gathered(q + 1, 2 * (k % 2) + 1, B[4])
                    for half in range(2):
                        act.wait_ge(pair_down, 8 * i + (2 * k + half + 1))
                        nc.scalar.activation(out_hi[:, half * 512:(half + 1) * 512], B[6 + half], ACT.Copy).then_inc(pair_hi, 1)
                    if k in shared_gu:
                        act.wait_ge(gu_ready, 2 * FFN_CHUNKS + shared_gu[k] + 1)
                        nc.scalar.activation(sig_s, B[5][:, 0:T], ACT.Sigmoid).then_inc(sig_ready, 1)

            for n in range(2):
                two_quads(n, n)
            with act.Fori(2, QUADS // 2 - 1) as i:
                two_quads(i)
            two_quads(QUADS // 2 - 1, QUADS // 2 - 1)
            act.wait_ge(flag_ready, 1)
            overflow = act.value_load(flag[0:1, :])
            with act.If(overflow > 0):
                with act.Fori(0, EXPERTS // UNITS) as i:
                    for s in range(2 * UNITS):
                        act.wait_ge(dense_gu, 2 * UNITS * i + (s + 1))
                        nc.scalar.activation(sig_f[:, s % 2, :], B[4 + s % 2][:, 0:T], ACT.Sigmoid).then_inc(dense_sig, 1)
            norm_squares(7)

        @block.vector
        def _(dve):
            steps = [0]

            def then(ins):
                steps[0] += 1
                ins.then_inc(dve_step, 1)
                dve.wait_ge(dve_step, steps[0])

            def norm_scale(k, weight, dst):
                dve.wait_ge(rt_ready, k + 1)
                then(nc.vector.reciprocal(rinv[:], rt[:]))
                for c in range(KC):
                    nc.vector.scalar_tensor_tensor(dst(c), x[:, c, :], weight(c), rinv[:], ALU.mult, ALU.mult).then_inc(h_ready, 1)

            def ffn(base, done, k, weight, meanwhile=None):
                def second_part(hi, s, lo, to, signal):
                    nc.vector.tensor_tensor(slot_lo[PLACE[base + s]][:, lo:to], slot(base + s)[:, lo:to], hi.bitcast(F32), ALU.subtract).then_inc(signal, 1)

                def split_gate_up(s, i):
                    dve.wait_ge(gu_hi_ready, RING * i + (done + s + 1))
                    second_part(gu_hi[s % 2], s, 0, 2 * TILE, gu_lo_ready)

                split_gate_up(0, 0)
                dve.wait_ge(rt_ready, k + 1)
                then(nc.vector.reciprocal(rinv[:], rt[:]))
                for c in range(0, KC + 4, 2):
                    if c < KC:
                        for n in (c, c + 1):
                            nc.vector.scalar_tensor_tensor(h[:, n, :], x[:, n, :], weight(n), rinv[:], ALU.mult, ALU.mult).then_inc(h_ready, 1)
                    if c >= 4:
                        n = c - 4
                        dve.wait_ge(h_hi_ready, (H_PARTS[k] + n) // 2 + 1)
                        nc.vector.tensor_tensor(h_lo[:, n:n + 2, :], h[:, n:n + 2, :], h_hi[:, n:n + 2, :].bitcast(F32), ALU.subtract).then_inc(h_lo_ready, 2)
                act_raw = act_f[:, 0, :]
                with dve.Fori(0, 2) as i:
                    for s in range(RING):
                        if s + 1 < RING:
                            split_gate_up(s + 1, i)
                        dve.wait_ge(sig_ready, RING * i + (done + s + 1))
                        gu, a = B[4 + s % 2], s % 2

                        def step(n, ins):
                            ins.then_inc(dve_step, 1)
                            dve.wait_ge(dve_step, 3 * RING * i + (steps[0] + 3 * s + n + 1))

                        step(0, nc.vector.tensor_tensor(gated[:, a, :], gu[:, 0:T], sig_f[:, a, :], ALU.mult))
                        step(1, nc.vector.tensor_tensor(act_raw, gated[:, a, :], gu[:, T:2 * T], ALU.mult))
                        step(2, nc.vector.tensor_copy(act_hi[a], act_raw))
                        nc.vector.tensor_tensor(act_lo[a], act_raw, act_hi[a].bitcast(F32), ALU.subtract).then_inc(act_ready, 1)
                        dve.wait_ge(down_hi_ready, RING * i + (done + s + 1))
                        second_part(down_hi[a], s, 2 * TILE, SLOT, down_lo_ready)
                    with dve.If(i < 1):
                        split_gate_up(0, 1)
                steps[0] += 3 * FFN_CHUNKS
                if meanwhile is not None:
                    meanwhile()
                dve.wait_ge(w_used, base + FFN_CHUNKS)
                for b in range(4):
                    xb = x[:, 2 * b:2 * b + 2, :]
                    nc.vector.tensor_tensor(xb, B[b].rearrange("p (a t) -> p a t", a=2), xb, ALU.add).then_inc(x_ready, 1)

            def attention(heads, n0, bias, extra, ex):
                for j in range(heads + 1):
                    if j < heads:
                        b, e, k = B[j % 2], ex[:, j % 3, :], 2 * (j % 3)
                        dve.wait_ge(s_ready, n0 + j + 1)
                        if j >= 3:
                            dve.wait_ge(pt_ready, n0 + j - 2)
                        nc.vector.scalar_tensor_tensor(e[:, 0:T], b[:, 0:T], HEAD ** -0.5, bias[:, j, :], ALU.mult, ALU.add)
                        m = nc.vector.scalar_tensor_tensor(e[:, T:T + P], b[:, T:T + P], HEAD ** -0.5, bias[:, j, P:T], ALU.mult, ALU.add)
                        m.then_inc(s_used, 1)
                        dve.wait_ge(s_used, n0 + j + 1)
                        if extra is not None:
                            then(nc.vector.tensor_tensor(e, e, extra, ALU.add))
                        nc.vector.tensor_reduce(nmax[:, k:k + 1], e[:, 0:T], AX_X, ALU.max, negate=True)
                        nc.vector.tensor_reduce(nmax[:, k + 1:k + 2], e[:, T:T + P], AX_X, ALU.max, negate=True).then_inc(max_ready, 1)
                    if j >= 1:
                        a = j - 1
                        e, k = ex[:, a % 3, :], 2 * (a % 3)
                        dve.wait_ge(exp_ready, n0 + a + 1)
                        then(nc.vector.reciprocal(rrec[:, k:k + 2], rsum[:, k:k + 2]))
                        nc.vector.tensor_scalar(e[:, 0:T], e[:, 0:T], rrec[:, k:k + 1], None, ALU.mult)
                        nc.vector.tensor_scalar(e[:, T:T + P], e[:, T:T + P], rrec[:, k + 1:k + 2], None, ALU.mult).then_inc(p_ready, 1)

            def residual(first):
                for b in range(4):
                    dve.wait_ge(res_ready, first + b + 1)
                    xb = x[:, 2 * b:2 * b + 2, :]
                    nc.vector.tensor_tensor(xb, B[b].rearrange("p (a t) -> p a t", a=2), xb, ALU.add).then_inc(x_ready, 1)

            nc.vector.memset(ones[:], 1.0)
            nc.vector.memset(zeros[:], 0.0)
            nc.vector.memset(eps, EPS)
            then(nc.vector.memset(gn_eps, GN_EPS))
            nc.vector.memset(hp[:, :, 0:PAD], 0.0).then_inc(ones_ready, 1)

            dve.wait_ge(vec_loaded, 16)
            norm_scale(0, lambda c: vcol("norm_mixer0", c), lambda c: hp[:, c, PAD:])
            dve.wait_ge(h_ready, KC)
            W = PAD + T
            then(nc.vector.tensor_tensor(pw_b[:, :, 1:W], hp[:, :, 1:W], hp[:, :, 0:W - 1], ALU.add))
            then(nc.vector.tensor_tensor(pw_c[:, 2:, 3:W], pw_b[:, 2:, 3:W], pw_b[:, 2:, 1:W - 2], ALU.add))
            then(nc.vector.tensor_tensor(pw_b[:, 4:, 7:W], pw_c[:, 4:, 7:W], pw_c[:, 4:, 3:W - 4], ALU.add))
            then(nc.vector.tensor_tensor(pw_c[:, 6:, 15:W], pw_b[:, 6:, 15:W], pw_b[:, 6:, 7:W - 8], ALU.add))
            dve.wait_ge(pool_loaded, 32)
            for g in range(4):
                win = (pw_b, pw_c)[g % 2][:, 2 * g:2 * g + 2, PAD:]
                hg = h[:, 2 * g:2 * g + 2, :]
                then(nc.vector.tensor_tensor(hg, win, icnt[:, g:g + 1, :].broadcast_to([P, 2, T]), ALU.mult))
                nc.vector.tensor_tensor(hg, hg, hp[:, 2 * g:2 * g + 2, PAD:], ALU.subtract).then_inc(pool_d, 1)
            for g in range(4):
                dve.wait_ge(pool_y, g + 1)
                for e in range(2):
                    c = 2 * g + e
                    last = nc.vector.scalar_tensor_tensor(x[:, c, :], B[g][:, e * T:(e + 1) * T], vcol("pool_scale", c), x[:, c, :], ALU.mult, ALU.add)
                last.then_inc(x_ready, 1)
            dve.wait_ge(csig_ready, 1)
            nc.vector.tensor_tensor(csil, csig, vecs[:, VEC["c"][0]:VEC["c"][1]], ALU.mult).then_inc(csil_ready, 1)
            dve.wait_ge(line_stored, 16)
            def second_part(n, dst, hi, at):
                dve.wait_ge(kvq_w_hi, n + 1)
                lo = SLOT * PLACE[S_KVQ] + at
                nc.vector.tensor_tensor(dst, ring[:, lo:lo + dst.shape[-1]], hi.bitcast(F32), ALU.subtract).then_inc(kvq_w_lo, 1)

            def value_parts(g):
                second_part(g, v_lo[g], v_hi[g % 2], 2 * TILE * g)

            def keys_queries_parts(n):
                i = KC + n
                second_part(V_PAIRS + n, slot_lo[PLACE[S_KVQ + i // 3]][:, i % 3 * TILE:(i % 3 + 1) * TILE], kq_hi[n % 3], i * TILE)

            ffn(S_FFN1, 0, 1, lambda c: vcol("norm_ffn0", c), meanwhile=lambda: value_parts(0))
            dve.wait_ge(rt_ready, 3)
            then(nc.vector.reciprocal(rinv[:], rt[:]))
            for c in range(0, KC + 4, 2):
                if c < KC:
                    for n in (c, c + 1):
                        nc.vector.scalar_tensor_tensor(h[:, n, :], x[:, n, :], vcol("kv_norm", n), rinv[:], ALU.mult, ALU.mult).then_inc(h_ready, 1)
                if c >= 4:
                    n = c - 4
                    dve.wait_ge(h_hi_ready, (KV_PARTS + n) // 2 + 1)
                    nc.vector.tensor_tensor(kv_lo[:, n:n + 2, :], h[:, n:n + 2, :], kv_hi[:, n:n + 2, :].bitcast(F32), ALU.subtract).then_inc(h_lo_ready, 2)
            value_parts(1)
            for c in range(KC):
                nc.vector.scalar_tensor_tensor(hq[:, c, :], x[:, c, :], vcol("norm_mixer1", c), rinv[:], ALU.mult, ALU.mult).then_inc(h_ready, 1)
            value_parts(2)
            value_parts(3)
            keys_queries_parts(0)
            keys_queries_parts(1)
            for c in range(0, KC, 2):
                dve.wait_ge(h_hi_ready, (HQ_PARTS + c) // 2 + 1)
                nc.vector.tensor_tensor(hq_lo[:, c:c + 2, :], hq[:, c:c + 2, :], hq_hi[:, c:c + 2, :].bitcast(F32), ALU.subtract).then_inc(h_lo_ready, 2)
            for n in range(2, KQ_TILES):
                keys_queries_parts(n)
            dve.wait_ge(bias_loaded, 16 * P // SHIFTS)
            attention(HEADS_1, 0, bias1, None, ex)
            residual(0)
            dve.wait_ge(mod_turned, 1)
            by_row = lambda a: a.rearrange("p (j q t) -> p j q t", j=3, q=4)
            for q in range(4):
                products = B[4 + q][:, 0:12].rearrange("p (j t) -> p j t", j=3)
                ins = nc.vector.tensor_tensor(by_row(mod[:])[:, :, q, :], products, by_row(vecs[:, VEC["ada_b"][0]:VEC["ada_b"][1]])[:, :, q, :], ALU.add)
            ins.then_inc(mod_ready, 1)
            dve.wait_ge(mod_ready, 1)
            for dst, col, g in ((scale1, 8, "norm1_g"), (scale2, 32, "norm2_g")):
                last = nc.vector.scalar_tensor_tensor(dst[:], mod[:, col:col + 8], 1.0, vecs[:, VEC[g][0]:VEC[g][1]], ALU.add, ALU.mult)
            then(last)
            ffn(S_FFN2, FFN_CHUNKS, 3, lambda c: vcol("norm_ffn1", c))
            dve.wait_ge(rt_ready, 5)
            then(nc.vector.reciprocal(rinv[:], rt[:]))
            for c in range(KC):
                last = nc.vector.scalar_tensor_tensor(x[:, c, :], x[:, c, :], vcol("final_norm", c), rinv[:], ALU.mult, ALU.mult)
                if c % 2:
                    last.then_inc(x_ready, 1)
            def norm_modulated(k, scale, shift, parts=None):
                dve.wait_ge(rt_ready, k + 1)
                then(nc.vector.reciprocal(rinv[:], rt[:]))
                for c in range(KC + 1):
                    if c < KC:
                        nc.vector.scalar_tensor_tensor(h[:, c, :], x[:, c, :], scale[:, c:c + 1], rinv[:], ALU.mult, ALU.mult).then_inc(dve_step, 1)
                    if c:
                        dve.wait_ge(dve_step, steps[0] + c)
                        nc.vector.tensor_scalar(h[:, c - 1, :], h[:, c - 1, :], mod[:, shift + c - 1:shift + c], None, ALU.add).then_inc(h_ready, 1)
                    if parts is not None and c >= 4 and c % 2 == 0:
                        parts(c - 4)
                steps[0] += KC

            def input_parts(c):
                dve.wait_ge(h_hi_ready, (IN_PARTS + c) // 2 + 1)
                nc.vector.tensor_tensor(in_lo[:, c:c + 2, :], h[:, c:c + 2, :], in_hi[:, c:c + 2, :].bitcast(F32), ALU.subtract).then_inc(h_lo_ready, 2)
            norm_modulated(5, scale1, 0, parts=input_parts)
            input_parts(KC - 2)
            dve.wait_ge(proj_used, U_Z + 4)
            then(nc.vector.tensor_scalar(iw, iw, IDX_HEADS ** -0.5 * IDX_DIM ** -0.5, None, ALU.mult))
            causal = cst("causal")
            parts = {1: slice(0, T), 0: slice(T, T + P)}
            dve.wait_ge(bias2_loaded, 16 * P // SHIFTS)
            then(nc.vector.memset(zr[:, :, 0:1], 0.0))

            def token_shift(lo, hi):
                first = U_Z + 4 + 18 - 5
                dve.wait_ge(proj_used, first + (ZR_ORDER.index(hi - 1) + 1))
                then(nc.vector.tensor_tensor(zs[:, lo:hi, :], zr[:, lo:hi, 0:T], zr[:, lo:hi, 1:], ALU.subtract))
                for c in range(lo, hi):
                    nc.vector.scalar_tensor_tensor(zs[:, c, :], zs[:, c, :], vcol("tshift_mu", c), zr[:, c, 1:], ALU.mult, ALU.add).then_inc(shifted, 1)

            for n in range(4):
                qb, cp = n // 2, n % 2
                nk = (qb + 1) * P
                dve.wait_ge(relu_ready, n + 1)
                for r in range(4):
                    for cc in range(2):
                        head = (2 * cp + cc) * 4 + r
                        acc, rl, w = work[:, parts[qb]], relu_i[:, 2 * r + cc, 0:nk], iw[:, qb, head:head + 1]
                        prev = causal[:, parts[qb]] if cp == 0 and r == 0 and cc == 0 else acc
                        then(nc.vector.scalar_tensor_tensor(acc, rl, w, prev, ALU.mult, ALU.add))
                dve.sem_inc(relu_used, 1)
                if n == 1:
                    token_shift(12, 14)
            for it in range(TOP_KEYS // 8):
                for qb in range(2):
                    last = nc.vector.max(top8[:, qb, :], work[:, parts[qb]])
                then(last)
                for qb in range(2):
                    last = nc.vector.match_replace(work[:, parts[qb]], top8[:, qb, :], work[:, parts[qb]], TAKEN)
                then(last)
            then(nc.vector.tensor_scalar(mask2, work, TAKEN / 2, MASKED, ALU.is_gt, ALU.mult))
            then(nc.vector.tensor_tensor(mask2, mask2, causal, ALU.add))
            token_shift(0, 12)
            dve.wait_ge(shifted, ZR)

            def per_chunk(fn):
                for c in range(AC):
                    last = fn(c)
                then(last)

            per_chunk(lambda c: nc.vector.tensor_scalar(b4[:, c, :], k_t[:, c, :], vcol("k_k", c), None, ALU.mult))
            nc.vector.tensor_tensor(b2, b4, b4, ALU.mult).then_inc(kk_sq, 1)
            dve.wait_ge(iclr_ready, 1)
            per_chunk(lambda c: nc.vector.tensor_scalar(b3[:, c, :], b5[:, c, :], 1.0, vcol("k_a", c), ALU.subtract, ALU.mult))
            then(nc.vector.scalar_tensor_tensor(k_t, b3, 1.0, k_t, ALU.add, ALU.mult))
            then(nc.vector.tensor_tensor(b3, r_t, k_t, ALU.mult))
            dve.wait_ge(kk_norm, 1)
            for c in range(AC):
                last = nc.vector.tensor_scalar(b2[:, c, :], b3[:, c, :], vcol("r_k", c), None, ALU.mult)
            last.then_inc(bonus_in, 1)
            then(nc.vector.tensor_scalar(b6, b6, 1e-12, None, ALU.max))
            then(nc.vector.reciprocal(b6, b6))
            then(nc.vector.tensor_tensor(b4, b4, b6, ALU.mult))
            starts = lambda a: a.rearrange("p a (c t) -> p a c t", t=CH)
            dve.wait_ge(decay_ready, 1)
            then(nc.vector.memset(b3, 0.0))
            then(nc.vector.tensor_copy(starts(b3)[:, :, :, 0], starts(b1)[:, :, :, 0]))
            then(nc.vector.memset(starts(b1)[:, :, :, 0:1], 0.0))
            dve.wait_ge(bonus_sum, 1)
            per_chunk(lambda c: nc.vector.tensor_tensor_scan(b2[:, c, :], b1[:, c, :], b3[:, c, :], 0.0, ALU.mult, ALU.add))
            nc.vector.tensor_copy(p_end, starts(b2)[:, :, :, CH - 1])
            then(nc.vector.tensor_copy(b3[:, :, 1:], b2[:, :, 0:T - 1]))
            then(nc.vector.memset(starts(b3)[:, :, :, 0:1], 1.0))
            then(nc.vector.reciprocal(b1, b2))
            then(nc.vector.tensor_tensor(b5, b4, b5, ALU.mult))
            then(nc.vector.scalar_tensor_tensor(b4, b4, -1.0, b3, ALU.mult, ALU.mult))
            nc.vector.tensor_tensor(b5, b5, b1, ALU.mult)
            nc.vector.tensor_tensor(b3, r_t, b2, ALU.mult)
            then(nc.vector.tensor_tensor(k_t, k_t, b1, ALU.mult))
            dve.sem_inc(tilde_ready, 1)
            nc.vector.tensor_tensor(b2, banks[:, 2:4, :].rearrange("p a (b t) -> p (a b) t", b=2), v_t, ALU.mult).then_inc(bonus_used, 1)

            attention(HEADS_2, HEADS_1, bias2, mask2, ex2)

            def pair_bank(b0):
                return banks[:, b0:b0 + 2, :].rearrange("p a (b t) -> p (a b) t", t=CH)

            def every(name, lo=0):
                a = CONST[name][0] + lo
                return con[:, a:a + CH].unsqueeze(1).broadcast_to([P, NCH * AC, CH])

            dve.wait_ge(pair_ready, 1)
            nc.vector.tensor_tensor(m_ab, pair_bank(6), every("strict_t"), ALU.mult).then_inc(pair_used, 1)
            dve.wait_ge(pair_used, 1)
            then(nc.vector.tensor_tensor(inv_t, m_ab, every("first_t"), ALU.mult))
            then(nc.vector.tensor_tensor(inv_t, inv_t, every("eye"), ALU.add))
            dve.wait_ge(pair_ready, 2)
            nc.vector.tensor_tensor(inv, pair_bank(0), every("first"), ALU.mult).then_inc(pair_used, 1)
            dve.wait_ge(pair_used, 2)
            then(nc.vector.tensor_tensor(inv, inv, every("eye"), ALU.add))
            for n, (dst, b0, m) in enumerate(((m_ak, 2, "strict_t"), (m_rb, 4, "upto_t"), (m_rk, 6, "upto_t"))):
                dve.wait_ge(pair_ready, n + 3)
                nc.vector.tensor_tensor(dst, pair_bank(b0), every(m), ALU.mult).then_inc(pair_used, 1)
            def level_mask(n, half):
                m = every("levels_t", CH * n)
                nc.vector.tensor_tensor(level_half(m_lev, half), level_half(m_ab, half), level_half(m, half), ALU.mult).then_inc(level_m, 1)

            for half in range(2):
                level_mask(0, half)
            for n in range(len(LEVELS)):
                for half in range(2):
                    dve.wait_ge(level_d, 2 * n + half + 1)
                    last_level = n == len(LEVELS) - 1
                    if not last_level:
                        nc.vector.tensor_tensor(level_half(inv, half), level_half(inv, half), level_bank(4, half, 0), ALU.add)
                    then(nc.vector.tensor_tensor(level_half(inv_t, half), level_half(inv_t, half), level_bank(4, half, T), ALU.add))
                    if not last_level:
                        level_mask(n + 1, half)
            dve.sem_inc(inv_ready, 1)
            for c in range(NCH - 1):
                dve.wait_ge(g_ready, c + 1)
                g_new, g_old = gst[:, c % 2], gst[:, (c - 1) % 2]
                g_new, g_old = by_bank(g_new), by_bank(g_old)
                pc = p_end[:, :, c].rearrange("p (a b) -> p a b", a=2).unsqueeze(3).broadcast_to([P, 2, 2, CH])
                if c:
                    dve.wait_ge(y_ready, c)
                    then(nc.vector.tensor_tensor(g_new, four_heads(4), g_old, ALU.add))
                    nc.vector.tensor_tensor(g_new, g_new, pc, ALU.mult).then_inc(state_ready, 1)
                else:
                    nc.vector.tensor_tensor(g_new, four_heads(4), pc, ALU.mult).then_inc(state_ready, 1)
                dve.wait_ge(state_ready, c + 1)
            dve.wait_ge(gn_sum, 1)
            full = lambda b0: banks[:, b0:b0 + 2, :].rearrange("p a (b t) -> p (a b) t", b=2)
            then(nc.vector.scalar_tensor_tensor(b1, full(6), -1.0 / HEAD, b1, ALU.mult, ALU.add))
            nc.vector.tensor_tensor(f0, b1, b1, ALU.mult).then_inc(gn_sq, 1)
            dve.wait_ge(gn_rt, 1)
            then(nc.vector.reciprocal(f1, f1))
            then(nc.vector.tensor_tensor(b1, b1, f1, ALU.mult))
            per_chunk(lambda c: nc.vector.tensor_scalar(b1[:, c, :], b1[:, c, :], vcol("lnx_g", c), vcol("lnx_b", c), ALU.mult, ALU.add))
            then(nc.vector.tensor_tensor(b1, b1, b2, ALU.add))
            nc.vector.tensor_tensor(rw, b1, b6, ALU.mult).then_inc(rw_ready, 1)
            two = lambda a, b: a[:, 2 * b:2 * b + 2, :]
            pair = lambda k: B[k].rearrange("p (a t) -> p a t", a=2)

            def mixed_part(b):
                dve.wait_ge(h_hi_ready, MIXED_PARTS // 2 + b + 1)
                nc.vector.tensor_tensor(two(mixed_lo, b), two(mixed, b), two(mixed_hi, b).bitcast(F32), ALU.subtract).then_inc(h_lo_ready, 2)

            for b in range(4):
                dve.wait_ge(br_ready, b + 1)
                nc.vector.tensor_tensor(two(mixed, b), pair(b), two(sig_a, b), ALU.mult)
                if b == 1:
                    dve.wait_ge(h_hi_ready, (RW_PARTS + AC) // 2)
                    nc.vector.tensor_tensor(rw_lo, rw.rearrange("p a t -> p (a t)"), rw_hi.bitcast(F32), ALU.subtract).then_inc(h_lo_ready, AC)
            for b in range(4):
                dve.wait_ge(br_ready, b + 5)
                then(nc.vector.tensor_tensor(two(mixed_r, b), pair(4 + b), two(sig_r, b), ALU.mult))
                nc.vector.tensor_tensor(two(mixed, b), two(mixed, b), two(mixed_r, b), ALU.add).then_inc(mixed_ready, 1)
                if b:
                    mixed_part(b - 1)
            mixed_part(3)

            def gated_residual(first, sem_of, gate):
                for b in range(4):
                    dve.wait_ge(sem_of, first + 2 * b + 2) if first is not None else None
                    for c in (2 * b, 2 * b + 1):
                        last = nc.vector.scalar_tensor_tensor(x[:, c, :], B[b][:, c % 2 * T:c % 2 * T + T], mod[:, gate + c:gate + c + 1], x[:, c, :], ALU.mult, ALU.add)
                    last.then_inc(x_ready, 1)

            gated_residual(4, res_ready, 16)
            norm_modulated(6, scale2, 24)
            nc.vector.tensor_copy(ident_r, ident)
            dve.wait_ge(scores_ready, 1)
            dve.wait_ge(router_loaded, 32)
            then(nc.vector.tensor_tensor(choice, score_e, rbias.unsqueeze(1).broadcast_to([P, TB, EXPERTS]), ALU.add))
            nc.vector.memset(gtop, 3e38)
            for tb in range(TB):
                for g in range(GROUPS):
                    last = nc.vector.max(grp8[:, tb, g, :], choice[:, tb, g * 8:(g + 1) * 8])
            then(last)
            then(nc.vector.tensor_tensor(gsum, grp8[:, :, :, 0], grp8[:, :, :, 1], ALU.add))
            for tb in range(TB):
                last = nc.vector.max(gwork[:, tb, :], gsum[:, tb, :])
            then(last)
            then(nc.vector.tensor_copy(gtop[:, :, 0:TOP_GROUPS], gwork[:, :, 0:TOP_GROUPS]))
            for tb in range(TB):
                last = nc.vector.match_replace(gwork[:, tb, :], gtop[:, tb, :], gsum[:, tb, :], TAKEN)
            then(last)
            then(nc.vector.tensor_scalar(gwork, gwork, TAKEN / 2, MASKED, ALU.is_gt, ALU.mult))
            by_group = lambda a: a.rearrange("p a (g e) -> p a g e", g=GROUPS)
            then(nc.vector.tensor_tensor(by_group(choice), by_group(choice), gwork.unsqueeze(3).broadcast_to([P, TB, GROUPS, 8]), ALU.add))
            for tb in range(TB):
                last = nc.vector.max(gtop[:, tb, :], choice[:, tb, :])
            then(last)
            for tb in range(TB):
                last = nc.vector.match_replace(cwork[:, tb, :], gtop[:, tb, :], choice[:, tb, :], TAKEN)
            then(last)
            nc.vector.tensor_scalar(mask_e, cwork, TAKEN / 2, None, ALU.is_lt).then_inc(mask_ready, 1)
            dve.wait_ge(mask_ready, 1)
            then(nc.vector.tensor_tensor(sel_e, mask_e, score_e, ALU.mult))
            then(nc.vector.tensor_reduce(den, sel_e, AX_X, ALU.add))
            then(nc.vector.reciprocal(den, den))
            for tb in range(TB):
                last = nc.vector.tensor_scalar(sel_e[:, tb, :], sel_e[:, tb, :], den[:, tb:tb + 1], ROUTED_SCALE, ALU.mult, ALU.mult)
            then(last)
            for b in range(4):
                dve.wait_ge(tok_hi_ready, b + 1)
                part = (slice(None), b // 2, slice(b % 2 * 512, (b % 2 + 1) * 512))
                nc.vector.tensor_tensor(tok_lo[part], B[4 + b], tok_hi[part].bitcast(F32), ALU.subtract).then_inc(tok_lo_ready, 1)
            then(nc.vector.tensor_copy(gate_hi, sel_e))
            nc.vector.tensor_tensor(gate_lo, sel_e, gate_hi.bitcast(F32), ALU.subtract)
            dve.wait_ge(rank_ready, 1)
            nc.vector.scalar_tensor_tensor(rank_e, mask_e, -NOT_CHOSEN, B[6][:, 0:2 * EXPERTS].rearrange("p (a e) -> p a e", a=TB), ALU.mult, ALU.add).then_inc(gates_ready, 1)
            dve.wait_ge(gates_ready, 1)

            def build_pick(buf, e):
                by_token = rank_e[:, :, e] if isinstance(e, slice) else rank_e[:, :, bass.ds(e, 4)]
                slots = cst("slots").unsqueeze(1).unsqueeze(1).broadcast_to([P, TB, 4, CAP])
                dst = pick[buf].rearrange("p a (e s) -> p a e s", e=4)
                nc.vector.tensor_tensor(dst, slots, by_token.unsqueeze(3).broadcast_to([P, TB, 4, CAP]), ALU.is_equal).then_inc(pick_ready, 1)

            build_pick(0, slice(0, 4))
            then(nc.vector.scalar_tensor_tensor(mask_e, rank_e, CAP - NOT_CHOSEN, mask_e, ALU.is_ge, ALU.mult))
            nc.vector.tensor_tensor(dense_e, mask_e, sel_e, ALU.mult)
            nc.vector.tensor_reduce(beyond, mask_e.rearrange("p a e -> p (a e)"), AX_X, ALU.add).then_inc(beyond_ready, 1)
            dve.wait_ge(beyond_sum, 1)
            nc.vector.tensor_copy(flag, B[6][:, T:T + 1]).then_inc(flag_ready, 1)

            base = steps[0]

            def two_quads(i, n=None):
                first, last = n == 0, n == QUADS // 2 - 1
                shared_gu = SHARED_GATE_UP.get(n, {})
                for k in range(4):
                    b = k % 2
                    if k % 2 == 0 and not (last and k == 2):
                        if not (first and k == 0):
                            dve.wait_ge(gather_ready, 8 * i + 2 * k + 4)
                        build_pick((k // 2 + 1) % 2, 8 * i + (4 * (k // 2) + 4))
                    dve.wait_ge(pair_sig, 4 * i + (k + 1))
                    nc.vector.tensor_tensor(gated_p, B[4][:, 0:T], sig_p, ALU.mult).then_inc(dve_step, 1)
                    dve.wait_ge(dve_step, 4 * i + (base + k + 1))
                    dve.wait_ge(spread_ready, 4 * i + (k + 1))
                    nc.vector.scalar_tensor_tensor(act_p, gated_p, slot_gate[b], B[4][:, T:2 * T], ALU.mult, ALU.mult).then_inc(pair_act, 1)
                    for half in range(2):
                        dve.wait_ge(pair_hi, 8 * i + (2 * k + half + 1))
                        part = (slice(None), slice(half * 512, (half + 1) * 512))
                        ins = nc.vector.tensor_tensor(out_lo[part], B[6 + half], out_hi[part].bitcast(F32), ALU.subtract)
                    ins.then_inc(pair_lo, 1)
                    if k in shared_gu:
                        dve.wait_ge(sig_ready, 2 * FFN_CHUNKS + shared_gu[k] + 1)
                        nc.vector.tensor_tensor(sig_s, B[5][:, 0:T], sig_s, ALU.mult).then_inc(shared_gated, 1)
                        dve.wait_ge(shared_gated, shared_gu[k] + 1)
                        nc.vector.tensor_tensor(act_s, sig_s, B[5][:, T:2 * T], ALU.mult).then_inc(act_ready, 1)

            for n in range(2):
                two_quads(n, n)
            with dve.Fori(2, QUADS // 2 - 1) as i:
                two_quads(i)
            two_quads(QUADS // 2 - 1, QUADS // 2 - 1)
            steps[0] = base + PAIRS
            dve.wait_ge(pair_spread, PAIRS)
            overflow = dve.value_load(flag[0:1, :])
            with dve.If(overflow > 0):
                with dve.Fori(0, EXPERTS // UNITS) as i:
                    for s in range(2 * UNITS):
                        gu = B[4 + s % 2]
                        dve.wait_ge(dense_sig, 2 * UNITS * i + (s + 1))
                        nc.vector.tensor_tensor(gated[:, s % 2, :], gu[:, 0:T], sig_f[:, s % 2, :], ALU.mult).then_inc(dense_step, 1)
                        dve.wait_ge(dense_step, 4 * UNITS * i + (2 * s + 1))
                        nc.vector.tensor_tensor(weighted[:, s % 2, :], gated[:, s % 2, :], gu[:, T:2 * T], ALU.mult).then_inc(dense_step, 1)
                        if s % 2 == 0:
                            dve.wait_ge(wb_landed[s // 2], 16 * i + 16)
                        dve.wait_ge(dense_step, 4 * UNITS * i + (2 * s + 2))
                        nc.vector.tensor_tensor(act_f[:, s % 2, :], weighted[:, s % 2, :], wb[:, s // 2, :], ALU.mult).then_inc(dense_act, 1)
                dve.wait_ge(unit_used, EXPERTS)
            gated_residual(None, None, 40)
            dve.wait_ge(rt_ready, 8)
            then(nc.vector.reciprocal(rinv[:], rt[:]))
            for c in range(KC):
                last = nc.vector.scalar_tensor_tensor(x[:, c, :], x[:, c, :], vcol("final_g", c), rinv[:], ALU.mult, ALU.mult)
                if c % 2:
                    last.then_inc(out_ready, 1)


def tiles_of(w):
    k, n = w.shape
    return w.reshape(k // P, P, n // P, P).transpose(2, 1, 0, 3).reshape(n // P, P, k)


def slots_of(tiles):
    n = -(-len(tiles) // 3) * 3
    out = np.zeros((n, P, TILE), np.float32)
    for i, t in enumerate(tiles):
        out[i] = t
    return out.reshape(n // 3, 3, P, TILE).transpose(0, 2, 1, 3).reshape(n // 3, P, SLOT)


def ffn_slots(gate_up, down):
    g = tiles_of(gate_up)
    d = down.reshape(FFN_CHUNKS, P, D)
    return np.concatenate([g[:FFN_CHUNKS], g[FFN_CHUNKS:], d], 2)


def half_tiles(w):
    t = tiles_of(w)
    return t.reshape(4, 2, P, 512).transpose(0, 2, 1, 3).reshape(4, P, TILE)


def columns(v):
    return np.asarray(v).reshape(-1, P).T


def layout(i):
    i = {k: np.asarray(v) for k, v in i.items()}
    vecs = {"norm_mixer0": i["norm_mixer"][0], "norm_mixer1": i["norm_mixer"][1], "norm_ffn0": i["norm_ffn"][0],
            "norm_ffn1": i["norm_ffn"][1], "pool_scale": i["pool_scale"][0], "kv_norm": i["kv_norm"], "final_norm": i["final_norm"],
            "norm1_g": i["norm1_g_2"][0], "norm2_g": i["norm2_g_2"][0], "final_g": i["final_g_2"], "c": i["c_2"][0], "ada_b": i["ada_b_2"][0],
            "tshift_mu": i["tshift_mu_2"][0], "decay_w0": i["decay_w0_2"][0], "iclr_a0": i["iclr_a0_2"][0], "k_k": i["k_k_2"][0], "k_a": i["k_a_2"][0],
            "r_k": i["r_k_2"][0].reshape(-1), "lnx_g": i["lnx_g_2"][0], "lnx_b": i["lnx_b_2"][0]}
    w_kv, w_in = i["w_kv"], i["w_in_2"][0]
    kvq = [*tiles_of(w_kv[:, D:]), *tiles_of(w_kv[:, :D]), *tiles_of(i["w_q"][0])]
    ada = i["ada_w_2"][0].reshape(KC, P, 2, SLOT).transpose(0, 2, 1, 3).reshape(16, P, SLOT)
    a = ATTN_W
    o = 3 * a
    iq, ik, iw = w_in[:, o:o + 512], w_in[:, o + 512:o + 544], w_in[:, o + 544:o + 560]
    zr, ga, gr = w_in[:, o + 560:o + 560 + ZR * P], w_in[:, o + 560 + ZR * P:o + 560 + ZR * P + D], w_in[:, o + 560 + ZR * P + D:]
    zr = zr.reshape(D, ZR, P)[:, ZR_ORDER, :].reshape(D, ZR * P)
    iw_tile = np.concatenate([iw, np.zeros((D, P - IDX_HEADS), np.float32)], 1)
    win = np.concatenate([w_in[:, 2 * a:3 * a], iw_tile, w_in[:, 0:2 * a], iq, ik, ik, ik, ik, zr, ga, gr], 1)
    br = [*half_tiles(i["w_attn_br_2"][0]), *half_tiles(i["w_rwkv_br_2"][0]), *tiles_of(i["w_out_2"][0])]
    ws = np.concatenate([ffn_slots(i["w_gate_up"][0], i["w_down"][0]), slots_of(kvq), ada, slots_of(tiles_of(i["w_o"][0])), ffn_slots(i["w_gate_up"][1], i["w_down"][1]),
                         slots_of(tiles_of(win)), slots_of(br)], 0)
    rel = np.concatenate([np.concatenate([i["rel_bias"], i["rel_bias_2"]], 1), np.ones((1, HEADS_1 + HEADS_2), np.float32)], 0)
    lora = np.concatenate([np.concatenate([i["decay_up_2"][0], i["iclr_up_2"][0]], 0), i["gate_up_2"][0]], 1)
    gate = np.concatenate([i["sh_gate_2"], i["exp_gate_2"][0]], 0)
    up = np.concatenate([i["sh_up_2"], i["exp_up_2"][0]], 0)
    dn = np.concatenate([i["sh_down_2"], i["exp_down_2"][0]], 0)
    n = EXPERTS + 1
    gu = np.concatenate([gate.reshape(n, KC, P, EXPERT_FF), up.reshape(n, KC, P, EXPERT_FF)], 3).transpose(0, 2, 1, 3).reshape(n, P, KC * 2 * EXPERT_FF)
    experts = np.concatenate([gu, dn.reshape(n, 2, P, D).transpose(0, 2, 1, 3).reshape(n, P, 2 * D)], 2)
    return {
        "xT": i["x"][0].T.reshape(KC, P, T).transpose(1, 0, 2),
        "vec": np.concatenate([columns(vecs[name]) for name, _ in VEC_PARTS], 1),
        "consts": constants(),
        "selector": bias_selector(),
        "inv_count": pool_inverse_counts(),
        "pool_w": i["pool_w"][0].reshape(4, 2, P, 256).transpose(2, 0, 1, 3),
        "ws": ws,
        "rel": rel,
        "lora": lora,
        "router": i["router_w_2"][0].reshape(KC, P, EXPERTS).transpose(1, 0, 2),
        "router_bias": i["router_bias_2"],
        "experts": experts,
    }


def kernel(**inputs):
    import concourse.bacc as bacc
    from concourse.bass_utils import run_bass_kernel_spmd

    nc = bacc.Bacc("TRN2", target_bir_lowering=False, num_devices=1)
    arrays = {name: np.ascontiguousarray(a) for name, a in layout(inputs).items()}
    aps = {name: nc.dram_tensor(name, a.shape, F32, kind="ExternalInput").ap() for name, a in arrays.items()}
    aps["out"] = nc.dram_tensor("out", (P, KC, T), F32, kind="ExternalOutput").ap()
    build(nc, **aps)
    result = run_bass_kernel_spmd(nc, [arrays], core_ids=[0]).results[0]["out"]
    return np.ascontiguousarray(result.transpose(1, 0, 2).reshape(D, T).T)[None]
```
